# Optimizing a Trainium2 kernel written in Bass

```python
import jax
import jax.numpy as jnp
from jax import lax
import numpy as np
import jax, jax.numpy as jnp

D_MODEL = 1024
BATCH = 1
SEQ = 256
DEPTH = 2

FOX_HEADS = 8
FOX_HEAD_DIM = 64
MLA_HEADS = 8
MLA_Q_RANK = 256
MLA_KV_RANK = 128
MLA_NOPE_DIM = 64
MLA_ROPE_DIM = 32
MLA_V_DIM = 64
ROPE_THETA = 10000.0
DN_HEADS = 8
DN_HEAD_DIM = 64
DN_CONV_WIDTH = 4
DN_CHUNK = 64
D_FF = 2816
Q_BLOCK = 128
N_BRANCH = 3
NORM_EPS = 1e-6

FOX_WIDTH = FOX_HEADS * FOX_HEAD_DIM
MLA_QK_DIM = MLA_NOPE_DIM + MLA_ROPE_DIM
MLA_WIDTH = MLA_HEADS * MLA_V_DIM
DN_WIDTH = DN_HEADS * DN_HEAD_DIM
IN_WIDTHS = (FOX_WIDTH, FOX_WIDTH, FOX_WIDTH, FOX_HEADS,
             MLA_Q_RANK, MLA_KV_RANK, MLA_ROPE_DIM,
             DN_WIDTH, DN_WIDTH, DN_WIDTH, DN_WIDTH, DN_HEADS, DN_HEADS,
             N_BRANCH * D_MODEL)
N_IN = sum(IN_WIDTHS)


def rmsnorm(x, gain):
    xf = x.astype(jnp.float32)
    y = xf * lax.rsqrt(jnp.mean(xf * xf, axis=-1, keepdims=True) + NORM_EPS)
    return (y * gain.astype(jnp.float32)).astype(x.dtype)

def l2norm(x):
    xf = x.astype(jnp.float32)
    return xf * lax.rsqrt(jnp.sum(xf * xf, axis=-1, keepdims=True) + NORM_EPS)

def swiglu(h, w_gu, w_down):
    gate, up = jnp.split(h @ w_gu, 2, axis=-1)
    return (jax.nn.silu(gate) * up) @ w_down

def rope_tables(positions):
    half = MLA_ROPE_DIM // 2
    inv_freq = ROPE_THETA ** (-jnp.arange(half, dtype=jnp.float32) / half)
    ang = positions.astype(jnp.float32)[..., None] * inv_freq
    return jnp.cos(ang)[:, :, None, :], jnp.sin(ang)[:, :, None, :]

def apply_rope(x, cos, sin):
    x1, x2 = jnp.split(x.astype(jnp.float32), 2, axis=-1)
    return jnp.concatenate([x1 * cos - x2 * sin, x2 * cos + x1 * sin], axis=-1).astype(x.dtype)

def causal_short_conv(x, w):
    width = w.shape[0]
    s = x.shape[1]
    xp = jnp.pad(x, ((0, 0), (width - 1, 0), (0, 0)))
    return sum(xp[:, i:i + s] * w[i] for i in range(width))

def block_causal_attention(q, k, v, scale, log_decay_cum=None):
    b, s, h, dqk = q.shape
    dv = v.shape[-1]
    nb = s // Q_BLOCK
    q_blocks = q.reshape(b, nb, Q_BLOCK, h, dqk).transpose(1, 0, 3, 2, 4)
    k_pos = jnp.arange(s)
    xs = (jnp.arange(nb), q_blocks)
    if log_decay_cum is not None:
        c = log_decay_cum.astype(jnp.float32).transpose(0, 2, 1)
        c_blocks = c.reshape(b, h, nb, Q_BLOCK).transpose(2, 0, 1, 3)
        xs = (jnp.arange(nb), q_blocks, c_blocks)

    def one_block(args):
        idx, q_blk = args[0], args[1]
        logits = jnp.einsum('bhqd,bkhd->bhqk', q_blk, k).astype(jnp.float32) * scale
        if log_decay_cum is not None:
            logits = logits + args[2][..., :, None] - c[:, :, None, :]
        q_pos = idx * Q_BLOCK + jnp.arange(Q_BLOCK)
        logits = jnp.where(k_pos[None, :] <= q_pos[:, None], logits, -jnp.inf)
        p = jax.nn.softmax(logits, axis=-1).astype(v.dtype)
        return jnp.einsum('bhqk,bkhd->bqhd', p, v)

    out = lax.map(one_block, xs)
    return out.transpose(1, 0, 2, 3, 4).reshape(b, s, h, dv)

def chunk_gated_delta_rule(q, k, v, g, beta):
    b, s, h, dk = q.shape
    dv = v.shape[-1]
    nc = s // DN_CHUNK

    def to_chunks(t):
        return jnp.moveaxis(t.reshape((b, nc, DN_CHUNK, h) + t.shape[3:]), 3, 2)

    q, k, v, g, beta = (to_chunks(t) for t in (q, k, v, g, beta))
    gc = jnp.cumsum(g, axis=-1)
    idx = jnp.arange(DN_CHUNK)
    causal = idx[:, None] >= idx[None, :]
    strict = idx[:, None] > idx[None, :]
    decay_mat = jnp.exp(jnp.where(causal, gc[..., :, None] - gc[..., None, :], -jnp.inf))
    k_beta = k * beta[..., None]
    v_beta = v * beta[..., None]
    m = jnp.where(strict, jnp.einsum('bnhid,bnhjd->bnhij', k_beta, k) * decay_mat, 0.0)
    eye = jnp.eye(DN_CHUNK, dtype=jnp.float32)
    t_inv = lax.linalg.triangular_solve(eye + m, jnp.broadcast_to(eye, m.shape),
                                        left_side=True, lower=True, unit_diagonal=True)
    w = t_inv @ (k_beta * jnp.exp(gc)[..., None])
    u = t_inv @ v_beta
    qk = jnp.einsum('bnhid,bnhjd->bnhij', q, k) * decay_mat
    q_dec = q * jnp.exp(gc)[..., None]
    k_dec = k * jnp.exp(gc[..., -1:] - gc)[..., None]
    g_last = jnp.exp(gc[..., -1])

    def step(state, xs_c):
        w_c, u_c, qk_c, q_c, k_c, gl = xs_c
        v_new = u_c - w_c @ state
        o_c = q_c @ state + qk_c @ v_new
        state = state * gl[..., None, None] + jnp.einsum('bhcd,bhce->bhde', k_c, v_new)
        return state, o_c

    xs = tuple(jnp.moveaxis(t, 1, 0) for t in (w, u, qk, q_dec, k_dec, g_last))
    state0 = jnp.zeros((b, h, dk, dv), jnp.float32)
    _, o = lax.scan(step, state0, xs)
    return o.transpose(1, 0, 3, 2, 4).reshape(b, s, h, dv)

def hybrid_mixer(h, cos, sin, w_in, b_gate, fox_b_f, mla_q_norm, mla_w_uq, mla_kv_norm, mla_w_ukv,
                 dn_conv_w, dn_a_log, dn_dt_bias, dn_o_norm, w_br_fox, w_br_mla, w_br_dn, w_out):
    b, s, _ = h.shape
    f32 = jnp.float32
    splits = np.cumsum(IN_WIDTHS)[:-1]
    (fox_q, fox_k, fox_v, fox_f, mla_cq, mla_ckv, mla_kr,
     dn_q, dn_k, dn_v, dn_z, dn_b, dn_a, gate_logits) = jnp.split(h @ w_in, splits, axis=-1)

    fox_shape = (b, s, FOX_HEADS, FOX_HEAD_DIM)
    log_f = jax.nn.log_sigmoid(fox_f.astype(f32) + fox_b_f.astype(f32))
    fox_out = block_causal_attention(fox_q.reshape(fox_shape), fox_k.reshape(fox_shape),
                                     fox_v.reshape(fox_shape), FOX_HEAD_DIM ** -0.5,
                                     jnp.cumsum(log_f, axis=1))
    y_fox = fox_out.reshape(b, s, FOX_WIDTH) @ w_br_fox

    q = (rmsnorm(mla_cq, mla_q_norm) @ mla_w_uq).reshape(b, s, MLA_HEADS, MLA_QK_DIM)
    q_nope, q_rope = jnp.split(q, [MLA_NOPE_DIM], axis=-1)
    kv = (rmsnorm(mla_ckv, mla_kv_norm) @ mla_w_ukv).reshape(b, s, MLA_HEADS, MLA_NOPE_DIM + MLA_V_DIM)
    k_nope, mla_v = jnp.split(kv, [MLA_NOPE_DIM], axis=-1)
    k_rope = apply_rope(mla_kr[:, :, None, :], cos, sin)
    q_full = jnp.concatenate([q_nope, apply_rope(q_rope, cos, sin)], axis=-1)
    k_full = jnp.concatenate([k_nope, jnp.broadcast_to(k_rope, (b, s, MLA_HEADS, MLA_ROPE_DIM))], axis=-1)
    mla_out = block_causal_attention(q_full, k_full, mla_v, MLA_QK_DIM ** -0.5)
    y_mla = mla_out.reshape(b, s, MLA_WIDTH) @ w_br_mla

    qkv = jax.nn.silu(causal_short_conv(jnp.concatenate([dn_q, dn_k, dn_v], axis=-1), dn_conv_w))
    cq, ck, cv = jnp.split(qkv, 3, axis=-1)
    dn_shape = (b, s, DN_HEADS, DN_HEAD_DIM)
    q_dn = l2norm(cq.reshape(dn_shape)) * (DN_HEAD_DIM ** -0.5)
    k_dn = l2norm(ck.reshape(dn_shape))
    v_dn = cv.reshape(dn_shape).astype(f32)
    beta = jax.nn.sigmoid(dn_b.astype(f32))
    g = -jnp.exp(dn_a_log.astype(f32)) * jax.nn.softplus(dn_a.astype(f32) + dn_dt_bias.astype(f32))
    o = chunk_gated_delta_rule(q_dn, k_dn, v_dn, g, beta)
    o = rmsnorm(o, dn_o_norm).astype(h.dtype) * jax.nn.silu(dn_z.reshape(dn_shape))
    y_dn = o.reshape(b, s, DN_WIDTH) @ w_br_dn

    g_fox, g_mla, g_dn = jnp.split(jax.nn.sigmoid(gate_logits + b_gate), N_BRANCH, axis=-1)
    return (g_fox * y_fox + g_mla * y_mla + g_dn * y_dn) @ w_out

def first_inputs(seed: int = 0) -> dict:
    key = jax.random.key(seed)
    ks = iter(list(jax.random.split(key, 32)))
    f32 = jnp.float32
    L = DEPTH

    def nrm(shape, scale):
        return jax.random.normal(next(ks), shape, f32) * scale

    def gain(shape):
        return 1.0 + nrm(shape, 0.1)

    x = jax.random.normal(next(ks), (BATCH, SEQ, D_MODEL), f32)
    positions = (jnp.arange(SEQ, dtype=jnp.int32)[None, :]
                 + jax.random.randint(next(ks), (BATCH, 1), 0, 1024, dtype=jnp.int32))
    ffn1_norm = gain((L, D_MODEL))
    ffn1_w_gu = nrm((L, D_MODEL, 2 * D_FF), D_MODEL ** -0.5)
    ffn1_w_down = nrm((L, D_FF, D_MODEL), D_FF ** -0.5)
    mix_norm = gain((L, D_MODEL))
    w_in = nrm((L, D_MODEL, N_IN), D_MODEL ** -0.5)
    b_gate = nrm((L, N_BRANCH * D_MODEL), 0.1)
    fox_b_f = 4.0 + nrm((L, FOX_HEADS), 0.5)
    mla_q_norm = gain((L, MLA_Q_RANK))
    mla_w_uq = nrm((L, MLA_Q_RANK, MLA_HEADS * MLA_QK_DIM), MLA_Q_RANK ** -0.5)
    mla_kv_norm = gain((L, MLA_KV_RANK))
    mla_w_ukv = nrm((L, MLA_KV_RANK, MLA_HEADS * (MLA_NOPE_DIM + MLA_V_DIM)), MLA_KV_RANK ** -0.5)
    dn_conv_w = nrm((L, DN_CONV_WIDTH, 3 * DN_WIDTH), DN_CONV_WIDTH ** -0.5)
    dn_a_log = jnp.log(jax.random.uniform(next(ks), (L, DN_HEADS), f32, 1.0, 16.0))
    dt = jnp.exp(jax.random.uniform(next(ks), (L, DN_HEADS), f32,
                                    float(np.log(1e-3)), float(np.log(1e-1))))
    dn_dt_bias = dt + jnp.log(-jnp.expm1(-dt))
    dn_o_norm = gain((L, DN_HEAD_DIM))
    w_br_fox = nrm((L, FOX_WIDTH, D_MODEL), FOX_WIDTH ** -0.5)
    w_br_mla = nrm((L, MLA_WIDTH, D_MODEL), MLA_WIDTH ** -0.5)
    w_br_dn = nrm((L, DN_WIDTH, D_MODEL), DN_WIDTH ** -0.5)
    w_out = nrm((L, D_MODEL, D_MODEL), D_MODEL ** -0.5)
    ffn2_norm = gain((L, D_MODEL))
    ffn2_w_gu = nrm((L, D_MODEL, 2 * D_FF), D_MODEL ** -0.5)
    ffn2_w_down = nrm((L, D_FF, D_MODEL), D_FF ** -0.5)
    final_norm = gain((D_MODEL,))
    return {'x': x, 'positions': positions,
            'ffn1_norm': ffn1_norm, 'ffn1_w_gu': ffn1_w_gu, 'ffn1_w_down': ffn1_w_down,
            'mix_norm': mix_norm, 'w_in': w_in, 'b_gate': b_gate, 'fox_b_f': fox_b_f,
            'mla_q_norm': mla_q_norm, 'mla_w_uq': mla_w_uq, 'mla_kv_norm': mla_kv_norm, 'mla_w_ukv': mla_w_ukv,
            'dn_conv_w': dn_conv_w, 'dn_a_log': dn_a_log, 'dn_dt_bias': dn_dt_bias, 'dn_o_norm': dn_o_norm,
            'w_br_fox': w_br_fox, 'w_br_mla': w_br_mla, 'w_br_dn': w_br_dn, 'w_out': w_out,
            'ffn2_norm': ffn2_norm, 'ffn2_w_gu': ffn2_w_gu, 'ffn2_w_down': ffn2_w_down,
            'final_norm': final_norm}

def first_block(x, positions, ffn1_norm, ffn1_w_gu, ffn1_w_down, mix_norm, w_in, b_gate, fox_b_f,
              mla_q_norm, mla_w_uq, mla_kv_norm, mla_w_ukv, dn_conv_w, dn_a_log, dn_dt_bias, dn_o_norm,
              w_br_fox, w_br_mla, w_br_dn, w_out, ffn2_norm, ffn2_w_gu, ffn2_w_down, final_norm):
    cos, sin = rope_tables(positions)
    for l in range(DEPTH):
        x = x + 0.5 * swiglu(rmsnorm(x, ffn1_norm[l]), ffn1_w_gu[l], ffn1_w_down[l])
        x = x + hybrid_mixer(rmsnorm(x, mix_norm[l]), cos, sin, w_in[l], b_gate[l], fox_b_f[l],
                             mla_q_norm[l], mla_w_uq[l], mla_kv_norm[l], mla_w_ukv[l],
                             dn_conv_w[l], dn_a_log[l], dn_dt_bias[l], dn_o_norm[l],
                             w_br_fox[l], w_br_mla[l], w_br_dn[l], w_out[l])
        x = x + 0.5 * swiglu(rmsnorm(x, ffn2_norm[l]), ffn2_w_gu[l], ffn2_w_down[l])
    return rmsnorm(x, final_norm)


CTX_LEN = 256
GRID_W = 64
HEAD_DIM = 64
AXIS_DIM = HEAD_DIM // 2
ATTN_WIDTH = D_MODEL // 2
N_Q_HEADS = ATTN_WIDTH // HEAD_DIM
N_KV_HEADS = N_Q_HEADS // 4
KV_WIDTH = N_KV_HEADS * HEAD_DIM
FOURIER_WIDTH = D_MODEL // 4
FOURIER_GROUP = 64
N_FOURIER_GROUPS = FOURIER_WIDTH // FOURIER_GROUP
GMLP_WIDTH = D_MODEL // 4
GMLP_HEAD = 64
N_GMLP_HEADS = GMLP_WIDTH // GMLP_HEAD
CHUNK = 128
MIX_WIDTH = ATTN_WIDTH + FOURIER_WIDTH + GMLP_WIDTH
IN_WIDTH = ATTN_WIDTH + 2 * KV_WIDTH + FOURIER_WIDTH + 2 * GMLP_WIDTH
SPLITS = [ATTN_WIDTH, ATTN_WIDTH + KV_WIDTH, ATTN_WIDTH + 2 * KV_WIDTH,
          ATTN_WIDTH + 2 * KV_WIDTH + FOURIER_WIDTH,
          ATTN_WIDTH + 2 * KV_WIDTH + FOURIER_WIDTH + GMLP_WIDTH]
D_FF_2 = 4 * D_MODEL
EPS = 1e-6


def rms_norm(x, g):
    xf = x.astype(jnp.float32)
    y = xf * lax.rsqrt(jnp.mean(xf * xf, axis=-1, keepdims=True) + EPS)
    return (y * g.astype(jnp.float32)).astype(x.dtype)

def modulate(h, shift, scale):
    return h * (1 + scale) + shift

def adaln(cond, w, b):
    return jnp.split(jax.nn.silu(cond) @ w + b, 6, axis=-1)

def axial_rope_tables(n, dtype):
    rows = n // GRID_W
    row = jnp.repeat(jnp.arange(rows, dtype=jnp.float32), GRID_W)
    col = jnp.tile(jnp.arange(GRID_W, dtype=jnp.float32), rows)
    inv = ROPE_THETA ** (-jnp.arange(0, AXIS_DIM, 2, dtype=jnp.float32) / AXIS_DIM)
    ar = (row[:, None] * inv)[:, None, :]
    ac = (col[:, None] * inv)[:, None, :]
    return tuple(t.astype(dtype) for t in (jnp.cos(ar), jnp.sin(ar), jnp.cos(ac), jnp.sin(ac)))

def rope_1d(x, cos, sin):
    x1, x2 = jnp.split(x, 2, axis=-1)
    return jnp.concatenate([x1 * cos - x2 * sin, x1 * sin + x2 * cos], axis=-1)

def apply_axial_rope(x, tabs):
    cr, sr, cc, sc = tabs
    xr, xc = jnp.split(x, 2, axis=-1)
    return jnp.concatenate([rope_1d(xr, cr, sr), rope_1d(xc, cc, sc)], axis=-1)

def heads(t, h):
    return t.reshape(t.shape[0], t.shape[1], h, HEAD_DIM)

def attend(q, k, v):
    s = jnp.einsum('bqkgd,btkd->bkgqt', q, k).astype(jnp.float32) * (HEAD_DIM ** -0.5)
    p = jax.nn.softmax(s, axis=-1).astype(v.dtype)
    return jnp.einsum('bkgqt,btkd->bqkgd', p, v)

def latent_attention(q, k, v):
    b, s, hq, d = q.shape
    g = hq // N_KV_HEADS
    nblk = s // Q_BLOCK
    qb = q.reshape(b, nblk, Q_BLOCK, N_KV_HEADS, g, d).transpose(1, 0, 2, 3, 4, 5)
    out = lax.map(lambda qblk: attend(qblk, k, v), qb)
    return out.transpose(1, 0, 2, 3, 4, 5).reshape(b, s, hq * d)

def context_attention(q, k, v):
    b, n, hq, d = q.shape
    g = hq // N_KV_HEADS
    return attend(q.reshape(b, n, N_KV_HEADS, g, d), k, v).reshape(b, n, hq * d)

def fourier_mix(f):
    b, n, _ = f.shape
    fg = f.astype(jnp.float32).reshape(b, n, N_FOURIER_GROUPS, FOURIER_GROUP)
    y = jnp.fft.fft2(fg, axes=(1, 3), norm='ortho').real
    return y.reshape(b, n, FOURIER_WIDTH).astype(f.dtype)

def chunk_spatial_gate(u, v, v_g, w_s, b_s):
    b, n, _ = u.shape
    u = jax.nn.gelu(u)
    vh = jax.nn.gelu(v).reshape(b, n // CHUNK, CHUNK, N_GMLP_HEADS, GMLP_HEAD)
    vh = rms_norm(vh, v_g.reshape(N_GMLP_HEADS, GMLP_HEAD))
    sp = jnp.einsum('hpq,bcqhd->bcphd', w_s, vh) + b_s.T[None, None, :, :, None]
    return u * sp.reshape(b, n, GMLP_WIDTH)

def squared_relu_mlp(h, w1, w2):
    return jnp.square(jax.nn.relu(h @ w1)) @ w2

def layer(x, ctx, c, c_ctx, w_ada, b_ada, g1, g2, w_in, q_g, k_g, v_g, w_s, b_s, w_out, w1, w2, update_ctx):
    sh1, sc1, gt1, sh2, sc2, gt2 = [m[:, None, :] for m in adaln(c, w_ada, b_ada)]
    csh1, csc1, cgt1, csh2, csc2, cgt2 = adaln(c_ctx, w_ada, b_ada)

    px = modulate(rms_norm(x, g1), sh1, sc1) @ w_in
    pc = modulate(rms_norm(ctx, g1), csh1, csc1) @ w_in
    qx, kx, vx, fx, ux, gvx = jnp.split(px, SPLITS, axis=-1)
    qc, kc, vc, fc, uc, gvc = jnp.split(pc, SPLITS, axis=-1)

    tabs = axial_rope_tables(x.shape[1], x.dtype)
    qx = apply_axial_rope(rms_norm(heads(qx, N_Q_HEADS), q_g), tabs)
    kx = apply_axial_rope(rms_norm(heads(kx, N_KV_HEADS), k_g), tabs)
    kc = rms_norm(heads(kc, N_KV_HEADS), k_g)
    vx = heads(vx, N_KV_HEADS)
    vc = heads(vc, N_KV_HEADS)
    k_all = jnp.concatenate([kc, kx], axis=1)
    v_all = jnp.concatenate([vc, vx], axis=1)

    mix_x = jnp.concatenate([latent_attention(qx, k_all, v_all),
                             fourier_mix(fx),
                             chunk_spatial_gate(ux, gvx, v_g, w_s, b_s)], axis=-1) @ w_out
    x = x + gt1 * mix_x
    x = x + gt2 * squared_relu_mlp(modulate(rms_norm(x, g2), sh2, sc2), w1, w2)

    if update_ctx:
        qc = rms_norm(heads(qc, N_Q_HEADS), q_g)
        mix_c = jnp.concatenate([context_attention(qc, kc, vc),
                                 fourier_mix(fc),
                                 chunk_spatial_gate(uc, gvc, v_g, w_s, b_s)], axis=-1) @ w_out
        ctx = ctx + cgt1 * mix_c
        ctx = ctx + cgt2 * squared_relu_mlp(modulate(rms_norm(ctx, g2), csh2, csc2), w1, w2)
    return x, ctx

def second_inputs(seed: int = 0) -> dict:
    key = jax.random.key(seed)
    ks = jax.random.split(key, 17)
    f32 = jnp.float32
    n = lambda k, s: jax.random.normal(k, s, dtype=f32)
    return {
        'x': n(ks[0], (BATCH, SEQ, D_MODEL)),
        'c': n(ks[1], (BATCH, D_MODEL)),
        'ctx': n(ks[2], (BATCH, CTX_LEN, D_MODEL)),
        'c_ctx': n(ks[3], (D_MODEL,)),
        'w_ada': n(ks[4], (DEPTH, D_MODEL, 6 * D_MODEL)) * (0.5 * D_MODEL ** -0.5),
        'b_ada': n(ks[5], (DEPTH, 6 * D_MODEL)) * 0.01,
        'norm1_g': 1.0 + 0.02 * n(ks[6], (DEPTH, D_MODEL)),
        'norm2_g': 1.0 + 0.02 * n(ks[7], (DEPTH, D_MODEL)),
        'w_in': n(ks[8], (DEPTH, D_MODEL, IN_WIDTH)) * D_MODEL ** -0.5,
        'q_norm_g': 1.0 + 0.02 * n(ks[9], (DEPTH, HEAD_DIM)),
        'k_norm_g': 1.0 + 0.02 * n(ks[10], (DEPTH, HEAD_DIM)),
        'gmlp_v_g': 1.0 + 0.02 * n(ks[11], (DEPTH, GMLP_WIDTH)),
        'w_spatial': n(ks[12], (DEPTH, N_GMLP_HEADS, CHUNK, CHUNK)) * CHUNK ** -0.5,
        'b_spatial': n(ks[13], (DEPTH, N_GMLP_HEADS, CHUNK)) * 0.02,
        'w_out': n(ks[14], (DEPTH, MIX_WIDTH, D_MODEL)) * MIX_WIDTH ** -0.5,
        'w_mlp1': n(ks[15], (DEPTH, D_MODEL, D_FF_2)) * D_MODEL ** -0.5,
        'w_mlp2': n(ks[16], (DEPTH, D_FF_2, D_MODEL)) * D_FF_2 ** -0.5,
    }

def second_block(x, c, ctx, c_ctx, w_ada, b_ada, norm1_g, norm2_g, w_in, q_norm_g, k_norm_g, gmlp_v_g,
              w_spatial, b_spatial, w_out, w_mlp1, w_mlp2):
    for l in range(DEPTH):
        x, ctx = layer(x, ctx, c, c_ctx, w_ada[l], b_ada[l], norm1_g[l], norm2_g[l], w_in[l],
                       q_norm_g[l], k_norm_g[l], gmlp_v_g[l], w_spatial[l], b_spatial[l], w_out[l],
                       w_mlp1[l], w_mlp2[l], l < DEPTH - 1)
    return x


def setup_inputs(seed=0):
    out = dict(first_inputs(seed))
    for name, value in second_inputs(seed + 1).items():
        if name != "x":
            out[name + "_2"] = value
    return out


def reference(
    x, positions, ffn1_norm, ffn1_w_gu, ffn1_w_down, mix_norm, w_in, b_gate, fox_b_f,
    mla_q_norm, mla_w_uq, mla_kv_norm, mla_w_ukv, dn_conv_w, dn_a_log, dn_dt_bias, dn_o_norm,
    w_br_fox, w_br_mla, w_br_dn, w_out, ffn2_norm, ffn2_w_gu, ffn2_w_down, final_norm, c_2,
    ctx_2, c_ctx_2, w_ada_2, b_ada_2, norm1_g_2, norm2_g_2, w_in_2, q_norm_g_2, k_norm_g_2,
    gmlp_v_g_2, w_spatial_2, b_spatial_2, w_out_2, w_mlp1_2, w_mlp2_2,
):
    x = first_block(
        x, positions, ffn1_norm, ffn1_w_gu, ffn1_w_down, mix_norm, w_in, b_gate, fox_b_f,
        mla_q_norm, mla_w_uq, mla_kv_norm, mla_w_ukv, dn_conv_w, dn_a_log, dn_dt_bias,
        dn_o_norm, w_br_fox, w_br_mla, w_br_dn, w_out, ffn2_norm, ffn2_w_gu, ffn2_w_down,
        final_norm,
    )
    return second_block(
        x, c_2, ctx_2, c_ctx_2, w_ada_2, b_ada_2, norm1_g_2, norm2_g_2, w_in_2, q_norm_g_2,
        k_norm_g_2, gmlp_v_g_2, w_spatial_2, b_spatial_2, w_out_2, w_mlp1_2, w_mlp2_2,
    )


_drawn_inputs = setup_inputs


def setup_inputs(seed=0):
    import zlib

    import numpy as np

    out = dict(_drawn_inputs(seed))
    spreads = {}
    factors = {'mla_q_norm': 3.885,
     'ctx_2': 3.888,
     'norm1_g_2': 8.0,
     'norm2_g_2': 4.58,
     'q_norm_g_2': 8.0,
     'k_norm_g_2': 8.0,
     'gmlp_v_g_2': 8.0,
     'b_spatial_2': 8.0}
    for name, (base, spread) in spreads.items():
        noise = np.random.default_rng([zlib.crc32(name.encode()), seed]).standard_normal(out[name].shape)
        drawn = base * np.exp(spread * noise) if base else spread * noise
        out[name] = jnp.asarray(drawn.astype(out[name].dtype))
    for name, factor in factors.items():
        out[name] = (out[name] * factor).astype(out[name].dtype)
    return out
```

```python
from contextlib import ExitStack

import numpy as np

import concourse.bass as bass
from concourse import mybir

F32 = mybir.dt.float32
BF16 = mybir.dt.bfloat16
I32 = mybir.dt.int32
ALU = mybir.AluOpType
ACT = mybir.ActivationFunctionType
AX_X = mybir.AxisListType.X
EXP_LN = "natural_log_exp_and_others"

P = 128
T = 256
TT = T // P
D = 1024
KD = D // P
DEPTH = 2
FF = 2816
KF = FF // P
GU_GROUPS = FF // 256
FF2 = 4096
KF2 = FF2 // P
H = 8
PAIRS = H // 2
HD = 64
CHUNK = 64
CHUNKS = T // CHUNK
TAPS = 4
EPS = 1e-6
NEG = -1e30
LEVELS = (1, 2, 4, 8, 16, 32)
SLOTS = 3
FULL = 8 * 512
FOX_SCALE = HD ** -0.5
MLA_SCALE = 96 ** -0.5
TURN = 2 * np.pi
TURN_PARTS = (6.28125, 2.0 ** -22 * round((TURN - 6.28125) * 2.0 ** 22))
TURN_PARTS += (TURN - sum(TURN_PARTS),)
ROUND = 1.5 * 2.0 ** 23
HALF_TURN, QUARTER_TURN = 3.1415925, float(np.float32(np.pi / 2))

FFN_GROUPS = [("gu", FULL, 2)] * GU_GROUPS + [("down", KF * P, 1)] * 8
MIX_GROUPS = ([(n, FULL, 2) for n in ("lat", "fq", "fk", "fv", "dq", "dk", "dv")]
              + [("uq", 2 * 1024, 4), ("uk", 512, 2), ("uv", 512, 2), ("dz", FULL, 2)]
              + [("gate", FULL, 2), ("br", 4 * 512, 2)] * 6 + [("out", FULL, 2)] * 2)
ONE_GROUPS = FFN_GROUPS + MIX_GROUPS + FFN_GROUPS
TWO_GROUPS = ([("q", FULL, 2), ("kuv", FULL, 2), ("fg", FULL, 2)] + [("out", FULL, 2)] * 2
              + [("m1", FULL, 2)] * 8 + [("m2", KF2 * P, 1)] * 8)
ADA_GROUPS = [("ada", FULL, 1)] * (DEPTH * 12)
KV_GROUPS = [("kuv", FULL, 2)]
SECTIONS = {"ada": (1, ADA_GROUPS), "ctx": (1, TWO_GROUPS), "kv": (1, KV_GROUPS), "one": (DEPTH, ONE_GROUPS),
            "fin": (1, []), "two": (DEPTH, TWO_GROUPS)}


def places(groups):
    seen, unit, out = {}, 0, {}
    for n, (name, width, units) in enumerate(groups):
        i = seen.get(name, 0)
        seen[name] = i + 1
        out[name, i] = (n, unit)
        unit += units
    return out


GROUP = {s: places(g) for s, (_, g) in SECTIONS.items()}
UNITS = {s: sum(g[2] for g in gs) for s, (_, gs) in SECTIONS.items()}
MIX_BASE = len(FFN_GROUPS)
FFN2_BASE = MIX_BASE + len(MIX_GROUPS)
FFN_UNITS = sum(g[2] for g in FFN_GROUPS)
FFN2_UNIT = UNITS["one"] - FFN_UNITS


def one_order():
    def lin(name, *parts):
        return [("lin", (name, i)) for i in parts]

    def one(*names):
        return [(n[:-1].removesuffix("_"), int(n[-1])) for n in names]

    order = (one("norm1") + lin("lat", 0, 1) + one("latnorm0") + lin("fq", 0) + one("rows0") + lin("fq", 1)
             + lin("fk", 0, 1) + one("rowcols0") + lin("fv", 0) + one("scores0") + lin("fv", 1)
             + one("scores1", "soft0") + lin("dq", 0) + one("turn0", "soft1", "scores2") + lin("dq", 1)
             + one("values0", "turn1", "soft2", "scores3") + lin("dk", 0) + one("values1", "turn2", "soft3")
             + lin("dk", 1) + one("values2", "turn3", "krot0") + lin("dv", 0) + one("values3") + lin("dv", 1)
             + one("conv0") + lin("uq", 0, 1) + one("conv1") + lin("uq", 2, 3) + lin("uk", 0, 1)
             + one("qrot0") + lin("uv", 0, 1) + one("conv2") + lin("dz", 0) + one("scores4", "conv3") + lin("dz", 1)
             + one("scores5", "soft4", "l2_0", "turn4", "soft5", "scores6", "spread0", "values4", "turn5", "soft6",
                   "scores7", "natural0", "values5", "turn6", "soft7", "decay0", "values6", "turn7", "kk0",
                   "values7", "qk0", "level1_0"))
    fill = [x for b in range(2) for g in range(2) for x in
            [("gate", 4 * b + 2 * g), ("gate", 4 * b + 2 * g + 1), ("br", 4 * b + 2 * g), ("br", 4 * b + 2 * g + 1)]]
    for s in range(1, 6):
        order += [("level", s)] + fill[:1]
        fill = fill[1:]
    order.append(("wu", 0))
    for c in range(CHUNKS):
        order += [("scan_v", c)] + fill[:1] + [("scan_s", c)] + fill[1:2]
        fill = fill[2:]
    order += fill + [("gate", 8), ("onorm", 0), ("gate", 9), ("br", 8), ("br", 9), ("gate", 10), ("gate", 11), ("br", 10), ("br", 11)]
    return order + [("out", i) for i in range(4)]


MIXER = one_order()


def two_order(rotary, whole=True):
    order = [("norm", 0)] + [("lin", ("q", i)) for i in range(2) if whole] + [("lin", ("kuv", 0)), ("lin", ("kuv", 1))]
    if not whole:
        return order + [("knorm", 0), ("kdup", 0)]
    order += [("squares", 0), ("lin", ("fg", 0)), ("lin", ("fg", 1)), ("qnorm", 0), ("knorm", 0)]
    order += [("rot", 0)] * rotary + [("fourier", 0), ("kdup", 0), ("scores", 0), ("scores", 1), ("soft", 0), ("spatial", 0)]
    for i in range(8):
        order += [("turn", i)] + [("soft", i + 1)] * (i < 7) + [("scores", i + 2)] * (i < 6) + [("values", i)]
    return order + [("out", i) for i in range(4)] + [("norm", 1)]


TWO, CTX, KV = two_order(True), two_order(False), two_order(False, False)
SPOTS_OF = {"l2": 2, "spread": 2, "natural": 2, "decay": 2, "kk": 2, "qk": 2, "level1": 2, "wu": 2,
            "rot": 2, "fourier": 2}
NO_SPOT = ("lin", "gate", "br", "out", "conv", "squares", "soft", "rows")


def spots(order):
    at, out = 0, {}
    for step in order:
        out[step] = at
        at += 0 if step[0] in NO_SPOT else (6 if step[1] < 5 else 4) if step[0] == "level" else SPOTS_OF.get(step[0], 1)
    return out, at


SPOT, SPOTS = {}, {}
for _s, _order in {"ada": [("ada", i) for i in range(DEPTH * 12)], "ctx": CTX, "kv": KV,
                   "one": [("norm", 0)] + MIXER + [("norm", 2)], "fin": [("norm", 0)], "two": TWO}.items():
    SPOT[_s], SPOTS[_s] = spots(_order)

V_FFN1, V_MIX, V_FFN2, V_BGATE, V_QN, V_KVN = 0, 8, 16, 24, 48, 50
V_TAP, V_ON, V_BIAS, V_ALOG = 51, 99, 100, 101
NV = 102
W_N1, W_N2, W_QG, W_KG, W_VG, W_BS, W_WS = 0, 8, 16, 17, 18, 20, 20 + 2 * P
NW = W_WS + 4 * P
C_ID, C_BLK, C_ROT, C_CAUSAL, C_DELTA, C_LEVEL = 0, 128, 256, 384, 512, 640
C_PAIR = C_LEVEL + 6 * P
C_FREQ = C_PAIR + PAIRS * P
C_SIGN, C_TWO, C_LIVE, C_FINAL, C_RESET = C_FREQ + 1, C_FREQ + 2, C_FREQ + 4, C_FREQ + 5, C_FREQ + 13
NC_ = C_RESET + T
B_DFT, B_CD, B_SD, B_COS, B_SIN, B_DUP = 0, TT * 512, TT * 512 + P, TT * 512 + 2 * P, TT * 512 + 2 * P + T, TT * 512 + 2 * P + 2 * T
NB = B_DUP + 2 * P
ROWA, ROWB = 32, 96
ROWS = 2 * H


class Signal:

    def __init__(self, handle, counts, first=0):
        self.handle, self.counts, self.start, at = handle, counts, {}, first
        for sec, (turns, _) in SECTIONS.items():
            self.start[sec] = at
            at += turns * counts.get(sec, 0)

    def at(self, c, k):
        return self.handle, self.counts.get(c.sec, 0) * c.turn + (self.start[c.sec] + k)


class Place:

    def __init__(self, sec, turn=0):
        self.sec, self.turn = sec, turn


def build(nc, stream, x_in, ctx_in, cond, positions, vec1, vec2, bada, consts, tables, out):
    with ExitStack() as ctx:
        def sb(name, shape, dt=F32):
            return ctx.enter_context(nc.sbuf_tensor(name, shape, dt))

        def sem(name):
            return ctx.enter_context(nc.semaphore(name))

        def signal(name, first=0, **counts):
            return Signal(sem(name), counts, first)

        slot = [sb(f"weights{s}", [P, FULL]) for s in range(SLOTS)]
        xT = sb("residual", [P, KD, T])
        act = sb("normed", [P, KD, T])
        hT = sb("hidden", [P, KF2, T])
        sq = sb("squares", [P, KD, T])
        part = sb("square_sums", [P, T])
        rstd = sb("rstd", [P, T])
        sg = sb("silu_gate", [P, 2, T])
        vec = sb("vectors", [P, NV])
        cst = sb("constants", [P, NC_])
        identb = sb("identity_bf16", [P, P], BF16)
        causal = sb("causal_bf16", [P, P], BF16)
        delta_mask = sb("delta_mask_bf16", [P, P], BF16)
        ones = sb("ones", [P, P])
        cossin = sb("cos_sin", [P, 2, T])
        lat = sb("latents", [P, 4, T])
        qk_f = sb("fox_qk", [P, 8, T])
        vn_f = sb("fox_values", [P, TT, 512])
        qk_m = sb("mla_qk", [P, 8, T])
        vn_m = sb("mla_values", [P, TT, 512])
        qr = sb("mla_q_rope", [P, PAIRS, T])
        kr = sb("mla_k_rope", [P, T])
        conv_in = sb("conv_in", [P, 12, T + TAPS - 1])
        qkv = sb("delta_qkv", [P, 12, T])
        row = sb("rows", [P, 6, T])
        cols = sb("row_columns", [P, TT, 48])
        mx = sb("negated_maxima", [P, 2, 2, 2])
        rs = sb("softmax_sums", [P, 2, 2, 2])
        probs = sb("probabilities", [P, 3072])
        vnew = sb("delta_new_values", [P, 512])
        state = sb("delta_state", [P, PAIRS, P])
        glast = sb("delta_chunk_decay", [P, PAIRS, CHUNKS])
        alog = sb("exp_a_log", [P, 1])
        mod = sb("modulation", [P, DEPTH * 48, 2])
        cur = sb("modulation_of_pass", [P, 48])
        k_ctx = sb("context_keys", [P, DEPTH, 2, T])
        v_ctx = sb("context_values", [P, DEPTH, TT, P])

        prob = probs[:, 0:1536].rearrange("p (b e c) -> p b e c", b=2, e=2)
        probT = probs[:, 1536:3072].rearrange("p (b e c) -> p b e c", b=2, e=2)
        o_att = hT[:, 24:32, :]

        def mats(tiles):
            return tiles.rearrange("p a (b c) -> p (a b) c", c=P).rearrange("p (t e q) c -> p t e q c", t=TT, e=2)

        m_t, inv, k_beta = mats(hT[:, 0:8, :]), mats(hT[:, 8:16, :]), hT[:, 16:20, :]
        x_m, inv_t, b_m = mats(sq[:, :, :]), mats(qk_f[:, :, :]), mats(qk_m[:, :, :])
        qk_t = probs[:, 0:2048].rearrange("p (t e q c) -> p t e q c", t=TT, e=2, q=PAIRS)
        conv_flat = conv_in[:, :, :].rearrange("p a b -> p (a b)")
        kbe, kdn, vb = (conv_flat[:, 1024 * i:1024 * (i + 1)].rearrange("p (t c) -> p t c", t=TT) for i in range(3))
        w_t, q_dec, zs = qr[:, :, :], hT[:, 20:24, :], lat[:, :, :]
        merged, o_dn = qkv[:, 0:8, :], qkv[:, 8:12, :]
        latn = hT[:, 4:7, :]
        tbl = qkv[:, 0:8, :].rearrange("p a t -> p (a t)")
        vec_b = conv_flat[:, 0:NW]
        cond_s, ada_s = qk_f[:, 0:1, :].rearrange("p a (k j) -> p (a k) j", k=KD), qk_f[:, 2:6, :].rearrange(
            "p (b a) t -> p b (a t)", b=2)
        bias_a = part[:, 0:DEPTH * 48]
        keys, vals = vn_f, vn_m[:, 0, :].rearrange("p (k c) -> p k c", k=4)
        f_nat, g_nat, u_two, f_mid = qr[:, 0:2, :], qr[:, 2:4, :], lat[:, 0:2, :], qk_f[:, 0:4, :]
        prob2, probT2 = probs[:, 0:2048].rearrange("p (b e c) -> p b e c", b=2, e=2), probs[:, 2048:3072].rearrange(
            "p (e c) -> p e c", e=2)
        gt = vn_m[:, :, :].rearrange("p a (m t) -> p a m t", m=2)

        lin = ctx.enter_context(nc.psum_tensor("units", [P, 2, 512], F32))
        spot = ctx.enter_context(nc.psum_tensor("spots", [P, 6, 512], F32))

        ident = cst[:, C_ID:C_ID + P]
        blk = cst[:, C_BLK:C_BLK + P]
        rot = cst[:, C_ROT:C_ROT + P]

        halves = {s: UNITS[s] // 2 for s in SECTIONS}
        lin_ready = signal("unit_summed", SLOTS, **UNITS)
        lin_taken = [signal(f"unit_taken{b}", 1, **halves) for b in range(2)]
        spot_ready = signal("spot_summed", 1, **SPOTS)
        spot_taken = [signal(f"spot_taken{s}", 1, **{k: (SPOTS[k] + 2 - s) // 3 for k in SECTIONS}) for s in range(3)]
        loaded = [signal(f"weights_loaded{s}", **{k: 16 * ((len(SECTIONS[k][1]) + 2 - s) // 3) for k in SECTIONS})
                  for s in range(SLOTS)]
        norms = {"ctx": 2, "kv": 1, "one": 3, "fin": 1, "two": 2}
        squares = signal("squares_made", **(norms | {"ctx": 3, "kv": 2, "one": 6, "two": 3}))
        sums = signal("square_sums_made", **norms)
        rstds = signal("rstd_made", **(norms | {"ctx": 5, "kv": 2, "one": 7, "two": 5}))
        normed = signal("tile_normed", **{k: KD * v for k, v in norms.items()})
        gate_made = signal("gate_activated", ctx=2 * 8, one=4 * GU_GROUPS, two=2 * 8)
        vec_here = signal("vectors_loaded", one=16)
        lat_made = signal("latents_normed", one=1)
        rows_abs = signal("rows_abs_made", one=1)
        rows_exp = signal("rows_exp_made", one=1)
        rows_cum = signal("rows_summed_up", one=1)
        rows_done = signal("rows_done", one=1)
        conv_done = signal("conv_done", one=1)
        qkv_done = signal("delta_qkv_done", one=1)
        l2_made = signal("delta_qk_normed", one=1)
        rope_q = signal("mla_q_turned", one=1)
        rope_k = signal("mla_k_turned", one=1)
        max_made = signal("maxima_made", ctx=8, one=8, two=8)
        prob_made = signal("probabilities_normed", ctx=8, one=8, two=8)
        k_beta_made = signal("k_beta_made", one=1)
        natural_made = signal("natural_keys_made", one=1)
        level_made = signal("level_part_made", one=6)
        state_made = signal("delta_state_made", one=1 + CHUNKS)
        z_made = signal("silu_z_made", one=1)
        delta_done = signal("delta_out_normed", one=1)
        merged_made = signal("branches_merged", one=1)
        qk_scaled = signal("qk_normed", ctx=1, kv=1, two=1)
        qk_turned = signal("qk_turned", two=1)
        g_sums = signal("gmlp_sums_made", ctx=1, two=1)
        g_made = signal("gmlp_normed", ctx=1, two=1)
        mix_made = signal("gmlp_done", ctx=1, two=1)
        kept = signal("context_kept", ctx=2, kv=2)
        given = signal("context_given", two=2)
        tables_here = signal("tables_loaded", ctx=16, kv=0, two=0)
        vec_b_here = signal("second_vectors_loaded", ctx=16, kv=16, two=16)
        tables_again = sem("tables_loaded_again")
        ctx_here = sem("context_loaded")
        cond_here = sem("condition_loaded")
        bias_here = sem("adaln_bias_loaded")
        cond_made = sem("condition_gate_made")
        cur_made = signal("modulation_chosen", ctx=1, kv=1, two=1)
        consts_here = sem("constants_loaded")
        consts_made = sem("constants_made")
        turn_here = sem("rotary_angles_made")
        turn_done = sem("rotary_tables_made")
        x_here = sem("residual_loaded")
        pos_here = sem("positions_loaded")
        cond_done = sem("cond_gate_made")
        stored = sem("output_stored")

        def unit(c, name, i, part=0):
            u = GROUP[c.sec][name, i][1] + part
            return u, u % 2

        def taken(c, u):
            return lin_taken[u % 2].at(c, u // 2 + 1)

        def spot_of(c, step, i=0):
            n = SPOT[c.sec][step] + i
            return n, spot[:, 2 * (n % 3):2 * (n % 3) + 2, :], n % 3

        block = ctx.enter_context(nc.Block())

        @block.sync
        def _(sp):
            sp.dma_start(cst[:, :], consts).then_inc(consts_here, 16)
            sp.sem_inc(lin_ready.handle, SLOTS)
            for signal_ in (*lin_taken, *spot_taken, spot_ready):
                sp.sem_inc(signal_.handle, 1)
            sp.dma_start(sq[:, 2, :].bitcast(I32), positions.to_broadcast([P, T])).then_inc(pos_here, 16)
            sp.dma_start(cond_s, cond).then_inc(cond_here, 16)
            sp.dma_start(bias_a, bada).then_inc(bias_here, 16)
            sp.dma_start(xT[:, :, :], ctx_in).then_inc(ctx_here, 16)
            base = 0
            for sec, (turns, groups) in SECTIONS.items():
                widths = [w for _, w, _ in groups]
                at = [base + P * sum(widths[:n]) for n in range(len(groups))]
                size = P * sum(widths)
                last = [u + g[2] for (_, u), g in zip(GROUP[sec].values(), groups)]

                def load(n, offset, wait):
                    sp.wait_ge(*wait)
                    sp.dma_start(slot[n % SLOTS][:, 0:widths[n]],
                                 stream[bass.ds(offset, P * widths[n])].rearrange("(p w) -> p w", p=P)
                                 ).then_inc(loaded[n % SLOTS].handle, 16)

                if sec == "ada":
                    with sp.Fori(0, len(groups) // 6) as it:
                        for s in range(6):
                            load(s, it * (6 * P * FULL) + s * P * FULL, lin_ready.at(Place(sec), it * 6 + (s - 2)))
                elif sec not in ("one", "two"):
                    for n in range(len(groups)):
                        load(n, at[n], lin_ready.at(Place(sec), last[n - SLOTS] if n >= SLOTS else 0))
                else:
                    sp.wait_ge(*lin_ready.at(Place(sec), 0))
                    if sec == "one":
                        for b in range(2):
                            sp.wait_ge(*lin_taken[b].at(Place(sec), 0))
                        sp.dma_start(xT[:, :, :], x_in).then_inc(x_here, 16)
                    with sp.Fori(0, turns) as l:
                        for n in range(len(groups)):
                            load(n, l * size + at[n],
                                 lin_ready.at(Place(sec, l), last[n - SLOTS] - (0 if n >= SLOTS else UNITS[sec])))
                base += turns * size
            for b in range(2):
                sp.wait_ge(*lin_taken[b].at(Place("two", DEPTH), 0))
            sp.dma_start(out, xT[:, :, :]).then_inc(stored, 16)
            sp.wait_ge(stored, 16)

        @block.gpsimd
        def _(pool):
            pool.dma_start(tbl[:, 0:NB], tables).then_inc(tables_here.handle, 16)
            pool.dma_start(vec_b, vec2[0]).then_inc(vec_b_here.handle, 16)

            def keep(c, l):
                n, _, s = spot_of(c, ("kdup", 0))
                pool.wait_ge(*spot_taken[s].at(c, n // 3 + 1))
                pool.tensor_copy(k_ctx[:, l], keys[:, :, T:]).then_inc(kept.handle, 1)
                pool.wait_ge(*taken(c, unit(c, "kuv", 0, 1)[0]))
                pool.tensor_copy(v_ctx[:, l], vals[:, TT:, :]).then_inc(kept.handle, 1)

            keep(Place("ctx"), 0)
            for b in range(2):
                pool.wait_ge(*lin_taken[b].at(Place("kv"), 0))
            pool.dma_start(vec_b, vec2[1]).then_inc(vec_b_here.handle, 16)
            keep(Place("kv"), 1)
            with pool.Fori(0, DEPTH) as l:
                c = Place("one", l)
                pool.wait_ge(*lin_taken[1].at(c, 0))
                pool.wait_ge(*lin_taken[0].at(c, 0))
                pool.dma_start(vec[:, :], vec1[bass.ds(l, 1)].rearrange("a p v -> (a p) v")).then_inc(vec_here.handle, 16)
            pool.wait_ge(*normed.at(Place("two"), 0))
            pool.dma_start(tbl[:, 0:NB], tables).then_inc(tables_again, 16)
            with pool.Fori(0, DEPTH) as l:
                c = Place("two", l)
                for b in range(2):
                    pool.wait_ge(*lin_taken[b].at(c, 0))
                pool.dma_start(vec_b, vec2[bass.ds(l, 1)].rearrange("a p v -> (a p) v")).then_inc(vec_b_here.handle, 16)
                pool.tensor_copy(keys[:, :, 0:T], k_ctx[:, bass.ds(l, 1)].rearrange("p a k t -> p (a k) t")
                                 ).then_inc(given.handle, 1)
                pool.tensor_copy(vals[:, 0:TT, :], v_ctx[:, bass.ds(l, 1)].rearrange("p a k t -> p (a k) t")
                                 ).then_inc(given.handle, 1)

        @block.tensor
        def _(pe):
            def group(c, name, i=0, turns=0):
                n = GROUP[c.sec][name, i][0]
                pe.wait_ge(*loaded[n % SLOTS].at(c, (turns + (n // SLOTS + 1)) * 16))
                return slot[n % SLOTS]

            def free_unit(c, u, before=0):
                pe.wait_ge(*lin_taken[u % 2].at(c, before + u // 2))
                return lin[:, u % 2, :]

            def free_spot(c, step, i=0, before=0):
                n, banks, s = spot_of(c, step, i)
                pe.wait_ge(*spot_taken[s].at(c, before + n // 3))
                return banks

            def product(dst, w, k, width, col, rhs, kt0=0):
                for kt in range(k):
                    mm = pe.matmul(dst, w[:, kt * width + col:kt * width + col + P], rhs[:, kt, :],
                                   start=(kt == 0), stop=(kt == k - 1))
                return mm

            def norm(c, i):
                banks = free_spot(c, ("norm", i))
                pe.wait_ge(*sums.at(c, i + 1))
                pe.matmul(banks[:, 0, 0:T], ones[:, :], part[:, :], start=True, stop=True
                          ).then_inc(spot_ready.handle, 1)

            def ffn(c, which):
                norm(c, 2 * which)
                gbase, ubase = (0, 0) if which == 0 else (FFN2_BASE, FFN2_UNIT)

                def gu(it, s):
                    n, u = gbase + s, ubase + 2 * s
                    pe.wait_ge(*normed.at(c, KD * (2 * which + 1)))
                    pe.wait_ge(*loaded[n % SLOTS].at(c, it * 16 + (n // SLOTS + 1) * 16))
                    w = slot[n % SLOTS]
                    for f in range(2):
                        dst = free_unit(c, u + f, it * 3)
                        for g in range(2):
                            mm = product(dst[:, g * T:g * T + T], w, KD, 512, g * 256 + f * P, act)
                        mm.then_inc(lin_ready.handle, 1)

                with pe.Fori(0, GU_GROUPS // 3) as it:
                    for s in range(3):
                        gu(it, s)
                for s in range(GU_GROUPS // 3 * 3, GU_GROUPS):
                    gu(0, s)
                last = ubase + 2 * GU_GROUPS
                pe.wait_ge(*taken(c, last - 1))
                pe.wait_ge(*taken(c, last - 2))
                for m in range(KD):
                    w = group(c, "down", 8 * which + m)
                    dst = free_unit(c, last + m)
                    product(dst[:, 0:T], w, KF, P, 0, hT).then_inc(lin_ready.handle, 1)

            def plain(c, name, i, part):
                u, bank = unit(c, name, i, part)
                w = group(c, name, i)
                dst = free_unit(c, u)
                if name == "fv":
                    for kt in range(KD):
                        mm = pe.matmul(dst, act[:, kt, part * P:part * P + P], w[:, kt * 512:kt * 512 + 512],
                                       start=(kt == 0), stop=(kt == KD - 1))
                elif name == "uv":
                    mm = pe.matmul(dst, latn[:, 2, part * P:part * P + P], w[:, 0:512], start=True, stop=True)
                else:
                    k, width, rhs = {"uq": (2, 1024, latn), "uk": (1, 512, latn[:, 2:3, :])}.get(name, (KD, 512, act))
                    if name == "uq" and part == 0:
                        pe.wait_ge(*lat_made.at(c, 1))
                    for m in range(2):
                        mm = product(dst[:, m * T:m * T + T], w, k, width, (2 * part + m) * P, rhs)
                mm.then_inc(lin_ready.handle, 1)

            def latnorm(c):
                banks = free_spot(c, ("latnorm", 0))
                pe.wait_ge(*squares.at(c, 3))
                pe.matmul(banks[:, 0, 0:T], ones[:, :], sq[:, 0, :], start=True, stop=False)
                pe.matmul(banks[:, 0, 0:T], ones[:, :], sq[:, 1, :], start=False, stop=True)
                pe.matmul(banks[:, 0, T:2 * T], ones[:, :], sq[:, 2, :], start=True, stop=True
                          ).then_inc(spot_ready.handle, 1)

            def rows(c):
                banks = free_spot(c, ("rowcols", 0))
                pe.wait_ge(*rows_done.at(c, 1))
                for t in range(TT):
                    tok = slice(t * P, t * P + P)
                    pe.matmul(banks[:, 0, t * 48:t * 48 + 16], row[ROWA:ROWA + ROWS, 4, tok],
                              cst[ROWA:ROWA + ROWS, ROWA:ROWA + ROWS], start=True, stop=True)
                    pe.matmul(banks[:, 0, t * 48 + 16:t * 48 + 32], row[ROWA:ROWA + ROWS, 5, tok],
                              cst[ROWA:ROWA + ROWS, ROWA:ROWA + ROWS], start=True, stop=True)
                for t in range(TT):
                    mm = pe.matmul(banks[:, 1, t * 8:t * 8 + 8], row[ROWB:ROWB + H, 1, t * P:t * P + P],
                                   cst[ROWB:ROWB + H, ROWB:ROWB + H], start=True, stop=True)
                mm.then_inc(spot_ready.handle, 1)

            def head_row(head):
                return cst[ROWA:ROWA + ROWS, ROWA + head:ROWA + head + 1]

            def scores(c, i):
                fox, p = i < PAIRS, i % PAIRS
                banks = free_spot(c, ("scores", i))
                if i == 0:
                    for u in (unit(c, "fq", 0)[0], unit(c, "fk", 0)[0]):
                        pe.wait_ge(*taken(c, u))
                        pe.wait_ge(*taken(c, u + 1))
                if i == PAIRS:
                    for u in (unit(c, "uq", 0)[0], unit(c, "uk", 0)[0]):
                        pe.wait_ge(*taken(c, u))
                        pe.wait_ge(*taken(c, u + 1))
                    pe.wait_ge(*rope_q.at(c, 1))
                    pe.wait_ge(*rope_k.at(c, 1))
                qk = qk_f if fox else qk_m
                for e in range(2):
                    rows_ = slice(HD * e, HD * e + HD)
                    for t, (col, keys) in enumerate(((0, P), (P, T))):
                        dst = banks[:, e, col:col + keys]
                        tok = slice(t * P, t * P + P)
                        pe.matmul(dst, qk[rows_, p, tok], qk[rows_, 4 + p, 0:keys], start=True, stop=False)
                        pe.matmul(dst[:, keys - P:keys], identb[:, :], causal[:, :], start=False, stop=False,
                                  skip_group_check=True)
                        if fox:
                            mm = pe.matmul(dst, head_row(2 * p + e).to_broadcast([ROWS, P]),
                                           row[ROWA:ROWA + ROWS, 1, 0:keys], start=False, stop=True)
                        else:
                            mm = pe.matmul(dst, qr[HD * e:HD * e + 32, p, tok], kr[HD * e:HD * e + 32, 0:keys],
                                           start=False, stop=True)
                mm.then_inc(spot_ready.handle, 1)

            def turn(c, i):
                banks = free_spot(c, ("turn", i))
                pe.wait_ge(*prob_made.at(c, i + 1))
                for e in range(2):
                    for b in range(3):
                        mm = pe.matmul(banks[:, e, b * P:b * P + P], prob[:, i % 2, e, b * P:b * P + P], ident,
                                       start=True, stop=True, is_transpose=True)
                mm.then_inc(spot_ready.handle, 1)

            def values(c, i):
                p, vn = i % PAIRS, vn_f if i < PAIRS else vn_m
                if i % PAIRS == 0:
                    u = unit(c, "fv" if i == 0 else "uv", 0)[0]
                    pe.wait_ge(*taken(c, u))
                    pe.wait_ge(*taken(c, u + 1))
                n, _, s = spot_of(c, ("turn", i))
                pe.wait_ge(*spot_taken[s].at(c, n // 3 + 1))
                banks = free_spot(c, ("values", i))
                for e in range(2):
                    col = (2 * p + e) * HD
                    dst = banks[HD * e:HD * e + HD, 0, :]
                    pe.matmul(dst[:, 0:P], vn[:, 0, col:col + HD], probT[:, i % 2, e, 0:P], start=True, stop=True)
                    pe.matmul(dst[:, P:T], vn[:, 0, col:col + HD], probT[:, i % 2, e, P:T], start=True, stop=False)
                    mm = pe.matmul(dst[:, P:T], vn[:, 1, col:col + HD], probT[:, i % 2, e, T:T + P],
                                   start=False, stop=True)
                mm.then_inc(spot_ready.handle, 1)

            def krot(c):
                banks = free_spot(c, ("krot", 0))
                pe.matmul(banks[:, 0, 0:T], rot, lat[:, 3, :], start=True, stop=True).then_inc(spot_ready.handle, 1)

            def qrot(c):
                u = unit(c, "uq", 0)[0]
                pe.wait_ge(*taken(c, u + 2))
                pe.wait_ge(*taken(c, u + 3))
                banks = free_spot(c, ("qrot", 0))
                for b in range(2):
                    mm = pe.matmul(banks[:, b, :], rot, qr[:, 2 * b:2 * b + 2, :], start=True, stop=True)
                mm.then_inc(spot_ready.handle, 1)

            def l2(c):
                pe.wait_ge(*squares.at(c, 4))
                for j in range(2):
                    banks = free_spot(c, ("l2", 0), j)
                    for b in range(2):
                        mm = pe.matmul(banks[:, b, :], blk, sq[:, 4 * j + 2 * b:4 * j + 2 * b + 2, :],
                                       start=True, stop=True)
                    mm.then_inc(spot_ready.handle, 1)

            def spread(c):
                for j, (r, n, k) in enumerate(((ROWB, H, 1), (ROWA, ROWS, 4))):
                    banks = free_spot(c, ("spread", 0), j)
                    for p in range(PAIRS):
                        mm = pe.matmul(banks[:, p // 2, p % 2 * T:p % 2 * T + T],
                                       cst[r:r + n, C_PAIR + p * P:C_PAIR + p * P + P], row[r:r + n, k, :],
                                       start=True, stop=True)
                    mm.then_inc(spot_ready.handle, 1)

            def natural(c):
                pe.wait_ge(*l2_made.at(c, 1))
                for j in range(2):
                    banks = free_spot(c, ("natural", 0), j)
                    for t in range(TT):
                        for p in range(PAIRS):
                            mm = pe.matmul(banks[:, t, p * P:p * P + P],
                                           qkv[:, 4 + 4 * j + p, t * P:t * P + P], ident,
                                           start=True, stop=True, is_transpose=True)
                    mm.then_inc(spot_ready.handle, 1)

            def decay(c):
                for t in range(TT):
                    banks = free_spot(c, ("decay", 0), t)
                    tok = slice(t * P, t * P + P)
                    for e in range(2):
                        for p in range(PAIRS):
                            dst = banks[:, e, p * P:p * P + P]
                            one = head_row(H + 2 * p + e).to_broadcast([ROWS, P])
                            pe.matmul(dst, one, row[ROWA:ROWA + ROWS, 2, tok], start=True, stop=False)
                            pe.matmul(dst, row[ROWA:ROWA + ROWS, 1, tok], one, start=False, stop=False)
                            mm = pe.matmul(dst, identb[:, :], delta_mask[:, :], start=False, stop=True)
                    mm.then_inc(spot_ready.handle, 1)

            def pairwise(c, name, rhs, signal_):
                pe.wait_ge(*signal_)
                for t in range(TT):
                    banks = free_spot(c, (name, 0), t)
                    tok = slice(t * P, t * P + P)
                    for e in range(2):
                        half = slice(HD * e, HD * e + HD)
                        for p in range(PAIRS):
                            mm = pe.matmul(banks[:, e, p * P:p * P + P], qkv[half, 4 + p, tok], rhs[half, p, tok],
                                           start=True, stop=True)
                    mm.then_inc(spot_ready.handle, 1)

            def sixteen(banks, t, lhs, rhs, turned=False):
                for e in range(2):
                    for p in range(PAIRS):
                        mm = pe.matmul(banks[:, e, p * P:p * P + P], lhs[:, t, e, p, :],
                                       rhs if turned else rhs[:, t, e, p, :], start=True, stop=True,
                                       is_transpose=turned)
                mm.then_inc(spot_ready.handle, 1)

            def level1(c):
                pe.wait_ge(*level_made.at(c, 1))
                for t in range(TT):
                    sixteen(free_spot(c, ("level1", 0), t), t, inv_t, ident, turned=True)

            def taken_spot(c, step, i):
                n, _, s = spot_of(c, step, i)
                pe.wait_ge(*spot_taken[s].at(c, n // 3 + 1))

            def level(c, s):
                before = ("level1", 0) if s == 1 else ("level", s - 1)
                pe.wait_ge(*level_made.at(c, s + 1))
                for t in range(TT):
                    taken_spot(c, before, t if s == 1 else 2 + 2 * t)
                    sixteen(free_spot(c, ("level", s), t), t, b_m, inv)
                for t in range(TT):
                    if s < 5:
                        taken_spot(c, ("level", s), t)
                        if s > 1:
                            taken_spot(c, before, 3 + 2 * t)
                        sixteen(free_spot(c, ("level", s), 2 + 2 * t), t, inv_t, x_m)
                        sixteen(free_spot(c, ("level", s), 3 + 2 * t), t, x_m, inv_t)
                    else:
                        taken_spot(c, ("level", s), t)
                        taken_spot(c, before, 3 + 2 * t)
                        sixteen(free_spot(c, ("level", s), 2 + t), t, x_m, inv_t)

            def wu(c):
                taken_spot(c, ("level", 5), 2)
                taken_spot(c, ("level", 5), 3)
                banks = free_spot(c, ("wu", 0), 0)
                for h in range(H):
                    p, e = h // 2, h % 2
                    for t in range(TT):
                        mm = pe.matmul(banks[HD * e:HD * e + HD, p // 2, p % 2 * T + t * P:p % 2 * T + t * P + P],
                                       kbe[:, t, h * HD:h * HD + HD], inv_t[:, t, e, p, :], start=True, stop=True)
                mm.then_inc(spot_ready.handle, 1)
                banks = free_spot(c, ("wu", 0), 1)
                for h in range(H):
                    for t in range(TT):
                        mm = pe.matmul(banks[:, t, h * HD:h * HD + HD], inv_t[:, t, h % 2, h // 2, :],
                                       vb[:, t, h * HD:h * HD + HD], start=True, stop=True)
                mm.then_inc(spot_ready.handle, 1)

            def scan_v(c, k):
                if k == 0:
                    taken_spot(c, ("wu", 0), 0)
                banks = free_spot(c, ("scan_v", k))
                pe.wait_ge(*state_made.at(c, k + 1))
                half = slice(HD * (k % 2), HD * (k % 2) + HD)
                for p in range(PAIRS):
                    mm = pe.matmul(banks[half, 0, p * P:p * P + P], w_t[:, p, k * CHUNK:(k + 1) * CHUNK],
                                   state[:, p, :], start=True, stop=True)
                mm.then_inc(spot_ready.handle, 1)

            def scan_s(c, k):
                taken_spot(c, ("scan_v", k), 0)
                banks = free_spot(c, ("scan_s", k))
                t, r = k // 2, HD * (k % 2)
                for p in range(PAIRS):
                    pe.matmul(banks[:, 0, p * CHUNK:(p + 1) * CHUNK], state[:, p, :],
                              q_dec[:, p, k * CHUNK:(k + 1) * CHUNK], start=True, stop=False, skip_group_check=True)
                    for e in range(2):
                        h = 2 * p + e
                        pe.matmul(banks[HD * e:HD * e + HD, 0, p * CHUNK:(p + 1) * CHUNK],
                                  vnew[:, h * HD:h * HD + HD], qk_t[:, t, e, p, r:r + CHUNK],
                                  start=False, stop=True, skip_group_check=True)
                for p in range(PAIRS):
                    mm = pe.matmul(banks[:, 1, p * P:p * P + P], kdn[r:r + HD, t, p * P:p * P + P],
                                   vnew[r:r + HD, p * P:p * P + P], start=True, stop=True)
                mm.then_inc(spot_ready.handle, 1)

            def onorm(c):
                pe.wait_ge(*squares.at(c, 5))
                banks = free_spot(c, ("onorm", 0))
                for b in range(2):
                    mm = pe.matmul(banks[:, b, :], blk, sq[:, 2 * b:2 * b + 2, :], start=True, stop=True)
                mm.then_inc(spot_ready.handle, 1)

            def branch(c, i):
                b, u = i // 4, unit(c, "br", i // 2, i % 2)[0]
                w = group(c, "br", i // 2)
                dst = free_unit(c, u)
                if i == 8:
                    pe.wait_ge(*delta_done.at(c, 1))
                if i in (0, 4):
                    taken_spot(c, ("values", 4 * b + 3), 0)
                src = (o_att[:, 0:4, :], o_att[:, 4:8, :], o_dn)[b]
                for m in range(2):
                    mm = product(dst[:, m * T:m * T + T], w, 4, 512, (2 * (i % 2) + m) * P, src)
                mm.then_inc(lin_ready.handle, 1)

            def mix_out(c, i):
                u = unit(c, "out", i // 2, i % 2)[0]
                w = group(c, "out", i // 2)
                dst = free_unit(c, u)
                if i == 0:
                    pe.wait_ge(*merged_made.at(c, 1))
                for m in range(2):
                    mm = product(dst[:, m * T:m * T + T], w, KD, 512, (2 * (i % 2) + m) * P, merged)
                mm.then_inc(lin_ready.handle, 1)

            def mixer(c):
                for step, i in MIXER:
                    if step == "norm":
                        norm(c, i)
                        pe.wait_ge(*normed.at(c, KD * 2))
                    elif step == "lin":
                        plain(c, i[0], 0, i[1])
                    elif step == "gate":
                        plain(c, "gate", i // 2, i % 2)
                    elif step == "kk":
                        pairwise(c, "kk", k_beta, k_beta_made.at(c, 1))
                    elif step == "qk":
                        pairwise(c, "qk", qkv, k_beta_made.at(c, 1))
                    elif step in ("latnorm", "rowcols", "krot", "qrot", "l2", "spread", "natural", "decay", "level1", "wu", "onorm"):
                        {"latnorm": latnorm, "rowcols": rows, "krot": krot, "qrot": qrot, "l2": l2, "spread": spread,
                         "natural": natural, "decay": decay, "level1": level1, "wu": wu, "onorm": onorm}[step](c)
                    elif step not in ("conv", "soft", "rows"):
                        {"scores": scores, "turn": turn, "values": values, "level": level, "scan_v": scan_v,
                         "scan_s": scan_s, "br": branch, "out": mix_out}[step](c, i)

            def adaln():
                pe.wait_ge(cond_made, 1)
                with pe.Fori(0, DEPTH * 2) as it:
                    c = Place("ada")
                    for s in range(6):
                        pe.wait_ge(*loaded[s % SLOTS].at(c, it * 32 + (s // SLOTS + 1) * 16))
                        dst = free_unit(c, s, it * 3)
                        for kt in range(KD):
                            q = kt % 4
                            mm = pe.matmul(dst[32 * q:32 * q + 32, :], cond_s[:, kt, :],
                                           slot[s % SLOTS][:, kt * 512:kt * 512 + 512], start=(kt < 4), stop=(kt >= 4))
                        mm.then_inc(lin_ready.handle, 1)
                        banks = free_spot(c, ("ada", s), 0, it * 2)
                        pe.wait_ge(*lin_taken[s % 2].at(c, it * 3 + (s // 2 + 1)))
                        for m in range(4):
                            mm = pe.matmul(banks[:, 0, 2 * m:2 * m + 2], ada_s[:, s % 2, m * P:m * P + P],
                                           cst[:, C_TWO:C_TWO + 2], start=True, stop=True)
                        mm.then_inc(spot_ready.handle, 1)

            def plain_two(c, name, part):
                u, _ = unit(c, name, 0, part)
                w = group(c, name)
                dst = free_unit(c, u)
                if name == "q":
                    for m in range(2):
                        mm = product(dst[:, m * T:m * T + T], w, KD, 512, (2 * part + m) * P, act)
                elif name == "kuv":
                    mm = product(dst[:, 0:T], w, KD, 512, 2 * part * P, act)
                    if part == 0:
                        mm = product(dst[:, T:2 * T], w, KD, 512, P, act)
                    else:
                        for t in range(TT):
                            for kt in range(KD):
                                mm = pe.matmul(dst[:, T + t * P:T + t * P + P], act[:, kt, t * P:t * P + P],
                                               w[:, kt * 512 + 384:kt * 512 + 512], start=(kt == 0), stop=(kt == KD - 1))
                else:
                    for kt in range(KD):
                        mm = pe.matmul(dst, act[:, kt, part * P:part * P + P], w[:, kt * 512:kt * 512 + 512],
                                       start=(kt == 0), stop=(kt == KD - 1))
                mm.then_inc(lin_ready.handle, 1)

            def scores_two(c, i):
                p, tok = i // 2, slice(i % 2 * P, i % 2 * P + P)
                first = 0 if c.sec == "two" else T
                if i == 0:
                    taken_spot(c, ("kdup", 0), 0)
                    if c.sec == "two":
                        pe.wait_ge(*given.at(c, 2))
                banks = free_spot(c, ("scores", i))
                for e in range(2):
                    half = slice(HD * e, HD * e + HD)
                    mm = pe.matmul(banks[:, e, 0:2 * T - first], qk_m[half, p, tok], keys[half, p // 2, first:],
                                   start=True, stop=True)
                mm.then_inc(spot_ready.handle, 1)

            def turn_two(c, i):
                banks = free_spot(c, ("turn", i))
                pe.wait_ge(*prob_made.at(c, i + 1))
                for e in range(2):
                    for b in range(4 if c.sec == "two" else 2):
                        mm = pe.matmul(banks[:, e, b * P:b * P + P], prob2[:, i % 2, e, b * P:b * P + P], ident,
                                       start=True, stop=True, is_transpose=True)
                mm.then_inc(spot_ready.handle, 1)

            def values_two(c, i):
                taken_spot(c, ("turn", i), 0)
                banks = free_spot(c, ("values", i))
                n, first = (4, 0) if c.sec == "two" else (2, 2)
                for e in range(2):
                    for b in range(n):
                        mm = pe.matmul(banks[HD * e:HD * e + HD, 0, 0:P], vals[:, first + b, i // 4 * HD:i // 4 * HD + HD],
                                       probT2[:, e, b * P:b * P + P], start=(b == 0), stop=(b == n - 1))
                mm.then_inc(spot_ready.handle, 1)

            def rest_two(c, step):
                rotated = c.sec == "two"
                if step == "qnorm":
                    pe.wait_ge(*squares.at(c, 2))
                    banks = free_spot(c, (step, 0))
                    for b in range(2):
                        mm = pe.matmul(banks[:, b, :], blk, sq[:, 2 * b:2 * b + 2, :], start=True, stop=True)
                elif step == "knorm":
                    pe.wait_ge(*squares.at(c, 2))
                    banks = free_spot(c, (step, 0))
                    mm = pe.matmul(banks[:, 0, 0:T], blk, sq[:, 4, :], start=True, stop=True)
                elif step == "rot":
                    pe.wait_ge(*qk_scaled.at(c, 1))
                    banks = free_spot(c, (step, 0), 0)
                    for b in range(2):
                        mm = pe.matmul(banks[:, b, :], rot, qk_m[:, 2 * b:2 * b + 2, :], start=True, stop=True)
                    mm.then_inc(spot_ready.handle, 1)
                    banks = free_spot(c, (step, 0), 1)
                    mm = pe.matmul(banks[:, 0, 0:T], rot, qk_m[:, 4, :], start=True, stop=True)
                elif step == "kdup":
                    pe.wait_ge(*(qk_turned if rotated else qk_scaled).at(c, 1))
                    banks = free_spot(c, (step, 0))
                    for k in range(2):
                        mm = pe.matmul(banks[:, 0, k * T:k * T + T], tbl[:, B_DUP + k * P:B_DUP + k * P + P],
                                       qk_m[:, 4, :], start=True, stop=True)
                elif step == "fourier":
                    for t in range(2):
                        pe.wait_ge(*taken(c, unit(c, "fg", 0, t)[0]))
                    banks = free_spot(c, (step, 0), 0)
                    for m in range(2):
                        for t in range(TT):
                            mm = pe.matmul(banks[:, m, :], f_nat[:, t, m * P:m * P + P],
                                           tbl[:, B_DFT + t * 512:B_DFT + t * 512 + 512], start=(t == 0), stop=(t == 1))
                    mm.then_inc(spot_ready.handle, 1)
                    taken_spot(c, (step, 0), 0)
                    banks = free_spot(c, (step, 0), 1)
                    for m in range(2):
                        dst = banks[:, 0, m * T:m * T + T]
                        pe.matmul(dst, tbl[:, B_CD:B_CD + P], f_mid[:, 2 * m, :], start=True, stop=False)
                        mm = pe.matmul(dst, tbl[:, B_SD:B_SD + P], f_mid[:, 2 * m + 1, :], start=False, stop=True)
                elif step == "spatial":
                    pe.wait_ge(*g_made.at(c, 1))
                    banks = free_spot(c, (step, 0))
                    for h in range(4):
                        for t in range(TT):
                            mm = pe.matmul(banks[HD * (h % 2):HD * (h % 2) + HD, 0, h // 2 * T + t * P:h // 2 * T + t * P + P],
                                           g_nat[:, t, h * HD:h * HD + HD], vec_b[:, W_WS + h * P:W_WS + h * P + P],
                                           start=True, stop=True)
                mm.then_inc(spot_ready.handle, 1)

            def out_two(c, i):
                u = unit(c, "out", i // 2, i % 2)[0]
                w = group(c, "out", i // 2)
                dst = free_unit(c, u)
                if i == 0:
                    pe.wait_ge(*mix_made.at(c, 1))
                    taken_spot(c, ("fourier", 0), 1)
                    taken_spot(c, ("values", 7), 0)
                for m in range(2):
                    mm = product(dst[:, m * T:m * T + T], w, KD, 512, (2 * (i % 2) + m) * P, o_att)
                mm.then_inc(lin_ready.handle, 1)

            def two(c, order):
                for step, i in order:
                    if step == "norm":
                        norm(c, i)
                        if i == 0:
                            pe.wait_ge(*normed.at(c, KD))
                    elif step == "lin":
                        plain_two(c, *i)
                    elif step in ("scores", "turn", "values", "out"):
                        {"scores": scores_two, "turn": turn_two, "values": values_two, "out": out_two}[step](c, i)
                    elif step not in ("squares", "soft"):
                        rest_two(c, step)
                if c.sec == "kv":
                    return
                n0, u0 = GROUP[c.sec]["m1", 0]

                def up(it, s):
                    n = n0 + s
                    pe.wait_ge(*normed.at(c, 2 * KD))
                    pe.wait_ge(*loaded[n % SLOTS].at(c, it * 16 + (n // SLOTS + 1) * 16))
                    for part in range(2):
                        dst = free_unit(c, u0 + 2 * s + part, it * 3)
                        for m in range(2):
                            mm = product(dst[:, m * T:m * T + T], slot[n % SLOTS], KD, 512, (2 * part + m) * P, act)
                        mm.then_inc(lin_ready.handle, 1)

                with pe.Fori(0, 2) as it:
                    for s in range(3):
                        up(it, s)
                for s in range(6, 8):
                    up(0, s)
                u1 = GROUP[c.sec]["m2", 0][1]
                pe.wait_ge(*taken(c, u1 - 1))
                pe.wait_ge(*taken(c, u1 - 2))
                for m in range(KD):
                    w = group(c, "m2", m)
                    dst = free_unit(c, u1 + m)
                    product(dst[:, 0:T], w, KF2, P, 0, hT).then_inc(lin_ready.handle, 1)

            pe.wait_ge(consts_made, 1)
            adaln()
            pe.wait_ge(tables_here.handle, 16)
            two(Place("ctx"), CTX)
            two(Place("kv"), KV)
            with pe.Fori(0, DEPTH) as l:
                c = Place("one", l)
                ffn(c, 0)
                mixer(c)
                ffn(c, 1)
            norm(Place("fin"), 0)
            pe.wait_ge(tables_again, 16)
            with pe.Fori(0, DEPTH) as l:
                two(Place("two", l), TWO)

        @block.scalar
        def _(act_e):
            e_ = act_e

            def activate(dst, src, func, **kw):
                return nc.scalar.activation(dst, src, func, **kw)

            def wait_spot(c, step, i=0):
                n, banks, s = spot_of(c, step, i)
                e_.wait_ge(*spot_ready.at(c, n + 1))
                return banks, spot_taken[s].handle

            def wait_unit(c, u, before=0):
                e_.wait_ge(*lin_ready.at(c, before + u + 1))
                return lin[:, u % 2, :], lin_taken[u % 2].handle

            def root(dst, src, scale, signal_):
                activate(dst, src, ACT.Ln, scale=scale, bias=EPS).then_inc(signal_, 1)
                e_.drain()
                return activate(dst, dst, ACT.Exp, scale=-0.5)

            def norm(c, i, last_unit):
                e_.drain()
                for u in last_unit:
                    e_.wait_ge(*taken(c, u))
                activate(sq[:, :, :], xT[:, :, :], ACT.Square).then_inc(squares.handle, 1)
                e_.preload_act_table_set(EXP_LN)
                banks, free = wait_spot(c, ("norm", i))
                root(rstd[:, :], banks[:, 0, 0:T], 1.0 / D, free).then_inc(rstds.handle, 1)

            def ffn(c, which):
                ubase = (0, FFN2_UNIT)[which]
                norm(c, 2 * which, (ubase - 1, ubase - 2))
                if which == 0:
                    e_.wait_ge(*vec_here.at(c, 16))

                def gu(it, s):
                    for f in range(2):
                        u = ubase + 2 * s + f
                        e_.wait_ge(*lin_taken[u % 2].at(c, it * 3 + u // 2))
                        src, _ = wait_unit(c, u, it * 6)
                        activate(sg[:, f, :], src[:, 0:T], ACT.Silu).then_inc(gate_made.handle, 1)

                with e_.Fori(0, GU_GROUPS // 3) as it:
                    for s in range(3):
                        gu(it, s)
                for s in range(GU_GROUPS // 3 * 3, GU_GROUPS):
                    gu(0, s)

            def plain(c, name, part):
                u = unit(c, name, 0, part)[0]
                if name == "lat":
                    src, free = wait_unit(c, u)
                    activate(lat[:, 2 * part:2 * part + 2, :].rearrange("p a t -> p (a t)"), src, ACT.Copy).then_inc(free, 1)
                if name == "fq":
                    src, free = wait_unit(c, u)
                    activate(qk_f[:, 2 * part:2 * part + 2, :].rearrange("p a t -> p (a t)"), src, ACT.Copy, scale=FOX_SCALE
                             ).then_inc(free, 1)
                if name in ("dq", "dk", "dv"):
                    src, free = wait_unit(c, u)
                    at = 4 * ("dq", "dk", "dv").index(name) + 2 * part
                    activate(conv_in[:, at:at + 2, TAPS - 1:], src.rearrange("p (a t) -> p a t", a=2), ACT.Copy
                             ).then_inc(free, 1)
                if name == "uq":
                    src, free = wait_unit(c, u)
                    dst = qk_m[:, 2 * part:2 * part + 2, :] if part < 2 else qr[:, 2 * part - 4:2 * part - 2, :]
                    activate(dst.rearrange("p a t -> p (a t)"), src, ACT.Copy, scale=MLA_SCALE).then_inc(free, 1)
                if name == "uk":
                    src, free = wait_unit(c, u)
                    activate(qk_m[:, 4 + 2 * part:6 + 2 * part, :].rearrange("p a t -> p (a t)"), src, ACT.Copy
                             ).then_inc(free, 1)
                if name == "dz":
                    src, free = wait_unit(c, u)
                    if part == 0:
                        e_.wait_ge(*rope_k.at(c, 1))
                        e_.wait_ge(*lat_made.at(c, 1))
                    activate(zs[:, 2 * part:2 * part + 2, :].rearrange("p a t -> p (a t)"), src, ACT.Copy
                             ).then_inc(free, 1)

            def latnorm(c):
                u = unit(c, "lat", 0)[0]
                e_.wait_ge(*taken(c, u))
                e_.wait_ge(*taken(c, u + 1))
                activate(sq[:, 0:3, :], lat[:, 0:3, :], ACT.Square).then_inc(squares.handle, 1)
                banks, free = wait_spot(c, ("latnorm", 0))
                activate(sg[:, 0, :], banks[:, 0, 0:T], ACT.Ln, scale=1.0 / 256, bias=EPS)
                activate(sg[:, 1, :], banks[:, 0, T:2 * T], ACT.Ln, scale=1.0 / P, bias=EPS).then_inc(free, 1)
                e_.drain()
                activate(sg[:, :, :], sg[:, :, :], ACT.Exp, scale=-0.5).then_inc(rstds.handle, 1)

            def rows(c):
                e_.wait_ge(*rows_abs.at(c, 1))
                a, b = slice(ROWA, ROWA + ROWS), slice(ROWB, ROWB + H)
                activate(row[a, 3, :], row[a, 3, :], ACT.Exp, scale=-1.0)
                activate(row[b, 0, :], lat[b, 3, :], ACT.Exp, scale=-1.0)
                activate(alog[a, :], vec[a, V_ALOG:V_ALOG + 1], ACT.Exp)
                e_.drain()
                activate(row[a, 3, :], row[a, 3, :], ACT.Ln, bias=1.0).then_inc(rows_exp.handle, 1)
                e_.wait_ge(*rows_cum.at(c, 1))
                activate(row[a, 4, :], row[a, 2, :], ACT.Exp)
                activate(row[a, 5, :], row[a, 3, :], ACT.Exp).then_inc(rows_done.handle, 1)

            def scores(c, i):
                banks, free = wait_spot(c, ("scores", i))
                e_.wait_ge(*max_made.at(c, i + 1))
                if i >= 2:
                    e_.wait_ge(*spot_ready.at(c, SPOT[c.sec]["turn", i - 2] + 1))
                for e in range(2):
                    for t, cols_ in enumerate((slice(0, P), slice(P, P + T))):
                        ins = activate(prob[:, i % 2, e, cols_], banks[:, e, cols_], ACT.Exp,
                                       bias=mx[:, i % 2, t, e:e + 1], accum_out=rs[:, i % 2, t, e:e + 1])
                ins.then_inc(free, 1)

            def turn(c, i):
                if i >= 2:
                    e_.wait_ge(*spot_ready.at(c, SPOT[c.sec]["values", i - 2] + 1))
                banks, free = wait_spot(c, ("turn", i))
                activate(probT[:, i % 2, :, :], banks[:, :, 0:384], ACT.Copy).then_inc(free, 1)

            def conv(c):
                e_.wait_ge(*conv_done.at(c, 1))
                activate(qkv[:, :, :], qkv[:, :, :], ACT.Silu)
                e_.drain()
                activate(sq[:, :, :], qkv[:, 0:8, :], ACT.Square).then_inc(squares.handle, 1)
                e_.preload_act_table_set(EXP_LN)

            def l2(c):
                for j in range(2):
                    banks, free = wait_spot(c, ("l2", 0), j)
                    dst = sq[:, 4 * j:4 * j + 4, :].rearrange("p (b a) t -> p b (a t)", b=2)
                    root(dst, banks, 1.0, free).then_inc(rstds.handle, 1)

            def decay(c):
                e_.wait_ge(*l2_made.at(c, 1))
                for t in range(TT):
                    banks, free = wait_spot(c, ("decay", 0), t)
                    activate(x_m[:, t].rearrange("p e q c -> p e (q c)"), banks, ACT.Exp).then_inc(free, 1)

            def copy_mats(c, step, i, dst, t):
                banks, free = wait_spot(c, step, i)
                activate(dst[:, t].rearrange("p e q c -> p e (q c)"), banks, ACT.Copy).then_inc(free, 1)

            def wu(c):
                banks, free = wait_spot(c, ("wu", 0), 0)
                activate(w_t.rearrange("p (b a) t -> p b (a t)", b=2), banks, ACT.Copy).then_inc(free, 1)

            def onorm(c):
                e_.wait_ge(*state_made.at(c, 1 + CHUNKS))
                activate(sq[:, 0:4, :], o_dn, ACT.Square).then_inc(squares.handle, 1)
                e_.preload_act_table_set(EXP_LN)
                banks, free = wait_spot(c, ("onorm", 0))
                root(sq[:, 4:8, :].rearrange("p (b a) t -> p b (a t)", b=2), banks, 1.0 / HD, free
                     ).then_inc(rstds.handle, 1)

            def gate(c, i):
                u = unit(c, "gate", i // 2, i % 2)[0]
                src, free = wait_unit(c, u)
                if i >= 2:
                    e_.wait_ge(*taken(c, unit(c, "br", (i - 2) // 2, i % 2)[0]))
                for m in range(2):
                    col = V_BGATE + 2 * i + m
                    ins = activate(gt[:, i % 2, m, :], src[:, m * T:m * T + T], ACT.Sigmoid, bias=vec[:, col:col + 1])
                ins.then_inc(free, 1)

            def mixer(c):
                for step, i in MIXER:
                    e_.drain()
                    if step == "norm":
                        norm(c, 1, (FFN_UNITS - 1, FFN_UNITS - 2))
                    elif step == "lin":
                        plain(c, *i)
                    elif step == "level1":
                        activate(zs, zs, ACT.Silu).then_inc(z_made.handle, 1)
                        for t in range(TT):
                            copy_mats(c, ("level1", 0), t, inv, t)
                    elif step == "level":
                        for t in range(TT):
                            copy_mats(c, ("level", i), t, x_m, t)
                    elif step in ("scores", "turn", "gate"):
                        {"scores": scores, "turn": turn, "gate": gate}[step](c, i)
                    elif step in ("latnorm", "rows", "l2", "decay", "wu", "onorm") or (step, i) == ("conv", TAPS - 1):
                        {"latnorm": latnorm, "rows": rows, "conv": conv, "l2": l2, "decay": decay, "wu": wu,
                         "onorm": onorm}[step](c)

            def adaln():
                e_.wait_ge(cond_here, 16)
                activate(cond_s, cond_s, ACT.Silu).then_inc(cond_made, 1)
                with e_.Fori(0, DEPTH * 2) as it:
                    c = Place("ada")
                    for s in range(6):
                        src, free = wait_unit(c, s, it * 6)
                        if s >= 2:
                            e_.wait_ge(*spot_ready.at(c, it * 6 + (s - 1)))
                        else:
                            e_.wait_ge(*spot_ready.at(c, it * 6))
                        activate(ada_s[:, s % 2, :], src, ACT.Copy).then_inc(free, 1)

            def lin_two(c, name, part):
                if name == "q":
                    return
                u = unit(c, name, 0, part)[0]
                src, free = wait_unit(c, u)
                if name == "kuv":
                    if c.sec == "kv":
                        e_.wait_ge(*kept.at(c, 0))
                    if part == 0:
                        activate(qk_m[:, 4, :], src[:, 0:T], ACT.Copy)
                        activate(u_two[:, 0, :], src[:, T:2 * T], ACT.Gelu_apprx_tanh).then_inc(free, 1)
                    else:
                        activate(u_two[:, 1, :], src[:, 0:T], ACT.Gelu_apprx_tanh)
                        activate(vals[:, TT:, :], src[:, T:2 * T].rearrange("p (t c) -> p t c", t=TT), ACT.Copy
                                 ).then_inc(free, 1)
                else:
                    activate(g_nat[:, part, :], src[:, T:2 * T], ACT.Gelu_apprx_tanh)
                    activate(f_nat[:, part, :], src[:, 0:T], ACT.Copy).then_inc(free, 1)

            def scores_two(c, i):
                banks, free = wait_spot(c, ("scores", i))
                n = 2 * T if c.sec == "two" else T
                e_.wait_ge(*max_made.at(c, i + 1))
                if i >= 2:
                    e_.wait_ge(*spot_ready.at(c, SPOT[c.sec]["turn", i - 2] + 1))
                for e in range(2):
                    ins = activate(prob2[:, i % 2, e, 0:n], banks[:, e, 0:n], ACT.Exp,
                                   bias=mx[:, i % 2, 0, e:e + 1], accum_out=rs[:, i % 2, 0, e:e + 1])
                ins.then_inc(free, 1)

            def rest_two(c, step):
                if step == "squares":
                    for part in range(2):
                        e_.wait_ge(*taken(c, unit(c, "q", 0, part)[0]))
                    activate(sq[:, 0:5, :], qk_m[:, 0:5, :], ACT.Square).then_inc(squares.handle, 1)
                elif step == "qnorm":
                    e_.preload_act_table_set(EXP_LN)
                    banks, free = wait_spot(c, (step, 0))
                    root(sq[:, 0:4, :].rearrange("p (b a) t -> p b (a t)", b=2), banks, 1.0 / HD, free
                         ).then_inc(rstds.handle, 1)
                elif step == "knorm":
                    if c.sec == "kv":
                        activate(sq[:, 4, :], qk_m[:, 4, :], ACT.Square).then_inc(squares.handle, 1)
                        e_.preload_act_table_set(EXP_LN)
                    banks, free = wait_spot(c, (step, 0))
                    root(sq[:, 4, :], banks[:, 0, 0:T], 1.0 / HD, free).then_inc(rstds.handle, 1)
                    if c.sec != "kv":
                        e_.wait_ge(*g_sums.at(c, 1))
                        activate(cols[:, 0, 0:8], cols[:, 0, 0:8], ACT.Ln, scale=1.0 / HD, bias=EPS)
                        e_.drain()
                        activate(cols[:, 0, 0:8], cols[:, 0, 0:8], ACT.Exp, scale=-0.5).then_inc(rstds.handle, 1)
                elif step == "kdup":
                    banks, free = wait_spot(c, (step, 0))
                    activate(keys[:, :, T:], banks[:, 0, :].rearrange("p (k t) -> p k t", k=2), ACT.Copy,
                             scale=HD ** -0.5).then_inc(free, 1)
                elif step == "fourier":
                    banks, free = wait_spot(c, (step, 0), 0)
                    activate(f_mid.rearrange("p (m a) t -> p m (a t)", m=2), banks, ACT.Copy).then_inc(free, 1)

            def two(c, order):
                for step, i in order:
                    e_.drain()
                    if step == "norm":
                        if i == 0:
                            norm(c, i, (-1, -2))
                        else:
                            u = unit(c, "out", 1, 1)[0]
                            norm(c, i, (u, u - 1))
                    elif step == "lin":
                        lin_two(c, *i)
                    elif step == "scores":
                        scores_two(c, i)
                    elif step == "turn":
                        if i:
                            e_.wait_ge(*spot_ready.at(c, SPOT[c.sec]["values", i - 1] + 1))
                        banks, free = wait_spot(c, ("turn", i))
                        n = 2 * T if c.sec == "two" else T
                        activate(probT2[:, :, 0:n], banks[:, :, 0:n], ACT.Copy).then_inc(free, 1)
                    else:
                        rest_two(c, step)
                if c.sec == "kv":
                    return
                u0 = GROUP[c.sec]["m1", 0][1]

                def up(it, s):
                    for k in (2 * s, 2 * s + 1):
                        e_.wait_ge(*lin_taken[(k - 1) % 2].at(c, it * 3 + (u0 + k - 1) // 2 + 1))
                        src, _ = wait_unit(c, u0 + k, it * 6)
                        activate(sg[:, :, :].rearrange("p a t -> p (a t)"), src, ACT.Relu).then_inc(gate_made.handle, 1)

                with e_.Fori(0, 2) as it:
                    for s in range(3):
                        up(it, s)
                for s in range(6, 8):
                    up(0, s)

            e_.wait_ge(turn_here, 1)
            activate(cossin[:, 1, :], sq[:, 0, :], ACT.Sin)
            activate(cossin[:, 0, :], sq[:, 1, :], ACT.Sin).then_inc(turn_done, 1)
            adaln()
            e_.wait_ge(ctx_here, 16)
            two(Place("ctx"), CTX)
            two(Place("kv"), KV)
            e_.wait_ge(*kept.at(Place("one"), 0))
            e_.wait_ge(x_here, 16)
            with e_.Fori(0, DEPTH) as l:
                c = Place("one", l)
                ffn(c, 0)
                mixer(c)
                ffn(c, 1)
            norm(Place("fin"), 0, (-1, -2))
            e_.wait_ge(*normed.at(Place("two"), 0))
            with e_.Fori(0, DEPTH) as l:
                two(Place("two", l), TWO)

        @block.vector
        def _(ve):
            def wait_spot(c, step, i=0):
                n, banks, s = spot_of(c, step, i)
                ve.wait_ge(*spot_ready.at(c, n + 1))
                return banks, spot_taken[s].handle

            def wait_unit(c, u, before=0):
                ve.wait_ge(*lin_ready.at(c, before + u + 1))
                return lin[:, u % 2, :], lin_taken[u % 2].handle

            def two(tile):
                return tile.rearrange("p (a t) -> p a t", a=2)

            def norm(c, i, dst, gain, k_sq, k_rs):
                ve.drain()
                ve.wait_ge(*squares.at(c, k_sq))
                ve.tensor_reduce(part[:, :], sq[:, :, :].rearrange("p k t -> p t k"), AX_X, ALU.add
                                 ).then_inc(sums.handle, 1)
                if c.sec == "one" and i == 0:
                    ve.wait_ge(*vec_here.at(c, 16))
                ve.wait_ge(*rstds.at(c, k_rs))
                for kt in range(KD):
                    ve.scalar_tensor_tensor(dst[:, kt, :], xT[:, kt, :], gain[:, kt:kt + 1], rstd[:, :],
                                            ALU.mult, ALU.mult).then_inc(normed.handle, 1)

            def ffn(c, which):
                ubase, gain = ((0, V_FFN1), (FFN2_UNIT, V_FFN2))[which]
                norm(c, 2 * which, act, vec[:, gain:gain + KD], (1, 6)[which], (1, 7)[which])
                def gu(it, s):
                    for f in range(2):
                        u = ubase + 2 * s + f
                        silus = 2 * GU_GROUPS * which + 2 * s + f + 1
                        ve.wait_ge(*gate_made.at(c, it * 6 + silus))
                        src, free = wait_unit(c, u, it * 6)
                        ve.tensor_tensor(hT[:, it * 6 + (2 * s + f), :], sg[:, f, :], src[:, T:2 * T], ALU.mult
                                         ).then_inc(free, 1)

                with ve.Fori(0, GU_GROUPS // 3) as it:
                    for s in range(3):
                        gu(it, s)
                for s in range(GU_GROUPS // 3 * 3, GU_GROUPS):
                    gu(0, s)
                for m in range(KD):
                    src, free = wait_unit(c, ubase + 2 * GU_GROUPS + m)
                    ve.scalar_tensor_tensor(xT[:, m, :], src[:, 0:T], 0.5, xT[:, m, :], ALU.mult, ALU.add
                                            ).then_inc(free, 1)

            def plain(c, name, part):
                u = unit(c, name, 0, part)[0]
                if name == "fk":
                    src, free = wait_unit(c, u)
                    ve.tensor_copy(qk_f[:, 4 + 2 * part:6 + 2 * part, :], two(src)).then_inc(free, 1)
                if name in ("fv", "uv"):
                    src, free = wait_unit(c, u)
                    ve.tensor_copy((vn_f if name == "fv" else vn_m)[:, part, :], src).then_inc(free, 1)

            def latnorm(c):
                ve.wait_ge(*rstds.at(c, 3))
                for j in range(3):
                    ins = ve.scalar_tensor_tensor(latn[:, j, :], lat[:, j, :], vec[:, V_QN + j:V_QN + j + 1],
                                                  sg[:, j // 2, :], ALU.mult, ALU.mult)
                ins.then_inc(lat_made.handle, 1)

            def rows(c):
                a, b = slice(ROWA, ROWA + ROWS), slice(ROWB, ROWB + H)
                ve.tensor_scalar(row[a, 0, :], lat[a, 3, :], vec[a, V_BIAS:V_BIAS + 1], cst[a, C_SIGN:C_SIGN + 1],
                                 ALU.add, ALU.mult)
                ve.drain()
                ve.scalar_tensor_tensor(row[a, 3, :], row[a, 0, :], -1.0, row[a, 0, :], ALU.mult, ALU.max
                                        ).then_inc(rows_abs.handle, 1)
                ve.wait_ge(*rows_exp.at(c, 1))
                ve.scalar_tensor_tensor(row[a, 0, :], row[a, 0, :], 0.0, row[a, 3, :], ALU.max, ALU.add)
                ve.tensor_scalar(row[b, 0, :], row[b, 0, :], 1.0, None, ALU.add)
                ve.drain()
                ve.tensor_scalar(row[a, 0, :], row[a, 0, :], alog[a, 0:1], None, ALU.mult)
                ve.reciprocal(row[b, 1, :], row[b, 0, :])
                ve.drain()
                ve.tensor_tensor_scan(row[a, 1, :], cst[a, C_RESET:C_RESET + T], row[a, 0, :], 0.0, ALU.mult, ALU.add)
                ve.drain()
                chunks = row[a, 1, :].rearrange("p (c i) -> p c i", c=CHUNKS)
                ve.tensor_tensor(row[a, 3, :].rearrange("p (c i) -> p c i", c=CHUNKS), chunks,
                                 chunks[:, :, CHUNK - 1:CHUNK].to_broadcast([ROWS, CHUNKS, CHUNK]), ALU.subtract)
                ve.tensor_scalar(row[a, 2, :], row[a, 1, :], -1.0, None, ALU.mult).then_inc(rows_cum.handle, 1)

            def rowcols(c):
                banks, free = wait_spot(c, ("rowcols", 0))
                ve.tensor_copy(cols[:, :, 0:32], banks[:, 0, 0:96].rearrange("p (t k) -> p t k", t=TT)[:, :, 0:32])
                ve.tensor_copy(cols[:, :, 32:40], banks[:, 1, 0:16].rearrange("p (t k) -> p t k", t=TT)
                               ).then_inc(free, 1)
                ve.drain()
                ve.tensor_tensor(cols[:, :, 40:48], cols[:, :, 32:40], cols[:, :, 8:16], ALU.mult)

            def krot(c):
                banks, free = wait_spot(c, ("krot", 0))
                ve.tensor_tensor(part[:, :], banks[:, 0, 0:T], cossin[:, 1, :], ALU.mult).then_inc(free, 1)
                ve.tensor_tensor(kr[:, :], lat[:, 3, :], cossin[:, 0, :], ALU.mult)
                ve.drain()
                ve.tensor_tensor(kr[:, :], kr[:, :], part[:, :], ALU.add).then_inc(rope_k.handle, 1)

            def qrot(c):
                banks, free = wait_spot(c, ("qrot", 0))
                def table(k):
                    return cossin[:, k, :].unsqueeze(1).to_broadcast([P, PAIRS, T])
                turned = hT[:, 0:4, :]
                ve.tensor_tensor(turned, banks.rearrange("p b (a t) -> p (b a) t", a=2), table(1), ALU.mult
                                 ).then_inc(free, 1)
                ve.tensor_tensor(qr[:, :, :], qr[:, :, :], table(0), ALU.mult)
                ve.drain()
                ve.tensor_tensor(qr[:, :, :], qr[:, :, :], turned, ALU.add).then_inc(rope_q.handle, 1)

            def scores(c, i):
                banks, _ = wait_spot(c, ("scores", i))
                for t, cols_ in enumerate((slice(0, P), slice(P, P + T))):
                    ins = ve.tensor_reduce(mx[:, i % 2, t, :], banks[:, :, cols_], AX_X, ALU.max, negate=True)
                ins.then_inc(max_made.handle, 1)

            def normalise(c, i):
                n, _, s = spot_of(c, ("scores", i))
                ve.wait_ge(*spot_taken[s].at(c, n // 3 + 1))
                ve.reciprocal(rs[:, i % 2, :, :], rs[:, i % 2, :, :])
                ve.drain()
                for t, cols_ in enumerate((slice(0, P), slice(P, P + T))):
                    keys = cols_.stop - cols_.start
                    ins = ve.tensor_tensor(prob[:, i % 2, :, cols_], prob[:, i % 2, :, cols_],
                                           rs[:, i % 2, t, :].unsqueeze(2).to_broadcast([P, 2, keys]), ALU.mult)
                ins.then_inc(prob_made.handle, 1)

            def values(c, i):
                banks, free = wait_spot(c, ("values", i))
                ve.tensor_copy(o_att[:, i, :], banks[:, 0, 0:T]).then_inc(free, 1)

            def conv(c, tap):
                u = unit(c, "dv", 0)[0]
                ve.wait_ge(*taken(c, u))
                ve.wait_ge(*taken(c, u + 1))
                for m in range(12):
                    w = vec[:, V_TAP + 12 * tap + m:V_TAP + 12 * tap + m + 1]
                    src = conv_in[:, m, tap:tap + T]
                    if tap == 0:
                        ins = ve.tensor_scalar(qkv[:, m, :], src, w, None, ALU.mult)
                    else:
                        ins = ve.scalar_tensor_tensor(qkv[:, m, :], src, w, qkv[:, m, :], ALU.mult, ALU.add)
                if tap == TAPS - 1:
                    ins.then_inc(conv_done.handle, 1)

            def l2(c):
                ve.wait_ge(*rstds.at(c, 4))
                ve.scalar_tensor_tensor(qkv[:, 0:4, :], qkv[:, 0:4, :], HD ** -0.5, sq[:, 0:4, :], ALU.mult, ALU.mult)
                ve.wait_ge(*rstds.at(c, 5))
                ve.tensor_tensor(qkv[:, 4:8, :], qkv[:, 4:8, :], sq[:, 4:8, :], ALU.mult).then_inc(l2_made.handle, 1)
                ve.drain()

            def spread(c):
                banks, free = wait_spot(c, ("spread", 0), 0)
                ve.tensor_tensor(k_beta, qkv[:, 4:8, :], banks.rearrange("p b (a t) -> p (b a) t", a=2), ALU.mult
                                 ).then_inc(free, 1)
                banks, free = wait_spot(c, ("spread", 0), 1)
                wide = banks.rearrange("p b (a t) -> p (b a) t", a=2)
                ve.tensor_copy(glast[:, :, :], wide[:, :, CHUNK - 1::CHUNK])
                ve.tensor_tensor(q_dec, qkv[:, 0:4, :], wide, ALU.mult).then_inc(free, 1)
                ve.drain()
                ve.memset(vnew[:, :], 0.0)
                ve.memset(state[:, :, :], 0.0)
                ve.drain().then_inc(k_beta_made.handle, 1)

            def natural(c):
                def per_head(col):
                    return cols[:, :, col:col + H].unsqueeze(3).to_broadcast([P, TT, H, HD])

                def heads(t):
                    return t.rearrange("p t (h d) -> p t h d", h=H)
                banks, free = wait_spot(c, ("natural", 0), 0)
                ve.tensor_tensor(heads(kbe), heads(banks), per_head(40), ALU.mult)
                ve.tensor_tensor(heads(kdn), heads(banks), per_head(24), ALU.mult).then_inc(free, 1)
                banks, free = wait_spot(c, ("natural", 0), 1)
                ve.tensor_tensor(heads(vb), heads(banks), per_head(32), ALU.mult).then_inc(free, 1)

            def with_decay(c, name, dst):
                for t in range(TT):
                    banks, free = wait_spot(c, (name, 0), t)
                    n, _, s = spot_of(c, ("decay", 0), t)
                    ve.wait_ge(*spot_taken[s].at(c, n // 3 + 1))
                    ve.tensor_tensor(dst[:, t].rearrange("p e q c -> p e (q c)"), banks,
                                     x_m[:, t].rearrange("p e q c -> p e (q c)"), ALU.mult).then_inc(free, 1)

            def all_mats(m):
                return m.rearrange("p t e q c -> p (t e q) c")

            def level_mask(s):
                mask = cst[:, C_LEVEL + s * P:C_LEVEL + s * P + P].unsqueeze(1).to_broadcast([P, 16, P])
                return ve.tensor_tensor(all_mats(b_m), all_mats(m_t), mask, ALU.mult)

            def level1(c):
                ve.drain()
                level_mask(0)
                ve.drain()
                ve.tensor_tensor(all_mats(inv_t), ident.unsqueeze(1).to_broadcast([P, 16, P]), all_mats(b_m),
                                 ALU.subtract).then_inc(level_made.handle, 1)
                ve.drain()
                level_mask(1).then_inc(level_made.handle, 1)

            def level(c, s):
                def less(i, t, dst):
                    banks, free = wait_spot(c, ("level", s), i)
                    flat = dst[:, t].rearrange("p e q c -> p e (q c)")
                    ve.tensor_tensor(flat, flat, banks, ALU.subtract).then_inc(free, 1)
                if s < 5:
                    wait_spot(c, ("level", s), 1)
                    level_mask(s + 1).then_inc(level_made.handle, 1)
                    for t in range(TT):
                        less(2 + 2 * t, t, inv)
                        less(3 + 2 * t, t, inv_t)
                else:
                    for t in range(TT):
                        less(2 + t, t, inv_t)

            def wu(c):
                banks, free = wait_spot(c, ("wu", 0), 1)
                ve.tensor_copy(kbe, banks).then_inc(free, 1)
                ve.drain().then_inc(state_made.handle, 1)

            def scan_v(c, k):
                banks, free = wait_spot(c, ("scan_v", k))
                half = slice(HD * (k % 2), HD * (k % 2) + HD)
                ve.tensor_tensor(vnew[half, :], kbe[half, k // 2, :], banks[half, 0, :], ALU.subtract).then_inc(free, 1)

            def scan_s(c, k):
                banks, free = wait_spot(c, ("scan_s", k))
                ve.tensor_copy(o_dn[:, :, k * CHUNK:(k + 1) * CHUNK],
                               banks[:, 0, 0:T].rearrange("p (a i) -> p a i", a=PAIRS))
                step = sg[:, :, :].rearrange("p a (b c) -> p (a b) c", c=P)
                ve.tensor_tensor(step, banks[:, 1, :].rearrange("p (q c) -> p q c", q=PAIRS),
                                 blk.unsqueeze(1).to_broadcast([P, PAIRS, P]), ALU.mult).then_inc(free, 1)
                ve.tensor_tensor(state[:, :, :], state[:, :, :], glast[:, :, k:k + 1].to_broadcast([P, PAIRS, P]),
                                 ALU.mult)
                ve.drain()
                ve.tensor_tensor(state[:, :, :], state[:, :, :], step, ALU.add).then_inc(state_made.handle, 1)
                ve.drain()

            def onorm(c):
                ve.wait_ge(*rstds.at(c, 6))
                ve.scalar_tensor_tensor(o_dn, o_dn, vec[:, V_ON:V_ON + 1], sq[:, 4:8, :], ALU.mult, ALU.mult)
                ve.drain()
                ve.wait_ge(*z_made.at(c, 1))
                ve.tensor_tensor(o_dn, o_dn, zs, ALU.mult).then_inc(delta_done.handle, 1)

            def branch(c, i):
                u, g = unit(c, "br", i // 2, i % 2)[0], unit(c, "gate", i // 2, i % 2)[0]
                src, free = wait_unit(c, u)
                ve.wait_ge(*taken(c, g))
                dst = merged[:, 2 * (i % 4):2 * (i % 4) + 2, :]
                if i < 4:
                    ve.tensor_tensor(dst, two(src), gt[:, i % 2], ALU.mult).then_inc(free, 1)
                else:
                    tmp = sg[:, :, :]
                    ve.tensor_tensor(tmp, two(src), gt[:, i % 2], ALU.mult).then_inc(free, 1)
                    ve.drain()
                    ve.tensor_tensor(dst, dst, tmp, ALU.add)
                    ve.drain()
                if i == 11:
                    ve.drain().then_inc(merged_made.handle, 1)

            def mix_out(c, i):
                src, free = wait_unit(c, unit(c, "out", i // 2, i % 2)[0])
                ve.tensor_tensor(xT[:, 2 * i:2 * i + 2, :], xT[:, 2 * i:2 * i + 2, :], two(src), ALU.add
                                 ).then_inc(free, 1)

            def mixer(c):
                for step, i in MIXER:
                    ve.drain()
                    if step == "norm":
                        ve.memset(conv_in[:, :, 0:TAPS - 1], 0.0)
                        norm(c, 1, act, vec[:, V_MIX:V_MIX + KD], 2, 2)
                    elif step == "lin":
                        plain(c, *i)
                    elif step == "kk":
                        with_decay(c, "kk", m_t)
                    elif step == "qk":
                        with_decay(c, "qk", qk_t)
                    elif step in ("latnorm", "rows", "rowcols", "krot", "qrot", "l2", "spread", "natural", "level1", "wu", "onorm"):
                        {"latnorm": latnorm, "rows": rows, "rowcols": rowcols, "krot": krot, "qrot": qrot, "l2": l2,
                         "spread": spread, "natural": natural, "level1": level1, "wu": wu, "onorm": onorm}[step](c)
                    elif step in ("conv", "scores", "soft", "values", "level", "scan_v", "scan_s", "br", "out"):
                        {"conv": conv, "scores": scores, "soft": normalise, "values": values, "level": level, "scan_v": scan_v, "scan_s": scan_s,
                         "br": branch, "out": mix_out}[step](c, i)

            def adaln():
                ve.wait_ge(bias_here, 16)
                with ve.Fori(0, DEPTH * 2) as it:
                    c = Place("ada")
                    for s in range(6):
                        ve.wait_ge(*spot_ready.at(c, it * 6 + (s + 1)))
                        _, banks, n = spot_of(c, ("ada", s))
                        ve.tensor_tensor(mod[:, bass.ds(it * 24 + 4 * s, 4), :],
                                         banks[:, 0, 0:8].rearrange("p (m j) -> p m j", m=4),
                                         bias_a[:, bass.ds(it * 24 + 4 * s, 4)].unsqueeze(2).to_broadcast([P, 4, 2]),
                                         ALU.add).then_inc(spot_taken[n].handle, 1)

            def norm_two(c, i):
                ve.wait_ge(*squares.at(c, 1 if i == 0 else 3))
                ve.tensor_reduce(part[:, :], sq[:, :, :].rearrange("p k t -> p t k"), AX_X, ALU.add
                                 ).then_inc(sums.handle, 1)
                if i == 0:
                    ve.wait_ge(*vec_b_here.at(c, 16))
                    if c.sec == "two":
                        ve.tensor_copy(cur[:, :], mod[:, bass.ds(c.turn * 48, 48), 0])
                    else:
                        l = 0 if c.sec == "ctx" else 1
                        ve.tensor_copy(cur[:, :], mod[:, 48 * l:48 * l + 48, 1])
                    ve.drain()
                    for at, w in ((8, W_N1), (32, W_N2)):
                        ve.scalar_tensor_tensor(cur[:, at:at + 8], cur[:, at:at + 8], 1.0, vec_b[:, w:w + 8],
                                                ALU.add, ALU.mult)
                    ve.drain()
                ve.wait_ge(*rstds.at(c, 1 if i == 0 else 5))
                for kt in range(KD):
                    ve.scalar_tensor_tensor(act[:, kt, :], xT[:, kt, :], cur[:, 24 * i + 8 + kt:24 * i + 9 + kt],
                                            rstd[:, :], ALU.mult, ALU.mult)
                ve.drain()
                for kt in range(KD):
                    ve.tensor_scalar(act[:, kt, :], act[:, kt, :], cur[:, 24 * i + kt:24 * i + 1 + kt], None, ALU.add
                                     ).then_inc(normed.handle, 1)

            def rest_two(c, step):
                if step == "knorm":
                    if c.sec != "kv":
                        for t in range(TT):
                            ve.wait_ge(*taken(c, unit(c, "fg", 0, t)[0]))
                        ve.tensor_tensor(hT[:, 0:2, :], g_nat, g_nat, ALU.mult)
                        ve.drain()
                        ve.tensor_reduce(cols[:, 0, 0:8].rearrange("p (t h) -> p t h", t=TT),
                                         hT[:, 0:2, :].rearrange("p t (h d) -> p t h d", h=4), AX_X, ALU.add
                                         ).then_inc(g_sums.handle, 1)
                        ve.wait_ge(*rstds.at(c, 2))
                        ve.scalar_tensor_tensor(qk_m[:, 0:4, :], qk_m[:, 0:4, :], vec_b[:, W_QG:W_QG + 1],
                                                sq[:, 0:4, :], ALU.mult, ALU.mult)
                    ve.wait_ge(*rstds.at(c, 2 if c.sec == "kv" else 3))
                    ve.scalar_tensor_tensor(qk_m[:, 4, :], qk_m[:, 4, :], vec_b[:, W_KG:W_KG + 1], sq[:, 4, :],
                                            ALU.mult, ALU.mult)
                    ve.drain().then_inc(qk_scaled.handle, 1)
                    if c.sec != "kv":
                        ve.wait_ge(*rstds.at(c, 4))
                        heads = g_nat.rearrange("p t (h d) -> p t h d", h=4)
                        ve.tensor_tensor(heads, heads, cols[:, 0, 0:8].rearrange("p (t h) -> p t h", t=TT
                                         ).unsqueeze(3).to_broadcast([P, TT, 4, HD]), ALU.mult).then_inc(g_made.handle, 1)
                elif step == "rot":
                    def table(at, n):
                        return tbl[:, at:at + T].unsqueeze(1).to_broadcast([P, n, T])
                    banks, free = wait_spot(c, (step, 0), 0)
                    ve.tensor_tensor(hT[:, 0:4, :], banks.rearrange("p b (a t) -> p (b a) t", a=2), table(B_SIN, 4),
                                     ALU.mult).then_inc(free, 1)
                    banks, free = wait_spot(c, (step, 0), 1)
                    ve.tensor_tensor(hT[:, 4, :], banks[:, 0, 0:T], tbl[:, B_SIN:B_SIN + T], ALU.mult).then_inc(free, 1)
                    ve.tensor_tensor(qk_m[:, 0:5, :], qk_m[:, 0:5, :], table(B_COS, 5), ALU.mult)
                    ve.drain()
                    ve.tensor_tensor(qk_m[:, 0:5, :], qk_m[:, 0:5, :], hT[:, 0:5, :], ALU.add
                                     ).then_inc(qk_turned.handle, 1)
                elif step == "fourier":
                    banks, free = wait_spot(c, (step, 0), 1)
                    ve.tensor_copy(o_att[:, 4:6, :], two_tiles(banks[:, 0, :])).then_inc(free, 1)
                elif step == "spatial":
                    banks, free = wait_spot(c, (step, 0))
                    for m in range(2):
                        ins = ve.scalar_tensor_tensor(
                            o_att[:, 6 + m, :].rearrange("p (t c) -> p t c", t=TT),
                            banks[:, 0, m * T:m * T + T].rearrange("p (t c) -> p t c", t=TT),
                            vec_b[:, W_VG + m:W_VG + m + 1],
                            vec_b[:, W_BS + m * P:W_BS + m * P + P].unsqueeze(1).to_broadcast([P, TT, P]),
                            ALU.mult, ALU.add)
                    ins.then_inc(free, 1)
                    ve.drain()
                    ve.tensor_tensor(o_att[:, 6:8, :], o_att[:, 6:8, :], u_two, ALU.mult).then_inc(mix_made.handle, 1)

            def two_tiles(tile):
                return tile.rearrange("p (a t) -> p a t", a=2)

            def two_pass(c, order):
                n = 2 * T if c.sec == "two" else T
                for step, i in order:
                    ve.drain()
                    if step == "norm":
                        norm_two(c, i)
                    elif step == "lin" and i[0] == "q":
                        src, free = wait_unit(c, unit(c, "q", 0, i[1])[0])
                        ve.tensor_copy(qk_m[:, 2 * i[1]:2 * i[1] + 2, :], two_tiles(src)).then_inc(free, 1)
                    elif step == "scores":
                        banks, _ = wait_spot(c, ("scores", i))
                        ve.tensor_reduce(mx[:, i % 2, 0, :], banks[:, :, 0:n], AX_X, ALU.max, negate=True
                                         ).then_inc(max_made.handle, 1)
                    elif step == "soft":
                        k, _, s = spot_of(c, ("scores", i))
                        ve.wait_ge(*spot_taken[s].at(c, k // 3 + 1))
                        ve.reciprocal(rs[:, i % 2, 0, :], rs[:, i % 2, 0, :])
                        ve.drain()
                        ve.tensor_tensor(prob2[:, i % 2, :, 0:n], prob2[:, i % 2, :, 0:n],
                                         rs[:, i % 2, 0, :].unsqueeze(2).to_broadcast([P, 2, n]), ALU.mult
                                         ).then_inc(prob_made.handle, 1)
                    elif step == "values":
                        banks, free = wait_spot(c, ("values", i))
                        ve.tensor_copy(o_att[:, i // 2, i % 2 * P:i % 2 * P + P], banks[:, 0, 0:P]).then_inc(free, 1)
                    elif step == "out":
                        src, free = wait_unit(c, unit(c, "out", i // 2, i % 2)[0])
                        for m in range(2):
                            ins = ve.scalar_tensor_tensor(xT[:, 2 * i + m, :], src[:, m * T:m * T + T],
                                                          cur[:, 16 + 2 * i + m:17 + 2 * i + m], xT[:, 2 * i + m, :],
                                                          ALU.mult, ALU.add)
                        ins.then_inc(free, 1)
                    else:
                        rest_two(c, step)
                if c.sec == "kv":
                    return
                u0 = GROUP[c.sec]["m1", 0][1]

                def up(it, s):
                    for part_ in range(2):
                        k = 2 * s + part_
                        ve.wait_ge(*lin_ready.at(c, it * 6 + (u0 + k + 1)))
                        src, free = lin[:, (u0 + k) % 2, :], lin_taken[(u0 + k) % 2].handle
                        ve.wait_ge(*gate_made.at(c, it * 6 + (k + 1)))
                        dst = hT[:, bass.ds(it * 12 + 2 * k, 2), :] if s < 6 else hT[:, 2 * k:2 * k + 2, :]
                        ve.tensor_tensor(dst, sg[:, :, :], two_tiles(src), ALU.mult).then_inc(free, 1)

                with ve.Fori(0, 2) as it:
                    for s in range(3):
                        up(it, s)
                for s in range(6, 8):
                    up(0, s)
                u1 = GROUP[c.sec]["m2", 0][1]
                for m in range(KD):
                    src, free = wait_unit(c, u1 + m)
                    ve.scalar_tensor_tensor(xT[:, m, :], src[:, 0:T], cur[:, 40 + m:41 + m], xT[:, m, :],
                                            ALU.mult, ALU.add).then_inc(free, 1)

            ve.wait_ge(consts_here, 16)
            ve.memset(ones[:, :], 1.0)
            ve.tensor_copy(identb[:, :], ident)
            ve.tensor_copy(causal[:, :], cst[:, C_CAUSAL:C_CAUSAL + P])
            ve.tensor_copy(delta_mask[:, :], cst[:, C_DELTA:C_DELTA + P])
            ve.drain().then_inc(consts_made, 1)

            ve.wait_ge(pos_here, 16)
            ve.tensor_copy(sq[:, 3, :], sq[:, 2, :].bitcast(I32))
            ve.drain()
            ve.tensor_scalar(sq[:, 3, :], sq[:, 3, :], cst[:, C_FREQ:C_FREQ + 1], None, ALU.mult)
            ve.drain()
            ve.tensor_scalar(sq[:, 4, :], sq[:, 3, :], 1 / TURN, None, ALU.mult)
            ve.drain()
            ve.tensor_scalar(sq[:, 4, :], sq[:, 4, :], ROUND, None, ALU.add)
            ve.drain()
            ve.tensor_scalar(sq[:, 4, :], sq[:, 4, :], ROUND, None, ALU.subtract)
            ve.drain()
            for piece in TURN_PARTS:
                ve.scalar_tensor_tensor(sq[:, 3, :], sq[:, 4, :], -piece, sq[:, 3, :], ALU.mult, ALU.add)
                ve.drain()
            ve.tensor_scalar(sq[:, 0, :], sq[:, 3, :], HALF_TURN, -HALF_TURN, ALU.min, ALU.max)
            ve.drain()
            ve.scalar_tensor_tensor(sq[:, 1, :], sq[:, 0, :], -1.0, sq[:, 0, :], ALU.mult, ALU.max)
            ve.drain()
            ve.tensor_scalar(sq[:, 1, :], sq[:, 1, :], -1.0, QUARTER_TURN, ALU.mult, ALU.add).then_inc(turn_here, 1)
            ve.wait_ge(turn_done, 1)
            for k in range(2):
                ins = ve.tensor_scalar(cossin[:, k, :], cossin[:, k, :], cst[:, C_LIVE:C_LIVE + 1], None, ALU.mult)
            ve.drain()
            adaln()
            ve.wait_ge(ctx_here, 16)
            two_pass(Place("ctx"), CTX)
            two_pass(Place("kv"), KV)
            ve.wait_ge(*kept.at(Place("one"), 0))
            ve.wait_ge(x_here, 16)
            with ve.Fori(0, DEPTH) as l:
                c = Place("one", l)
                ffn(c, 0)
                mixer(c)
                ffn(c, 1)
            norm(Place("fin"), 0, xT, cst[:, C_FINAL:C_FINAL + KD], 1, 1)
            ve.wait_ge(tables_again, 16)
            with ve.Fori(0, DEPTH) as l:
                two_pass(Place("two", l), TWO)


def tiles(w, width):
    *lead, k, n = w.shape
    w = w.reshape(*lead, k // P, P, n // width, width)
    order = list(range(len(lead))) + [len(lead) + 2, len(lead) + 1, len(lead), len(lead) + 3]
    return w.transpose(order).reshape(*lead, n // width, P, k // P * width)


def feature_major(v):
    return np.moveaxis(v.reshape(*v.shape[:-1], -1, P), -1, -2)


def pack_one(i, l):
    def ffn(gu, down):
        both = np.stack([gu[:, :FF].reshape(D, GU_GROUPS, 256), gu[:, FF:].reshape(D, GU_GROUPS, 256)], 2)
        return [tiles(both.reshape(D, 2 * FF), 512), tiles(down, P)]

    w = i["w_in"][l]
    ends = np.cumsum([512, 512, 512, 8, 256, 128, 32, 512, 512, 512, 512, 8, 8, 3072])
    fq, fk, fv, ff, cq, ckv, kr, dq, dk, dv, dz, db, da, gate = np.split(w, ends[:-1], axis=1)
    rows = np.zeros((D, P), w.dtype)
    rows[:, 0:32] = rows[:, 64:96] = kr
    rows[:, 32:40], rows[:, 40:48], rows[:, 96:104] = ff, da, db
    uq = i["mla_w_uq"][l].reshape(256, H, 96)
    rope = np.zeros((256, H, HD), w.dtype)
    rope[:, :, 0:32] = uq[:, :, HD:]
    uq = np.concatenate([uq[:, :, :HD].reshape(256, 512), rope.reshape(256, 512)], 1)
    ukv = i["mla_w_ukv"][l].reshape(P, H, 2, HD)
    parts = ffn(i["ffn1_w_gu"][l], i["ffn1_w_down"][l])
    parts += [tiles(np.concatenate([cq, ckv, rows], 1), 512)]
    parts += [tiles(x, 512) for x in (fq, fk, fv, dq, dk, dv)]
    parts += [tiles(uq, 1024), tiles(ukv[:, :, 0].reshape(P, 512), 512), tiles(ukv[:, :, 1].reshape(P, 512), 512),
              tiles(dz, 512)]
    gates = tiles(gate, 512)
    branches = np.concatenate([tiles(i[n][l], 512) for n in ("w_br_fox", "w_br_mla", "w_br_dn")])
    for g in range(6):
        parts += [gates[g], branches[g]]
    parts += [tiles(i["w_out"][l], 512)]
    return parts + ffn(i["ffn2_w_gu"][l], i["ffn2_w_down"][l])


def vectors_one(i):
    out = np.zeros((DEPTH, P, NV), np.float32)
    for at, name in ((V_FFN1, "ffn1_norm"), (V_MIX, "mix_norm"), (V_FFN2, "ffn2_norm"), (V_BGATE, "b_gate"),
                     (V_QN, "mla_q_norm"), (V_KVN, "mla_kv_norm")):
        v = feature_major(i[name])
        out[:, :, at:at + v.shape[-1]] = v
    taps = feature_major(i["dn_conv_w"])
    out[:, :, V_TAP:V_TAP + 48] = taps.transpose(0, 2, 1, 3).reshape(DEPTH, P, 48)
    out[:, 0:HD, V_ON] = out[:, HD:, V_ON] = i["dn_o_norm"]
    out[:, 32:40, V_BIAS], out[:, 40:48, V_BIAS], out[:, 40:48, V_ALOG] = i["fox_b_f"], i["dn_dt_bias"], i["dn_a_log"]
    return out


def constants():
    c = np.zeros((P, NC_), np.float32)
    p = np.arange(P)
    row, col = p[:, None], p[None, :]
    c[:, C_ID:C_ID + P] = np.eye(P)
    c[:, C_BLK:C_BLK + P] = row // HD == col // HD
    c[:, C_ROT:C_ROT + P] = 1.0 * ((row == col - 16) & (col % 32 >= 16)) - 1.0 * ((row == col + 16) & (col % 32 < 16))
    c[:, C_CAUSAL:C_CAUSAL + P] = np.where(col <= row, 0, NEG)
    c[:, C_DELTA:C_DELTA + P] = np.where((row // CHUNK == col // CHUNK) & (row <= col), 0, NEG)
    for n, s in enumerate(LEVELS):
        c[:, C_LEVEL + n * P:C_LEVEL + n * P + P] = (row // (2 * s) == col // (2 * s)) & (row // s % 2 == 0) & (col // s % 2 == 1)
    for pair in range(PAIRS):
        for e in range(2):
            at = C_PAIR + pair * P + e * HD
            c[ROWA + H + 2 * pair + e, at:at + HD] = 1
            c[ROWB + 2 * pair + e, at:at + HD] = 1
    freq = np.float32(10000.0) ** (-np.arange(16, dtype=np.float32) / np.float32(16))
    for at in (0, 16, 64, 80):
        c[at:at + 16, C_FREQ] = freq
        c[at:at + 16, C_LIVE] = 1
    c[32:40, C_SIGN], c[40:48, C_SIGN] = -1, 1
    c[ROWA:ROWA + ROWS, C_RESET:C_RESET + T] = 1
    c[ROWA + H:ROWA + ROWS, C_RESET:C_RESET + T:CHUNK] = 0
    for j in range(2):
        c[j::32, C_TWO + j] = 1
    return c


def second_tables():
    t = np.zeros((P, NB), np.float64)
    n, d = np.arange(T), np.arange(HD)
    angle = 2 * np.pi * (n[:, None] * n[None, :] % T) / T
    dft = np.concatenate([np.cos(angle), np.sin(angle)], 1) / np.sqrt(T * HD)
    t[:, B_DFT:B_DFT + TT * 512] = dft.reshape(TT, P, 512).transpose(1, 0, 2).reshape(P, TT * 512)
    angle = 2 * np.pi * (d[:, None] * d[None, :] % HD) / HD
    t[:, B_CD:B_CD + P] = np.kron(np.eye(2), np.cos(angle))
    t[:, B_SD:B_SD + P] = np.kron(np.eye(2), -np.sin(angle))
    inv = np.float32(10000.0) ** (-np.arange(0, 32, 2, dtype=np.float32) / np.float32(32))
    at = np.stack([n // 64, n % 64]).astype(np.float32)
    both = (at[:, None, :] * inv[None, :, None]).repeat(2, 0).reshape(2, 2, 16, T).reshape(HD, T)
    t[:, B_COS:B_COS + T] = np.tile(np.cos(both), (2, 1))
    t[:, B_SIN:B_SIN + T] = np.tile(np.sin(both), (2, 1))
    for k in range(2):
        for e in range(2):
            t[k * HD + d, B_DUP + k * P + e * HD + d] = 1
    return t.astype(np.float32)


def pack_two(i, l):
    q, k, v, f, u, g = np.split(i["w_in_2"][l], np.cumsum([512, P, P, 256, 256]), axis=1)
    parts = [tiles(q, 512), tiles(np.concatenate([k, u, v], 1), 512), tiles(np.concatenate([f, g], 1), 512)]
    return parts + [tiles(i["w_out_2"][l], 512), tiles(i["w_mlp1_2"][l], 512), tiles(i["w_mlp2_2"][l], P)]


def vectors_two(i):
    out = np.zeros((DEPTH, P, NW), np.float32)
    out[:, :, W_N1:W_N1 + 8], out[:, :, W_N2:W_N2 + 8] = feature_major(i["norm1_g_2"]), feature_major(i["norm2_g_2"])
    out[:, :, W_QG], out[:, :, W_KG] = np.tile(i["q_norm_g_2"], (1, 2)), np.tile(i["k_norm_g_2"], (1, 2))
    out[:, :, W_VG:W_VG + 2] = feature_major(i["gmlp_v_g_2"])
    bias = i["b_spatial_2"].reshape(DEPTH, 2, 2, 1, P).repeat(HD, 3)
    out[:, :, W_BS:W_BS + 2 * P] = bias.transpose(0, 2, 3, 1, 4).reshape(DEPTH, P, 2 * P)
    out[:, :, W_WS:] = i["w_spatial_2"].transpose(0, 3, 1, 2).reshape(DEPTH, P, 4 * P)
    return out


def tokens(x):
    return x.reshape(T, KD, P).transpose(2, 1, 0)


def laid_out(i):
    two = [pack_two(i, l) for l in range(DEPTH)]
    parts = [tiles(i["w_ada_2"][l], 512) for l in range(DEPTH)] + two[0] + [two[1][1]]
    for l in range(DEPTH):
        parts += pack_one(i, l)
    parts += two[0] + two[1]
    consts = constants()
    consts[:, C_FINAL:C_FINAL + KD] = feature_major(i["final_norm"])
    cond = np.zeros((P, KD, 32), np.float32)
    cond[:, :, 0], cond[:, :, 1] = feature_major(i["c_2"][0]), feature_major(i["c_ctx_2"])
    bada = feature_major(i["b_ada_2"]).transpose(1, 0, 2).reshape(P, DEPTH * 48)
    return {"stream": np.concatenate([p.ravel() for p in parts]), "x_in": tokens(i["x"][0]),
            "ctx_in": tokens(i["ctx_2"][0]), "cond": cond, "positions": i["positions"].astype(np.int32),
            "vec1": vectors_one(i), "vec2": vectors_two(i), "bada": bada, "consts": consts,
            "tables": second_tables()}


def kernel(**inputs):
    import concourse.bacc as bacc
    from concourse.bass_utils import run_bass_kernel_spmd

    nc = bacc.Bacc("TRN2", target_bir_lowering=False, num_devices=1)
    arrays, args = {}, []
    for name, a in laid_out({k: np.asarray(v) for k, v in inputs.items()}).items():
        arrays[name] = np.ascontiguousarray(a)
        args.append(nc.dram_tensor(name, a.shape, mybir.dt.from_np(a.dtype), kind="ExternalInput").ap())
    out = nc.dram_tensor("out", (P, KD, T), F32, kind="ExternalOutput").ap()
    build(nc, *args, out)
    got = run_bass_kernel_spmd(nc, [arrays], core_ids=[0]).results[0]["out"]
    return np.ascontiguousarray(got.transpose(2, 1, 0).reshape(1, T, D))
```

```python
from contextlib import ExitStack

import numpy as np

import concourse.bass as bass
from concourse import mybir

F32 = mybir.dt.float32
BF16 = mybir.dt.bfloat16
I32 = mybir.dt.int32
ALU = mybir.AluOpType
ACT = mybir.ActivationFunctionType
AX_X = mybir.AxisListType.X
EXP_LN = "natural_log_exp_and_others"

P = 128
T = 256
TT = T // P
D = 1024
KD = D // P
DEPTH = 2
FF = 2816
KF = FF // P
GU_GROUPS = FF // 256
FF2 = 4096
KF2 = FF2 // P
H = 8
PAIRS = H // 2
HD = 64
CHUNK = 64
CHUNKS = T // CHUNK
TAPS = 4
EPS = 1e-6
NEG = -1e30
LEVELS = (1, 2, 4, 8, 16, 32)
SLOTS = 3
FULL = 8 * 512
FOX_SCALE = HD ** -0.5
MLA_SCALE = 96 ** -0.5
TURN = 2 * np.pi
TURN_PARTS = (6.28125, 2.0 ** -22 * round((TURN - 6.28125) * 2.0 ** 22))
TURN_PARTS += (TURN - sum(TURN_PARTS),)
ROUND = 1.5 * 2.0 ** 23
HALF_TURN, QUARTER_TURN = 3.1415925, float(np.float32(np.pi / 2))

ADA = [("ada", FULL, 1)]
FFN_GROUPS = [("gu", FULL, 2)] * GU_GROUPS + ([("down", KF * P, 1)] + ADA + [("down", KF * P, 1)]) * 4 + ADA
MIX_GROUPS = ([(n, FULL, 2) for n in ("lat", "fq", "fk", "fv", "dq", "dk", "dv")]
              + [("uq", 2 * 1024, 4), ("uk", 512, 2), ("uv", 512, 2), ("dz", FULL, 2)]
              + [("gate", FULL, 2), ("br", 4 * 512, 2)] * 6 + ([("out", FULL, 2)] + ADA) * 2)
ONE_GROUPS = FFN_GROUPS + MIX_GROUPS + FFN_GROUPS
TWO_GROUPS = ([("q", FULL, 2), ("kuv", FULL, 2), ("fg", FULL, 2)] + [("out", FULL, 2)] * 2
              + [("m1", FULL, 2)] * 8 + [("m2", KF2 * P, 1)] * 8)
KV_GROUPS = [("kuv", FULL, 2)]
SECTIONS = {"load": (1, []), "one": (DEPTH, ONE_GROUPS), "cload": (1, []), "ctx": (1, TWO_GROUPS),
            "kv": (1, KV_GROUPS), "two": (DEPTH, TWO_GROUPS)}
ADA_TURN = 12


def places(groups):
    seen, unit, out = {}, 0, {}
    for n, (name, width, units) in enumerate(groups):
        i = seen.get(name, 0)
        seen[name] = i + 1
        out[name, i] = (n, unit)
        unit += units
    return out


GROUP = {s: places(g) for s, (_, g) in SECTIONS.items()}
UNITS = {s: sum(g[2] for g in gs) for s, (_, gs) in SECTIONS.items()}
MIX_BASE = len(FFN_GROUPS)
FFN2_BASE = MIX_BASE + len(MIX_GROUPS)
FFN_UNITS = sum(g[2] for g in FFN_GROUPS)
FFN2_UNIT = UNITS["one"] - FFN_UNITS


def one_order():
    def lin(name, *parts):
        return [("lin", (name, i)) for i in parts]

    def one(*names):
        return [(n[:-1].removesuffix("_"), int(n[-1])) for n in names]

    order = (one("norm1") + lin("lat", 0, 1) + one("latnorm0") + lin("fq", 0) + one("rows0") + lin("fq", 1)
             + lin("fk", 0, 1) + one("rowcols0") + lin("fv", 0) + one("scores0") + lin("fv", 1)
             + one("scores1", "soft0") + lin("dq", 0) + one("turn0", "soft1", "scores2") + lin("dq", 1)
             + one("values0", "turn1", "soft2", "scores3") + lin("dk", 0) + one("values1", "turn2", "soft3")
             + lin("dk", 1) + one("values2", "turn3", "krot0") + lin("dv", 0) + one("values3") + lin("dv", 1)
             + one("conv0") + lin("uq", 0, 1) + one("conv1") + lin("uq", 2, 3) + lin("uk", 0, 1)
             + lin("uv", 0, 1) + one("qrot0", "conv2") + lin("dz", 0) + one("scores4", "conv3") + lin("dz", 1)
             + one("scores5", "soft4", "l2_0", "turn4", "soft5", "scores6", "spread0", "values4", "turn5", "soft6",
                   "scores7", "natural0", "values5", "turn6", "soft7", "decay0", "values6", "turn7", "kk0",
                   "values7", "qk0"))
    fill = [x for b in range(2) for g in range(2) for x in
            [("gate", 4 * b + 2 * g), ("gate", 4 * b + 2 * g + 1), ("br", 4 * b + 2 * g), ("br", 4 * b + 2 * g + 1)]]
    order += fill[:1] + one("level1_0")
    fill = fill[1:]
    for s in range(1, 6):
        order += [("level", s)] + fill[:1 + (s == 5)]
        fill = fill[1 + (s == 5):]
    order.append(("wu", 0))
    for c in range(CHUNKS):
        order += [("scan_v", c)] + fill[:1] + [("scan_s", c)] + fill[1:2]
        fill = fill[2:]
    order += fill + [("gate", 8), ("onorm", 0), ("gate", 9), ("br", 8), ("br", 9), ("gate", 10), ("gate", 11), ("br", 10), ("br", 11)]
    return order + [("out", i) for i in range(4)]


def ffn_order(which):
    a = 7 * which
    return [("ada", a + n) for n in range(4)] + [("sum", 2 * which), ("ada", a + 4)]


MIXER = one_order()


def two_order(rotary, whole=True):
    if not whole:
        return [("norm", 0), ("final", 0), ("lin", ("kuv", 0)), ("sum", 0), ("lin", ("kuv", 1)), ("knorm", 0), ("kdup", 0)]
    order = [("norm", 0)] + [("lin", (n, i)) for n in ("q", "kuv") for i in range(2)]
    order += [("squares", 0), ("lin", ("fg", 0)), ("lin", ("fg", 1)), ("qnorm", 0), ("knorm", 0)]
    order += [("rot", 0)] * rotary + [("fourier", 0), ("kdup", 0), ("scores", 0), ("scores", 1), ("soft", 0), ("spatial", 0)]
    for i in range(8):
        order += [("turn", i)] + [("soft", i + 1)] * (i < 7) + [("scores", i + 2)] * (i < 6) + [("values", i)]
    return order + [("out", i) for i in range(4)] + [("sum", 0), ("norm", 1)]


TWO, CTX, KV = two_order(True), two_order(False), two_order(False, False)
SPOTS_OF = {"l2": 2, "spread": 2, "natural": 2, "decay": 2, "kk": 2, "qk": 2, "level1": 2, "wu": 2,
            "rot": 2, "fourier": 2}
NO_SPOT = ("lin", "gate", "br", "out", "conv", "squares", "soft", "rows", "norm", "final")


def spots(order):
    at, out = 0, {}
    for step in order:
        out[step] = at
        at += 0 if step[0] in NO_SPOT else (6 if step[1] < 5 else 4) if step[0] == "level" else SPOTS_OF.get(step[0], 1)
    return out, at


SPOT, SPOTS = {}, {}
for _s, _order in {"load": [("sum", 0)], "cload": [("sum", 0)], "kv": KV,
                   "ctx": CTX + [("sum", 1)], "two": TWO + [("sum", 1)],
                   "one": ffn_order(0) + MIXER + [("ada", 5), ("sum", 1), ("ada", 6)] + ffn_order(1)}.items():
    SPOT[_s], SPOTS[_s] = spots(_order)

V_FFN1, V_MIX, V_FFN2, V_BGATE, V_QN, V_KVN = 0, 8, 16, 24, 48, 50
V_TAP, V_ON, V_BIAS, V_ALOG = 51, 99, 100, 101
NV = 102
W_N1, W_N2, W_QG, W_KG, W_VG, W_BS, W_WS = 0, 8, 16, 17, 18, 20, 20 + 2 * P
NW = W_WS + 4 * P
C_ID, C_BLK, C_ROT, C_CAUSAL, C_DELTA, C_LEVEL = 0, 128, 256, 384, 512, 640
C_PAIR = C_LEVEL + 6 * P
C_FREQ = C_PAIR + PAIRS * P
C_SIGN, C_TWO, C_LIVE, C_FINAL, C_RESET = C_FREQ + 1, C_FREQ + 2, C_FREQ + 4, C_FREQ + 5, C_FREQ + 13
NC_ = C_RESET + T
B_DFT, B_CD, B_SD, B_COS, B_SIN, B_DUP = 0, TT * 512, TT * 512 + P, TT * 512 + 2 * P, TT * 512 + 2 * P + T, TT * 512 + 2 * P + 2 * T
NB = B_DUP + 2 * P
ROWA, ROWB = 32, 96
ROWS = 2 * H


class Signal:

    def __init__(self, handle, counts, first=0):
        self.handle, self.counts, self.start, at = handle, counts, {}, first
        for sec, (turns, _) in SECTIONS.items():
            self.start[sec] = at
            at += turns * counts.get(sec, 0)

    def at(self, c, k):
        return self.handle, self.counts.get(c.sec, 0) * c.turn + (self.start[c.sec] + k)


class Place:

    def __init__(self, sec, turn=0):
        self.sec, self.turn = sec, turn


def build(nc, stream, x_in, ctx_in, cond, positions, vec1, vec2, bada, consts, tables, out):
    with ExitStack() as ctx:
        def sb(name, shape, dt=F32):
            return ctx.enter_context(nc.sbuf_tensor(name, shape, dt))

        def sem(name):
            return ctx.enter_context(nc.semaphore(name))

        def signal(name, first=0, **counts):
            return Signal(sem(name), counts, first)

        slot = [sb(f"weights{s}", [P, FULL]) for s in range(SLOTS)]
        xT = sb("residual", [P, KD, T])
        act = sb("normed", [P, KD, T])
        hT = sb("hidden", [P, KF2, T])
        sq = sb("squares", [P, KD, T])
        part = sb("square_sums", [P, T])
        rstd = sb("rstd", [P, T])
        sg = sb("silu_gate", [P, 2, T])
        vec = sb("vectors", [P, NV])
        cst = sb("constants", [P, NC_])
        identb = sb("identity_bf16", [P, P], BF16)
        causal = sb("causal_bf16", [P, P], BF16)
        delta_mask = sb("delta_mask_bf16", [P, P], BF16)
        ones = sb("ones", [P, P])
        cossin = sb("cos_sin", [P, 2, T])
        lat = sb("latents", [P, 4, T])
        qk_f = sb("fox_qk", [P, 8, T])
        vn_f = sb("fox_values", [P, TT, 512])
        qk_m = sb("mla_qk", [P, 8, T])
        vn_m = sb("mla_values", [P, TT, 512])
        qr = sb("mla_q_rope", [P, PAIRS, T])
        kr = sb("mla_k_rope", [P, T])
        conv_in = sb("conv_in", [P, 12, T + TAPS - 1])
        qkv = sb("delta_qkv", [P, 12, T])
        row = sb("rows", [P, 6, T])
        cols = sb("row_columns", [P, TT, 48])
        mx = sb("negated_maxima", [P, 2, 2, 2])
        rs = sb("softmax_sums", [P, 2, 2, 2])
        probs = sb("probabilities", [P, 3072])
        vnew = sb("delta_new_values", [P, 512])
        state = sb("delta_state", [P, PAIRS, P])
        glast = sb("delta_chunk_decay", [P, PAIRS, CHUNKS])
        alog = sb("exp_a_log", [P, 1])
        mod = sb("modulation", [P, DEPTH * 48, 2])
        cur = sb("modulation_of_pass", [P, 48])
        k_ctx = sb("context_keys", [P, DEPTH, 2, T])
        v_ctx = sb("context_values", [P, DEPTH, TT, P])

        prob = probs[:, 0:1536].rearrange("p (b e c) -> p b e c", b=2, e=2)
        probT = probs[:, 1536:3072].rearrange("p (b e c) -> p b e c", b=2, e=2)
        o_att = hT[:, 24:32, :]

        def mats(tiles):
            return tiles.rearrange("p a (b c) -> p (a b) c", c=P).rearrange("p (t e q) c -> p t e q c", t=TT, e=2)

        m_t, inv, k_beta = mats(hT[:, 0:8, :]), mats(hT[:, 8:16, :]), hT[:, 16:20, :]
        x_m, inv_t, b_m = mats(sq[:, :, :]), mats(qk_f[:, :, :]), mats(qk_m[:, :, :])
        qk_t = probs[:, 0:2048].rearrange("p (t e q c) -> p t e q c", t=TT, e=2, q=PAIRS)
        conv_flat = conv_in[:, :, :].rearrange("p a b -> p (a b)")
        kbe, kdn, vb = (conv_flat[:, 1024 * i:1024 * (i + 1)].rearrange("p (t c) -> p t c", t=TT) for i in range(3))
        w_t, q_dec, zs = qr[:, :, :], hT[:, 20:24, :], lat[:, :, :]
        merged, o_dn = qkv[:, 0:8, :], qkv[:, 8:12, :]
        latn = hT[:, 4:7, :]
        tbl = qkv[:, 0:8, :].rearrange("p a t -> p (a t)")
        vec_b = conv_flat[:, 0:NW]
        cond_s, ada_s = k_ctx[:, 0, 0:1, :].rearrange("p a (k j) -> p (a k) j", k=KD), qk_f[:, 2:6, :].rearrange(
            "p (b a) t -> p b (a t)", b=2)
        vec_k = row[:, 1:5, :].rearrange("p a t -> p (a t)")[:, 0:NW]
        bias_a = k_ctx[:, 0, 1, 0:DEPTH * 48]
        ctx_res = conv_flat[:, 1024:1024 + KD * T].rearrange("p (k t) -> p k t", k=KD)
        ctx_rstd = row[:, 0, :]
        angle = qkv[:, 0:5, :]
        keys, vals = vn_f, vn_m[:, 0, :].rearrange("p (k c) -> p k c", k=4)
        f_nat, g_nat, u_two, f_mid = qr[:, 0:2, :], qr[:, 2:4, :], lat[:, 0:2, :], qk_f[:, 0:4, :]
        prob2, probT2 = probs[:, 0:2048].rearrange("p (b e c) -> p b e c", b=2, e=2), probs[:, 2048:3072].rearrange(
            "p (e c) -> p e c", e=2)
        gt = vn_m[:, :, :].rearrange("p a (m t) -> p a m t", m=2)

        lin = ctx.enter_context(nc.psum_tensor("units", [P, 2, 512], F32))
        spot = ctx.enter_context(nc.psum_tensor("spots", [P, 6, 512], F32))

        ident = cst[:, C_ID:C_ID + P]
        blk = cst[:, C_BLK:C_BLK + P]
        rot = cst[:, C_ROT:C_ROT + P]

        halves = {s: UNITS[s] // 2 for s in SECTIONS}
        lin_ready = signal("unit_summed", SLOTS, **UNITS)
        lin_taken = [signal(f"unit_taken{b}", 1, **halves) for b in range(2)]
        spot_ready = signal("spot_summed", 1, **SPOTS)
        spot_taken = [signal(f"spot_taken{s}", 1, **{k: (SPOTS[k] + 2 - s) // 3 for k in SECTIONS}) for s in range(3)]
        loaded = [signal(f"weights_loaded{s}", **{k: 16 * ((len(SECTIONS[k][1]) + 2 - s) // 3) for k in SECTIONS})
                  for s in range(SLOTS)]
        squares = signal("squares_made", one=3, ctx=1, kv=1, two=1)
        rstds = signal("rstd_made", one=4, ctx=3, kv=1, two=3)
        res_squares = signal("residual_squares_made", load=1, one=20, cload=1, ctx=12, kv=1, two=12)
        res_sums = signal("residual_squares_summed", load=1, one=3, cload=1, ctx=2, kv=1, two=2)
        res_rstd = signal("residual_rstd_made", load=1, one=3, cload=1, ctx=2, kv=1, two=2)
        scaled = signal("tile_scaled", ctx=2 * KD, kv=KD, two=2 * KD)
        final_made = sem("final_norm_made")
        normed = signal("tile_normed", one=3 * KD, ctx=2 * KD, kv=KD, two=2 * KD)
        gate_made = signal("gate_activated", ctx=2 * 8, one=4 * GU_GROUPS, two=2 * 8)
        vec_here = signal("vectors_loaded", one=16)
        lat_made = signal("latents_normed", one=1)
        rows_abs = signal("rows_abs_made", one=1)
        rows_exp = signal("rows_exp_made", one=1)
        rows_cum = signal("rows_summed_up", one=1)
        rows_done = signal("rows_done", one=1)
        conv_done = signal("conv_done", one=1)
        l2_made = signal("delta_qk_normed", one=1)
        rope_q = signal("mla_q_turned", one=1)
        rope_k = signal("mla_k_turned", one=1)
        max_made = signal("maxima_made", ctx=8, one=8, two=8)
        prob_made = signal("probabilities_normed", ctx=8, one=8, two=8)
        k_beta_made = signal("k_beta_made", one=1)
        level_made = signal("level_part_made", one=6)
        state_made = signal("delta_state_made", one=1 + CHUNKS)
        z_made = signal("silu_z_made", one=1)
        delta_done = signal("delta_out_normed", one=1)
        merged_made = signal("branches_merged", one=1)
        qk_scaled = signal("qk_normed", ctx=1, kv=1, two=1)
        qk_turned = signal("qk_turned", two=1)
        g_sums = signal("gmlp_sums_made", ctx=1, two=1)
        g_made = signal("gmlp_normed", ctx=1, two=1)
        mix_made = signal("gmlp_done", ctx=1, two=1)
        kept = signal("context_kept", ctx=2, kv=2)
        given = signal("context_given", two=2)
        tables_here = sem("tables_loaded")
        vec_b_here = signal("second_vectors_loaded", ctx=16, kv=16, two=16)
        ctx_here = sem("context_loaded")
        cond_here = sem("condition_loaded")
        bias_here = sem("adaln_bias_loaded")
        cond_made = sem("condition_gate_made")
        consts_here = sem("constants_loaded")
        consts_made = sem("constants_made")
        turn_here = sem("rotary_angles_made")
        turn_done = sem("rotary_tables_made")
        x_here = sem("residual_loaded")
        pos_here = sem("positions_loaded")
        stored = sem("output_stored")

        def unit(c, name, i, part=0):
            u = GROUP[c.sec][name, i][1] + part
            return u, u % 2

        def taken(c, u):
            return lin_taken[u % 2].at(c, u // 2 + 1)

        def spot_of(c, step, i=0):
            n = SPOT[c.sec][step] + i
            return n, spot[:, 2 * (n % 3):2 * (n % 3) + 2, :], n % 3

        def residual(c):
            return (ctx_res, ctx_rstd) if c.sec in ("cload", "ctx", "kv") else (xT, rstd)

        def summed(c):
            return (xT, rstd) if c.sec == "kv" else residual(c)

        def vectors(c):
            return vec_k if c.sec == "kv" else vec_b

        def pieces(c, i):
            if c.sec in ("load", "cload", "kv"):
                return [], 0
            if c.sec == "one":
                if i == 1:
                    return [unit(c, "out", k // 2, k % 2)[0] for k in range(4)], 8
                return [unit(c, "down", 4 * i + m)[0] for m in range(KD)], (0, 0, 12)[i]
            if i == 0:
                return [unit(c, "out", k // 2, k % 2)[0] for k in range(4)], 0
            return [unit(c, "m2", m)[0] for m in range(KD)], 4

        block = ctx.enter_context(nc.Block())

        @block.sync
        def _(sp):
            sp.dma_start(xT[:, :, :], x_in).then_inc(x_here, 16)
            sp.sem_inc(lin_ready.handle, SLOTS)
            for signal_ in (*lin_taken, *spot_taken, spot_ready):
                sp.sem_inc(signal_.handle, 1)
            sp.dma_start(angle[:, 2, :].bitcast(I32), positions.to_broadcast([P, T])).then_inc(pos_here, 16)
            sp.dma_start(cst[:, :], consts).then_inc(consts_here, 16)
            sp.dma_start(cond_s, cond).then_inc(cond_here, 16)
            sp.dma_start(bias_a, bada).then_inc(bias_here, 16)
            base = 0
            for sec, (turns, groups) in SECTIONS.items():
                widths = [w for _, w, _ in groups]
                at = [base + P * sum(widths[:n]) for n in range(len(groups))]
                size = P * sum(widths)
                last = [u + g[2] for (_, u), g in zip(GROUP[sec].values(), groups)]

                def before(c, n):
                    return lin_ready.at(c, last[n - SLOTS] if n >= SLOTS else n - (SLOTS - 1))

                if sec == "two":
                    sp.wait_ge(*lin_ready.at(Place(sec), 0))

                def load(n, offset, wait):
                    sp.wait_ge(*wait)
                    sp.dma_start(slot[n % SLOTS][:, 0:widths[n]],
                                 stream[bass.ds(offset, P * widths[n])].rearrange("(p w) -> p w", p=P)
                                 ).then_inc(loaded[n % SLOTS].handle, 16)

                if turns == 1:
                    for n in range(len(groups)):
                        load(n, at[n], before(Place(sec), n))
                else:
                    with sp.Fori(0, turns) as l:
                        for n in range(len(groups)):
                            load(n, l * size + at[n], before(Place(sec, l), n))
                base += turns * size
            for b in range(2):
                sp.wait_ge(*lin_taken[b].at(Place("two", DEPTH), 0))
            sp.dma_start(out, xT[:, :, :]).then_inc(stored, 16)
            sp.wait_ge(stored, 16)

        @block.gpsimd
        def _(pool):
            def keep(c, l):
                n, _, s = spot_of(c, ("kdup", 0))
                pool.wait_ge(*spot_taken[s].at(c, n // 3 + 1))
                pool.tensor_copy(k_ctx[:, l], keys[:, :, T:]).then_inc(kept.handle, 1)
                pool.wait_ge(*taken(c, unit(c, "kuv", 0, 1)[0]))
                pool.tensor_copy(v_ctx[:, l], vals[:, TT:, :]).then_inc(kept.handle, 1)

            def give(l):
                pool.tensor_copy(keys[:, :, 0:T], k_ctx[:, l].rearrange("p a k t -> p (a k) t")).then_inc(given.handle, 1)
                pool.tensor_copy(vals[:, 0:TT, :], v_ctx[:, l].rearrange("p a k t -> p (a k) t")).then_inc(given.handle, 1)

            pool.dma_start(vec[:, :], vec1[0]).then_inc(vec_here.handle, 16)
            with pool.Fori(0, DEPTH - 1) as l:
                pool.wait_ge(*normed.at(Place("one", l), 3 * KD))
                pool.dma_start(vec[:, :], vec1[bass.ds(l + 1, 1)].rearrange("a p v -> (a p) v")
                               ).then_inc(vec_here.handle, 16)
            pool.wait_ge(*normed.at(Place("one", DEPTH - 1), 3 * KD))
            pool.dma_start(ctx_res, ctx_in).then_inc(ctx_here, 16)
            pool.dma_start(vec_b, vec2[0]).then_inc(vec_b_here.handle, 16)
            pool.dma_start(tbl[:, 0:NB], tables).then_inc(tables_here, 16)
            pool.wait_ge(*vec_b_here.at(Place("ctx"), 16))
            pool.dma_start(vec_k, vec2[1]).then_inc(vec_b_here.handle, 16)
            keep(Place("ctx"), 0)
            keep(Place("kv"), 1)
            give(slice(0, 1))
            with pool.Fori(0, DEPTH - 1) as l:
                c = Place("two", l)
                pool.wait_ge(*mix_made.at(c, 1))
                pool.dma_start(vec_b, vec2[bass.ds(l + 1, 1)].rearrange("a p v -> (a p) v")).then_inc(vec_b_here.handle, 16)
                n, _, s = spot_of(c, ("values", 7))
                pool.wait_ge(*spot_taken[s].at(c, n // 3 + 1))
                give(bass.ds(l + 1, 1))

        @block.tensor
        def _(pe):
            def group(c, name, i=0, turns=0):
                n = GROUP[c.sec][name, i][0]
                pe.wait_ge(*loaded[n % SLOTS].at(c, (turns + (n // SLOTS + 1)) * 16))
                return slot[n % SLOTS]

            def free_unit(c, u, before=0):
                pe.wait_ge(*lin_taken[u % 2].at(c, before + u // 2))
                return lin[:, u % 2, :]

            def free_spot(c, step, i=0, before=0):
                n, banks, s = spot_of(c, step, i)
                pe.wait_ge(*spot_taken[s].at(c, before + n // 3))
                return banks

            def product(dst, w, k, width, col, rhs, each=None):
                for kt in range(k):
                    if each:
                        pe.wait_ge(*normed.at(each[0], each[1] + kt + 1))
                    mm = pe.matmul(dst, w[:, kt * width + col:kt * width + col + P], rhs[:, kt, :],
                                   start=(kt == 0), stop=(kt == k - 1))
                return mm

            def square_sums(c, i):
                banks = free_spot(c, ("sum", i))
                units, n = pieces(c, i)
                pe.wait_ge(*res_sums.at(c, i + 1))
                mm = pe.matmul(banks[:, 0, 0:T], ones[:, :], part[:, :], start=True, stop=not units)
                if units:
                    pe.wait_ge(*res_squares.at(c, n + len(units)))
                    for kt in range(KD - KD // len(units), KD):
                        mm = pe.matmul(banks[:, 0, 0:T], ones[:, :], sq[:, kt, :], start=False, stop=(kt == KD - 1))
                mm.then_inc(spot_ready.handle, 1)

            def ada_sums(c, i):
                w = group(c, "ada", i)
                dst = free_unit(c, unit(c, "ada", i)[0])
                for kt in range(KD):
                    q = kt % 4
                    mm = pe.matmul(dst[32 * q:32 * q + 32, :], cond_s[:, kt, :], w[:, kt * 512:kt * 512 + 512],
                                   start=(kt < 4), stop=(kt >= 4))
                mm.then_inc(lin_ready.handle, 1)

            def ada_turn(c, i):
                pe.wait_ge(*taken(c, unit(c, "ada", i)[0]))
                banks = free_spot(c, ("ada", i))
                for m in range(4):
                    mm = pe.matmul(banks[:, 0, 2 * m:2 * m + 2], ada_s[:, i % 2, m * P:m * P + P],
                                   cst[:, C_TWO:C_TWO + 2], start=True, stop=True)
                mm.then_inc(spot_ready.handle, 1)

            def ffn(c, which):
                gbase, ubase = (0, 0) if which == 0 else (FFN2_BASE, FFN2_UNIT)

                def gu(it, s):
                    n, u = gbase + s, ubase + 2 * s
                    pe.wait_ge(*loaded[n % SLOTS].at(c, it * 16 + (n // SLOTS + 1) * 16))
                    w = slot[n % SLOTS]
                    for f in range(2):
                        dst = free_unit(c, u + f, it * 3)
                        for g in range(2):
                            mm = product(dst[:, g * T:g * T + T], w, KD, 512, g * 256 + f * P, act,
                                         (c, 2 * KD * which) if (s, f, g) == (0, 0, 0) else None)
                        mm.then_inc(lin_ready.handle, 1)

                with pe.Fori(0, GU_GROUPS // 3) as it:
                    for s in range(3):
                        gu(it, s)
                for s in range(GU_GROUPS // 3 * 3, GU_GROUPS):
                    gu(0, s)
                last = ubase + 2 * GU_GROUPS
                pe.wait_ge(*taken(c, last - 1))
                pe.wait_ge(*taken(c, last - 2))
                for m in range(KD):
                    w = group(c, "down", 8 * which + m)
                    dst = free_unit(c, unit(c, "down", 8 * which + m)[0])
                    product(dst[:, 0:T], w, KF, P, 0, hT).then_inc(lin_ready.handle, 1)
                    if m % 2 == 0:
                        ada_sums(c, 7 * which + m // 2)
                    else:
                        ada_turn(c, 7 * which + m // 2)
                ada_sums(c, 7 * which + 4)
                square_sums(c, 2 * which)
                ada_turn(c, 7 * which + 4)

            def plain(c, name, i, part):
                u, _ = unit(c, name, i, part)
                w = group(c, name, i)
                dst = free_unit(c, u)
                if name == "fv":
                    for kt in range(KD):
                        mm = pe.matmul(dst, act[:, kt, part * P:part * P + P], w[:, kt * 512:kt * 512 + 512],
                                       start=(kt == 0), stop=(kt == KD - 1))
                elif name == "uv":
                    mm = pe.matmul(dst, latn[:, 2, part * P:part * P + P], w[:, 0:512], start=True, stop=True)
                else:
                    k, width, rhs = {"uq": (2, 1024, latn), "uk": (1, 512, latn[:, 2:3, :])}.get(name, (KD, 512, act))
                    if name == "uq" and part == 0:
                        pe.wait_ge(*lat_made.at(c, 1))
                    for m in range(2):
                        mm = product(dst[:, m * T:m * T + T], w, k, width, (2 * part + m) * P, rhs,
                                     (c, KD) if (name, part, m) == ("lat", 0, 0) else None)
                mm.then_inc(lin_ready.handle, 1)

            def latnorm(c):
                banks = free_spot(c, ("latnorm", 0))
                pe.wait_ge(*squares.at(c, 1))
                pe.matmul(banks[:, 0, 0:T], ones[:, :], sq[:, 0, :], start=True, stop=False)
                pe.matmul(banks[:, 0, 0:T], ones[:, :], sq[:, 1, :], start=False, stop=True)
                pe.matmul(banks[:, 0, T:2 * T], ones[:, :], sq[:, 2, :], start=True, stop=True
                          ).then_inc(spot_ready.handle, 1)

            def rows(c):
                banks = free_spot(c, ("rowcols", 0))
                pe.wait_ge(*rows_done.at(c, 1))
                for t in range(TT):
                    tok = slice(t * P, t * P + P)
                    pe.matmul(banks[:, 0, t * 48:t * 48 + 16], row[ROWA:ROWA + ROWS, 4, tok],
                              cst[ROWA:ROWA + ROWS, ROWA:ROWA + ROWS], start=True, stop=True)
                    pe.matmul(banks[:, 0, t * 48 + 16:t * 48 + 32], row[ROWA:ROWA + ROWS, 5, tok],
                              cst[ROWA:ROWA + ROWS, ROWA:ROWA + ROWS], start=True, stop=True)
                for t in range(TT):
                    mm = pe.matmul(banks[:, 1, t * 8:t * 8 + 8], row[ROWB:ROWB + H, 1, t * P:t * P + P],
                                   cst[ROWB:ROWB + H, ROWB:ROWB + H], start=True, stop=True)
                mm.then_inc(spot_ready.handle, 1)

            def head_row(head):
                return cst[ROWA:ROWA + ROWS, ROWA + head:ROWA + head + 1]

            def scores(c, i):
                fox, p = i < PAIRS, i % PAIRS
                banks = free_spot(c, ("scores", i))
                if i == 0:
                    u = unit(c, "fk", 0)[0]
                    pe.wait_ge(*taken(c, u))
                    pe.wait_ge(*taken(c, u + 1))
                if i == PAIRS:
                    u = unit(c, "uk", 0)[0]
                    pe.wait_ge(*taken(c, u))
                    pe.wait_ge(*taken(c, u + 1))
                    pe.wait_ge(*rope_q.at(c, 1))
                    pe.wait_ge(*rope_k.at(c, 1))
                qk = qk_f if fox else qk_m
                for e in range(2):
                    rows_ = slice(HD * e, HD * e + HD)
                    for t, (col, keys) in enumerate(((0, P), (P, T))):
                        dst = banks[:, e, col:col + keys]
                        tok = slice(t * P, t * P + P)
                        pe.matmul(dst, qk[rows_, p, tok], qk[rows_, 4 + p, 0:keys], start=True, stop=False)
                        pe.matmul(dst[:, keys - P:keys], identb[:, :], causal[:, :], start=False, stop=False,
                                  skip_group_check=True)
                        if fox:
                            mm = pe.matmul(dst, head_row(2 * p + e).to_broadcast([ROWS, P]),
                                           row[ROWA:ROWA + ROWS, 1, 0:keys], start=False, stop=True)
                        else:
                            mm = pe.matmul(dst, qr[HD * e:HD * e + 32, p, tok], kr[HD * e:HD * e + 32, 0:keys],
                                           start=False, stop=True)
                mm.then_inc(spot_ready.handle, 1)

            def turn(c, i):
                banks = free_spot(c, ("turn", i))
                pe.wait_ge(*prob_made.at(c, i + 1))
                for e in range(2):
                    for b in range(3):
                        mm = pe.matmul(banks[:, e, b * P:b * P + P], prob[:, i % 2, e, b * P:b * P + P], ident,
                                       start=True, stop=True, is_transpose=True)
                mm.then_inc(spot_ready.handle, 1)

            def values(c, i):
                p, vn = i % PAIRS, vn_f if i < PAIRS else vn_m
                if i % PAIRS == 0:
                    u = unit(c, "fv" if i == 0 else "uv", 0)[0]
                    pe.wait_ge(*taken(c, u))
                    pe.wait_ge(*taken(c, u + 1))
                n, _, s = spot_of(c, ("turn", i))
                pe.wait_ge(*spot_taken[s].at(c, n // 3 + 1))
                banks = free_spot(c, ("values", i))
                for e in range(2):
                    col = (2 * p + e) * HD
                    dst = banks[HD * e:HD * e + HD, 0, :]
                    pe.matmul(dst[:, 0:P], vn[:, 0, col:col + HD], probT[:, i % 2, e, 0:P], start=True, stop=True)
                    pe.matmul(dst[:, P:T], vn[:, 0, col:col + HD], probT[:, i % 2, e, P:T], start=True, stop=False)
                    mm = pe.matmul(dst[:, P:T], vn[:, 1, col:col + HD], probT[:, i % 2, e, T:T + P],
                                   start=False, stop=True)
                mm.then_inc(spot_ready.handle, 1)

            def krot(c):
                banks = free_spot(c, ("krot", 0))
                pe.matmul(banks[:, 0, 0:T], rot, lat[:, 3, :], start=True, stop=True).then_inc(spot_ready.handle, 1)

            def qrot(c):
                u = unit(c, "uq", 0)[0]
                pe.wait_ge(*taken(c, u + 2))
                pe.wait_ge(*taken(c, u + 3))
                banks = free_spot(c, ("qrot", 0))
                for b in range(2):
                    mm = pe.matmul(banks[:, b, :], rot, qr[:, 2 * b:2 * b + 2, :], start=True, stop=True)
                mm.then_inc(spot_ready.handle, 1)

            def l2(c):
                pe.wait_ge(*squares.at(c, 2))
                for j in range(2):
                    banks = free_spot(c, ("l2", 0), j)
                    for b in range(2):
                        mm = pe.matmul(banks[:, b, :], blk, sq[:, 4 * j + 2 * b:4 * j + 2 * b + 2, :],
                                       start=True, stop=True)
                    mm.then_inc(spot_ready.handle, 1)

            def spread(c):
                for j, (r, n, k) in enumerate(((ROWB, H, 1), (ROWA, ROWS, 4))):
                    banks = free_spot(c, ("spread", 0), j)
                    for p in range(PAIRS):
                        mm = pe.matmul(banks[:, p // 2, p % 2 * T:p % 2 * T + T],
                                       cst[r:r + n, C_PAIR + p * P:C_PAIR + p * P + P], row[r:r + n, k, :],
                                       start=True, stop=True)
                    mm.then_inc(spot_ready.handle, 1)

            def natural(c):
                pe.wait_ge(*l2_made.at(c, 1))
                for j in range(2):
                    banks = free_spot(c, ("natural", 0), j)
                    for t in range(TT):
                        for p in range(PAIRS):
                            mm = pe.matmul(banks[:, t, p * P:p * P + P],
                                           qkv[:, 4 + 4 * j + p, t * P:t * P + P], ident,
                                           start=True, stop=True, is_transpose=True)
                    mm.then_inc(spot_ready.handle, 1)

            def decay(c):
                for t in range(TT):
                    banks = free_spot(c, ("decay", 0), t)
                    tok = slice(t * P, t * P + P)
                    for e in range(2):
                        for p in range(PAIRS):
                            dst = banks[:, e, p * P:p * P + P]
                            one = head_row(H + 2 * p + e).to_broadcast([ROWS, P])
                            pe.matmul(dst, one, row[ROWA:ROWA + ROWS, 2, tok], start=True, stop=False)
                            pe.matmul(dst, row[ROWA:ROWA + ROWS, 1, tok], one, start=False, stop=False)
                            mm = pe.matmul(dst, identb[:, :], delta_mask[:, :], start=False, stop=True)
                    mm.then_inc(spot_ready.handle, 1)

            def pairwise(c, name, rhs, signal_):
                pe.wait_ge(*signal_)
                for t in range(TT):
                    banks = free_spot(c, (name, 0), t)
                    tok = slice(t * P, t * P + P)
                    for e in range(2):
                        half = slice(HD * e, HD * e + HD)
                        for p in range(PAIRS):
                            mm = pe.matmul(banks[:, e, p * P:p * P + P], qkv[half, 4 + p, tok], rhs[half, p, tok],
                                           start=True, stop=True)
                    mm.then_inc(spot_ready.handle, 1)

            def sixteen(banks, t, lhs, rhs, turned=False):
                for e in range(2):
                    for p in range(PAIRS):
                        mm = pe.matmul(banks[:, e, p * P:p * P + P], lhs[:, t, e, p, :],
                                       rhs if turned else rhs[:, t, e, p, :], start=True, stop=True,
                                       is_transpose=turned)
                mm.then_inc(spot_ready.handle, 1)

            def level1(c):
                pe.wait_ge(*level_made.at(c, 1))
                for t in range(TT):
                    sixteen(free_spot(c, ("level1", 0), t), t, inv_t, ident, turned=True)

            def taken_spot(c, step, i):
                n, _, s = spot_of(c, step, i)
                pe.wait_ge(*spot_taken[s].at(c, n // 3 + 1))

            def level(c, s):
                before = ("level1", 0) if s == 1 else ("level", s - 1)
                pe.wait_ge(*level_made.at(c, s + 1))
                for t in range(TT):
                    taken_spot(c, before, t if s == 1 else 2 + 2 * t)
                    sixteen(free_spot(c, ("level", s), t), t, b_m, inv)
                for t in range(TT):
                    if s < 5:
                        taken_spot(c, ("level", s), t)
                        if s > 1:
                            taken_spot(c, before, 3 + 2 * t)
                        sixteen(free_spot(c, ("level", s), 2 + 2 * t), t, inv_t, x_m)
                        sixteen(free_spot(c, ("level", s), 3 + 2 * t), t, x_m, inv_t)
                    else:
                        taken_spot(c, ("level", s), t)
                        taken_spot(c, before, 3 + 2 * t)
                        sixteen(free_spot(c, ("level", s), 2 + t), t, x_m, inv_t)

            def wu(c):
                taken_spot(c, ("level", 5), 2)
                taken_spot(c, ("level", 5), 3)
                banks = free_spot(c, ("wu", 0), 0)
                for h in range(H):
                    p, e = h // 2, h % 2
                    for t in range(TT):
                        mm = pe.matmul(banks[HD * e:HD * e + HD, p // 2, p % 2 * T + t * P:p % 2 * T + t * P + P],
                                       kbe[:, t, h * HD:h * HD + HD], inv_t[:, t, e, p, :], start=True, stop=True)
                mm.then_inc(spot_ready.handle, 1)
                banks = free_spot(c, ("wu", 0), 1)
                for h in range(H):
                    for t in range(TT):
                        mm = pe.matmul(banks[:, t, h * HD:h * HD + HD], inv_t[:, t, h % 2, h // 2, :],
                                       vb[:, t, h * HD:h * HD + HD], start=True, stop=True)
                mm.then_inc(spot_ready.handle, 1)

            def scan_v(c, k):
                if k == 0:
                    taken_spot(c, ("wu", 0), 0)
                banks = free_spot(c, ("scan_v", k))
                pe.wait_ge(*state_made.at(c, k + 1))
                half = slice(HD * (k % 2), HD * (k % 2) + HD)
                for p in range(PAIRS):
                    mm = pe.matmul(banks[half, 0, p * P:p * P + P], w_t[:, p, k * CHUNK:(k + 1) * CHUNK],
                                   state[:, p, :], start=True, stop=True)
                mm.then_inc(spot_ready.handle, 1)

            def scan_s(c, k):
                taken_spot(c, ("scan_v", k), 0)
                banks = free_spot(c, ("scan_s", k))
                t, r = k // 2, HD * (k % 2)
                for p in range(PAIRS):
                    pe.matmul(banks[:, 0, p * CHUNK:(p + 1) * CHUNK], state[:, p, :],
                              q_dec[:, p, k * CHUNK:(k + 1) * CHUNK], start=True, stop=False, skip_group_check=True)
                    for e in range(2):
                        h = 2 * p + e
                        pe.matmul(banks[HD * e:HD * e + HD, 0, p * CHUNK:(p + 1) * CHUNK],
                                  vnew[:, h * HD:h * HD + HD], qk_t[:, t, e, p, r:r + CHUNK],
                                  start=False, stop=True, skip_group_check=True)
                for p in range(PAIRS):
                    mm = pe.matmul(banks[:, 1, p * P:p * P + P], kdn[r:r + HD, t, p * P:p * P + P],
                                   vnew[r:r + HD, p * P:p * P + P], start=True, stop=True)
                mm.then_inc(spot_ready.handle, 1)

            def onorm(c):
                pe.wait_ge(*squares.at(c, 3))
                banks = free_spot(c, ("onorm", 0))
                for b in range(2):
                    mm = pe.matmul(banks[:, b, :], blk, sq[:, 2 * b:2 * b + 2, :], start=True, stop=True)
                mm.then_inc(spot_ready.handle, 1)

            def branch(c, i):
                b, u = i // 4, unit(c, "br", i // 2, i % 2)[0]
                w = group(c, "br", i // 2)
                dst = free_unit(c, u)
                if i == 8:
                    pe.wait_ge(*delta_done.at(c, 1))
                if i in (0, 4):
                    taken_spot(c, ("values", 4 * b + 3), 0)
                src = (o_att[:, 0:4, :], o_att[:, 4:8, :], o_dn)[b]
                for m in range(2):
                    mm = product(dst[:, m * T:m * T + T], w, 4, 512, (2 * (i % 2) + m) * P, src)
                mm.then_inc(lin_ready.handle, 1)

            def mix_out(c, i):
                u = unit(c, "out", i // 2, i % 2)[0]
                w = group(c, "out", i // 2)
                dst = free_unit(c, u)
                if i == 0:
                    pe.wait_ge(*merged_made.at(c, 1))
                for m in range(2):
                    mm = product(dst[:, m * T:m * T + T], w, KD, 512, (2 * (i % 2) + m) * P, merged)
                mm.then_inc(lin_ready.handle, 1)
                if i == 1:
                    ada_sums(c, 5)
                if i == 2:
                    ada_turn(c, 5)
                if i == 3:
                    ada_sums(c, 6)
                    square_sums(c, 1)
                    ada_turn(c, 6)

            def mixer(c):
                for step, i in MIXER:
                    if step == "lin":
                        plain(c, i[0], 0, i[1])
                    elif step == "gate":
                        plain(c, "gate", i // 2, i % 2)
                    elif step == "kk":
                        pairwise(c, "kk", k_beta, k_beta_made.at(c, 1))
                    elif step == "qk":
                        pairwise(c, "qk", qkv, k_beta_made.at(c, 1))
                    elif step in ("latnorm", "rowcols", "krot", "qrot", "l2", "spread", "natural", "decay", "level1", "wu", "onorm"):
                        {"latnorm": latnorm, "rowcols": rows, "krot": krot, "qrot": qrot, "l2": l2, "spread": spread,
                         "natural": natural, "decay": decay, "level1": level1, "wu": wu, "onorm": onorm}[step](c)
                    elif step not in ("norm", "conv", "soft", "rows"):
                        {"scores": scores, "turn": turn, "values": values, "level": level, "scan_v": scan_v,
                         "scan_s": scan_s, "br": branch, "out": mix_out}[step](c, i)

            def plain_two(c, name, part):
                u, _ = unit(c, name, 0, part)
                w = group(c, name)
                dst = free_unit(c, u)
                if name == "q":
                    for m in range(2):
                        mm = product(dst[:, m * T:m * T + T], w, KD, 512, (2 * part + m) * P, act,
                                     (c, 0) if (part, m) == (0, 0) else None)
                elif name == "kuv":
                    mm = product(dst[:, 0:T], w, KD, 512, 2 * part * P, act,
                                 (c, 0) if (c.sec, part) == ("kv", 0) else None)
                    if part == 0:
                        mm = product(dst[:, T:2 * T], w, KD, 512, P, act)
                    else:
                        for t in range(TT):
                            for kt in range(KD):
                                mm = pe.matmul(dst[:, T + t * P:T + t * P + P], act[:, kt, t * P:t * P + P],
                                               w[:, kt * 512 + 384:kt * 512 + 512], start=(kt == 0), stop=(kt == KD - 1))
                else:
                    for kt in range(KD):
                        mm = pe.matmul(dst, act[:, kt, part * P:part * P + P], w[:, kt * 512:kt * 512 + 512],
                                       start=(kt == 0), stop=(kt == KD - 1))
                mm.then_inc(lin_ready.handle, 1)

            def scores_two(c, i):
                p, tok = i // 2, slice(i % 2 * P, i % 2 * P + P)
                first = 0 if c.sec == "two" else T
                if i == 0:
                    taken_spot(c, ("kdup", 0), 0)
                    if c.sec == "two":
                        pe.wait_ge(*given.at(c, 2))
                banks = free_spot(c, ("scores", i))
                for e in range(2):
                    half = slice(HD * e, HD * e + HD)
                    mm = pe.matmul(banks[:, e, 0:2 * T - first], qk_m[half, p, tok], keys[half, p // 2, first:],
                                   start=True, stop=True)
                mm.then_inc(spot_ready.handle, 1)

            def turn_two(c, i):
                banks = free_spot(c, ("turn", i))
                pe.wait_ge(*prob_made.at(c, i + 1))
                for e in range(2):
                    for b in range(4 if c.sec == "two" else 2):
                        mm = pe.matmul(banks[:, e, b * P:b * P + P], prob2[:, i % 2, e, b * P:b * P + P], ident,
                                       start=True, stop=True, is_transpose=True)
                mm.then_inc(spot_ready.handle, 1)

            def values_two(c, i):
                taken_spot(c, ("turn", i), 0)
                banks = free_spot(c, ("values", i))
                n, first = (4, 0) if c.sec == "two" else (2, 2)
                for e in range(2):
                    for b in range(n):
                        mm = pe.matmul(banks[HD * e:HD * e + HD, 0, 0:P], vals[:, first + b, i // 4 * HD:i // 4 * HD + HD],
                                       probT2[:, e, b * P:b * P + P], start=(b == 0), stop=(b == n - 1))
                mm.then_inc(spot_ready.handle, 1)

            def rest_two(c, step):
                rotated = c.sec == "two"
                if step == "qnorm":
                    pe.wait_ge(*squares.at(c, 1))
                    banks = free_spot(c, (step, 0))
                    for b in range(2):
                        mm = pe.matmul(banks[:, b, :], blk, sq[:, 2 * b:2 * b + 2, :], start=True, stop=True)
                elif step == "knorm":
                    pe.wait_ge(*squares.at(c, 1))
                    banks = free_spot(c, (step, 0))
                    mm = pe.matmul(banks[:, 0, 0:T], blk, sq[:, 4, :], start=True, stop=True)
                elif step == "rot":
                    pe.wait_ge(*qk_scaled.at(c, 1))
                    banks = free_spot(c, (step, 0), 0)
                    for b in range(2):
                        mm = pe.matmul(banks[:, b, :], rot, qk_m[:, 2 * b:2 * b + 2, :], start=True, stop=True)
                    mm.then_inc(spot_ready.handle, 1)
                    banks = free_spot(c, (step, 0), 1)
                    mm = pe.matmul(banks[:, 0, 0:T], rot, qk_m[:, 4, :], start=True, stop=True)
                elif step == "kdup":
                    pe.wait_ge(*(qk_turned if rotated else qk_scaled).at(c, 1))
                    banks = free_spot(c, (step, 0))
                    for k in range(2):
                        mm = pe.matmul(banks[:, 0, k * T:k * T + T], tbl[:, B_DUP + k * P:B_DUP + k * P + P],
                                       qk_m[:, 4, :], start=True, stop=True)
                elif step == "fourier":
                    for t in range(2):
                        pe.wait_ge(*taken(c, unit(c, "fg", 0, t)[0]))
                    banks = free_spot(c, (step, 0), 0)
                    for m in range(2):
                        for t in range(TT):
                            mm = pe.matmul(banks[:, m, :], f_nat[:, t, m * P:m * P + P],
                                           tbl[:, B_DFT + t * 512:B_DFT + t * 512 + 512], start=(t == 0), stop=(t == 1))
                    mm.then_inc(spot_ready.handle, 1)
                    taken_spot(c, (step, 0), 0)
                    banks = free_spot(c, (step, 0), 1)
                    for m in range(2):
                        dst = banks[:, 0, m * T:m * T + T]
                        pe.matmul(dst, tbl[:, B_CD:B_CD + P], f_mid[:, 2 * m, :], start=True, stop=False)
                        mm = pe.matmul(dst, tbl[:, B_SD:B_SD + P], f_mid[:, 2 * m + 1, :], start=False, stop=True)
                elif step == "spatial":
                    pe.wait_ge(*g_made.at(c, 1))
                    banks = free_spot(c, (step, 0))
                    for h in range(4):
                        for t in range(TT):
                            mm = pe.matmul(banks[HD * (h % 2):HD * (h % 2) + HD, 0, h // 2 * T + t * P:h // 2 * T + t * P + P],
                                           g_nat[:, t, h * HD:h * HD + HD], vec_b[:, W_WS + h * P:W_WS + h * P + P],
                                           start=True, stop=True)
                mm.then_inc(spot_ready.handle, 1)

            def out_two(c, i):
                u = unit(c, "out", i // 2, i % 2)[0]
                w = group(c, "out", i // 2)
                dst = free_unit(c, u)
                if i == 0:
                    pe.wait_ge(*mix_made.at(c, 1))
                    taken_spot(c, ("fourier", 0), 1)
                    taken_spot(c, ("values", 7), 0)
                for m in range(2):
                    mm = product(dst[:, m * T:m * T + T], w, KD, 512, (2 * (i % 2) + m) * P, o_att)
                mm.then_inc(lin_ready.handle, 1)

            def two(c, order):
                for step, i in order:
                    if step == "sum":
                        square_sums(c, i)
                    elif step == "lin":
                        plain_two(c, *i)
                    elif step in ("scores", "turn", "values", "out"):
                        {"scores": scores_two, "turn": turn_two, "values": values_two, "out": out_two}[step](c, i)
                    elif step not in ("norm", "final", "squares", "soft"):
                        rest_two(c, step)
                if c.sec == "kv":
                    return
                n0, u0 = GROUP[c.sec]["m1", 0]

                def up(it, s):
                    n = n0 + s
                    pe.wait_ge(*loaded[n % SLOTS].at(c, it * 16 + (n // SLOTS + 1) * 16))
                    for part in range(2):
                        dst = free_unit(c, u0 + 2 * s + part, it * 3)
                        for m in range(2):
                            mm = product(dst[:, m * T:m * T + T], slot[n % SLOTS], KD, 512, (2 * part + m) * P, act,
                                         (c, KD) if (s, part, m) == (0, 0, 0) else None)
                        mm.then_inc(lin_ready.handle, 1)

                with pe.Fori(0, 2) as it:
                    for s in range(3):
                        up(it, s)
                for s in range(6, 8):
                    up(0, s)
                u1 = GROUP[c.sec]["m2", 0][1]
                pe.wait_ge(*taken(c, u1 - 1))
                pe.wait_ge(*taken(c, u1 - 2))
                for m in range(KD):
                    w = group(c, "m2", m)
                    dst = free_unit(c, u1 + m)
                    product(dst[:, 0:T], w, KF2, P, 0, hT).then_inc(lin_ready.handle, 1)
                square_sums(c, 1)

            pe.wait_ge(consts_made, 1)
            square_sums(Place("load"), 0)
            pe.wait_ge(cond_made, 1)
            with pe.Fori(0, DEPTH) as l:
                c = Place("one", l)
                ffn(c, 0)
                mixer(c)
                ffn(c, 1)
            square_sums(Place("cload"), 0)
            pe.wait_ge(tables_here, 16)
            two(Place("ctx"), CTX)
            two(Place("kv"), KV)
            with pe.Fori(0, DEPTH) as l:
                two(Place("two", l), TWO)

        @block.scalar
        def _(act_e):
            e_ = act_e

            def activate(dst, src, func, **kw):
                return nc.scalar.activation(dst, src, func, **kw)

            def wait_spot(c, step, i=0):
                n, banks, s = spot_of(c, step, i)
                e_.wait_ge(*spot_ready.at(c, n + 1))
                return banks, spot_taken[s].handle

            def wait_unit(c, u, before=0):
                e_.wait_ge(*lin_ready.at(c, before + u + 1))
                return lin[:, u % 2, :], lin_taken[u % 2].handle

            def root(dst, src, scale, signal_):
                activate(dst, src, ACT.Ln, scale=scale, bias=EPS).then_inc(signal_, 1)
                e_.drain()
                return activate(dst, dst, ACT.Exp, scale=-0.5)

            def square_piece(c, i, k):
                units, _ = pieces(c, i)
                n = KD // max(len(units), 1)
                e_.drain()
                if units:
                    e_.wait_ge(*taken(c, units[k]))
                activate(sq[:, n * k:n * k + n, :], summed(c)[0][:, n * k:n * k + n, :], ACT.Square
                         ).then_inc(res_squares.handle, 1)

            def res_root(c, i):
                e_.preload_act_table_set(EXP_LN)
                banks, free = wait_spot(c, ("sum", i))
                root(summed(c)[1][:, :], banks[:, 0, 0:T], 1.0 / D, free).then_inc(res_rstd.handle, 1)

            def ada_copy(c, i):
                src, free = wait_unit(c, unit(c, "ada", i)[0])
                activate(ada_s[:, i % 2, :], src, ACT.Copy).then_inc(free, 1)

            def ffn(c, which):
                ubase = (0, FFN2_UNIT)[which]

                def gu(it, s):
                    for f in range(2):
                        u = ubase + 2 * s + f
                        e_.wait_ge(*lin_taken[u % 2].at(c, it * 3 + u // 2))
                        src, _ = wait_unit(c, u, it * 6)
                        activate(sg[:, f, :], src[:, 0:T], ACT.Silu).then_inc(gate_made.handle, 1)

                with e_.Fori(0, GU_GROUPS // 3) as it:
                    for s in range(3):
                        gu(it, s)
                for s in range(GU_GROUPS // 3 * 3, GU_GROUPS):
                    gu(0, s)
                for m in range(KD):
                    square_piece(c, 2 * which, m)
                    if m % 2 == 0:
                        ada_copy(c, 7 * which + m // 2)
                ada_copy(c, 7 * which + 4)
                res_root(c, 2 * which)

            def plain(c, name, part):
                u = unit(c, name, 0, part)[0]
                if name == "lat":
                    src, free = wait_unit(c, u)
                    activate(lat[:, 2 * part:2 * part + 2, :].rearrange("p a t -> p (a t)"), src, ACT.Copy).then_inc(free, 1)
                if name == "fq":
                    src, free = wait_unit(c, u)
                    activate(qk_f[:, 2 * part:2 * part + 2, :].rearrange("p a t -> p (a t)"), src, ACT.Copy, scale=FOX_SCALE
                             ).then_inc(free, 1)
                if name in ("dq", "dk", "dv"):
                    src, free = wait_unit(c, u)
                    at = 4 * ("dq", "dk", "dv").index(name) + 2 * part
                    activate(conv_in[:, at:at + 2, TAPS - 1:], src.rearrange("p (a t) -> p a t", a=2), ACT.Copy
                             ).then_inc(free, 1)
                if name == "uq":
                    src, free = wait_unit(c, u)
                    dst = qk_m[:, 2 * part:2 * part + 2, :] if part < 2 else qr[:, 2 * part - 4:2 * part - 2, :]
                    activate(dst.rearrange("p a t -> p (a t)"), src, ACT.Copy, scale=MLA_SCALE).then_inc(free, 1)
                if name == "uk":
                    src, free = wait_unit(c, u)
                    activate(qk_m[:, 4 + 2 * part:6 + 2 * part, :].rearrange("p a t -> p (a t)"), src, ACT.Copy
                             ).then_inc(free, 1)
                if name == "dz":
                    src, free = wait_unit(c, u)
                    if part == 0:
                        e_.wait_ge(*rope_k.at(c, 1))
                        e_.wait_ge(*lat_made.at(c, 1))
                    activate(zs[:, 2 * part:2 * part + 2, :].rearrange("p a t -> p (a t)"), src, ACT.Copy
                             ).then_inc(free, 1)

            def latnorm(c):
                u = unit(c, "lat", 0)[0]
                e_.wait_ge(*taken(c, u))
                e_.wait_ge(*taken(c, u + 1))
                activate(sq[:, 0:3, :], lat[:, 0:3, :], ACT.Square).then_inc(squares.handle, 1)
                banks, free = wait_spot(c, ("latnorm", 0))
                activate(sg[:, 0, :], banks[:, 0, 0:T], ACT.Ln, scale=1.0 / 256, bias=EPS)
                activate(sg[:, 1, :], banks[:, 0, T:2 * T], ACT.Ln, scale=1.0 / P, bias=EPS).then_inc(free, 1)
                e_.drain()
                activate(sg[:, :, :], sg[:, :, :], ACT.Exp, scale=-0.5).then_inc(rstds.handle, 1)

            def rows(c):
                e_.wait_ge(*vec_here.at(c, 16))
                e_.wait_ge(*rows_abs.at(c, 1))
                a, b = slice(ROWA, ROWA + ROWS), slice(ROWB, ROWB + H)
                activate(row[a, 3, :], row[a, 3, :], ACT.Exp, scale=-1.0)
                activate(row[b, 0, :], lat[b, 3, :], ACT.Exp, scale=-1.0)
                activate(alog[a, :], vec[a, V_ALOG:V_ALOG + 1], ACT.Exp)
                e_.drain()
                activate(row[a, 3, :], row[a, 3, :], ACT.Ln, bias=1.0).then_inc(rows_exp.handle, 1)
                e_.wait_ge(*rows_cum.at(c, 1))
                activate(row[a, 4, :], row[a, 2, :], ACT.Exp)
                activate(row[a, 5, :], row[a, 3, :], ACT.Exp).then_inc(rows_done.handle, 1)

            def scores(c, i):
                banks, free = wait_spot(c, ("scores", i))
                e_.wait_ge(*max_made.at(c, i + 1))
                if i >= 2:
                    e_.wait_ge(*spot_ready.at(c, SPOT[c.sec]["turn", i - 2] + 1))
                for e in range(2):
                    for t, cols_ in enumerate((slice(0, P), slice(P, P + T))):
                        ins = activate(prob[:, i % 2, e, cols_], banks[:, e, cols_], ACT.Exp,
                                       bias=mx[:, i % 2, t, e:e + 1], accum_out=rs[:, i % 2, t, e:e + 1])
                ins.then_inc(free, 1)

            def turn(c, i):
                if i >= 2:
                    e_.wait_ge(*spot_ready.at(c, SPOT[c.sec]["values", i - 2] + 1))
                banks, free = wait_spot(c, ("turn", i))
                activate(probT[:, i % 2, :, :], banks[:, :, 0:384], ACT.Copy).then_inc(free, 1)

            def conv(c):
                e_.wait_ge(*conv_done.at(c, 1))
                activate(qkv[:, :, :], qkv[:, :, :], ACT.Silu)
                e_.drain()
                activate(sq[:, :, :], qkv[:, 0:8, :], ACT.Square).then_inc(squares.handle, 1)
                e_.preload_act_table_set(EXP_LN)

            def l2(c):
                for j in range(2):
                    banks, free = wait_spot(c, ("l2", 0), j)
                    dst = sq[:, 4 * j:4 * j + 4, :].rearrange("p (b a) t -> p b (a t)", b=2)
                    root(dst, banks, 1.0, free).then_inc(rstds.handle, 1)

            def decay(c):
                e_.wait_ge(*l2_made.at(c, 1))
                for t in range(TT):
                    banks, free = wait_spot(c, ("decay", 0), t)
                    activate(x_m[:, t].rearrange("p e q c -> p e (q c)"), banks, ACT.Exp).then_inc(free, 1)

            def copy_mats(c, step, i, dst, t):
                banks, free = wait_spot(c, step, i)
                activate(dst[:, t].rearrange("p e q c -> p e (q c)"), banks, ACT.Copy).then_inc(free, 1)

            def wu(c):
                banks, free = wait_spot(c, ("wu", 0), 0)
                activate(w_t.rearrange("p (b a) t -> p b (a t)", b=2), banks, ACT.Copy).then_inc(free, 1)

            def onorm(c):
                e_.wait_ge(*state_made.at(c, 1 + CHUNKS))
                activate(sq[:, 0:4, :], o_dn, ACT.Square).then_inc(squares.handle, 1)
                e_.preload_act_table_set(EXP_LN)
                banks, free = wait_spot(c, ("onorm", 0))
                root(sq[:, 4:8, :].rearrange("p (b a) t -> p b (a t)", b=2), banks, 1.0 / HD, free
                     ).then_inc(rstds.handle, 1)

            def gate(c, i):
                u = unit(c, "gate", i // 2, i % 2)[0]
                src, free = wait_unit(c, u)
                if i >= 2:
                    e_.wait_ge(*taken(c, unit(c, "br", (i - 2) // 2, i % 2)[0]))
                for m in range(2):
                    col = V_BGATE + 2 * i + m
                    ins = activate(gt[:, i % 2, m, :], src[:, m * T:m * T + T], ACT.Sigmoid, bias=vec[:, col:col + 1])
                ins.then_inc(free, 1)

            def mixer(c):
                for step, i in MIXER:
                    e_.drain()
                    if step == "out":
                        square_piece(c, 1, i)
                        if i in (1, 3):
                            ada_copy(c, 5 + i // 2)
                        if i == 3:
                            res_root(c, 1)
                    elif step == "lin":
                        plain(c, *i)
                    elif step == "level1":
                        activate(zs, zs, ACT.Silu).then_inc(z_made.handle, 1)
                        for t in range(TT):
                            copy_mats(c, ("level1", 0), t, inv, t)
                    elif step == "level":
                        for t in range(TT):
                            copy_mats(c, ("level", i), t, x_m, t)
                    elif step in ("scores", "turn", "gate"):
                        {"scores": scores, "turn": turn, "gate": gate}[step](c, i)
                    elif step in ("latnorm", "rows", "l2", "decay", "wu", "onorm") or (step, i) == ("conv", TAPS - 1):
                        {"latnorm": latnorm, "rows": rows, "conv": conv, "l2": l2, "decay": decay, "wu": wu,
                         "onorm": onorm}[step](c)

            def shifts(c, i):
                for kt in range(KD):
                    e_.wait_ge(*scaled.at(c, KD * i + kt + 1))
                    activate(act[:, kt, :], act[:, kt, :], ACT.Identity, bias=cur[:, 24 * i + kt:24 * i + 1 + kt]
                             ).then_inc(normed.handle, 1)

            def lin_two(c, name, part):
                if name == "q":
                    return
                u = unit(c, name, 0, part)[0]
                src, free = wait_unit(c, u)
                if name == "kuv":
                    if c.sec == "kv":
                        e_.wait_ge(*kept.at(c, 0))
                    if part == 0:
                        activate(qk_m[:, 4, :], src[:, 0:T], ACT.Copy)
                        activate(u_two[:, 0, :], src[:, T:2 * T], ACT.Gelu_apprx_tanh).then_inc(free, 1)
                    else:
                        activate(u_two[:, 1, :], src[:, 0:T], ACT.Gelu_apprx_tanh)
                        activate(vals[:, TT:, :], src[:, T:2 * T].rearrange("p (t c) -> p t c", t=TT), ACT.Copy
                                 ).then_inc(free, 1)
                else:
                    activate(g_nat[:, part, :], src[:, T:2 * T], ACT.Gelu_apprx_tanh)
                    activate(f_nat[:, part, :], src[:, 0:T], ACT.Copy).then_inc(free, 1)

            def scores_two(c, i):
                banks, free = wait_spot(c, ("scores", i))
                n = 2 * T if c.sec == "two" else T
                e_.wait_ge(*max_made.at(c, i + 1))
                if i >= 2:
                    e_.wait_ge(*spot_ready.at(c, SPOT[c.sec]["turn", i - 2] + 1))
                for e in range(2):
                    ins = activate(prob2[:, i % 2, e, 0:n], banks[:, e, 0:n], ACT.Exp,
                                   bias=mx[:, i % 2, 0, e:e + 1], accum_out=rs[:, i % 2, 0, e:e + 1])
                ins.then_inc(free, 1)

            def rest_two(c, step):
                if step == "squares":
                    for part in range(2):
                        e_.wait_ge(*taken(c, unit(c, "q", 0, part)[0]))
                    activate(sq[:, 0:5, :], qk_m[:, 0:5, :], ACT.Square).then_inc(squares.handle, 1)
                elif step == "qnorm":
                    e_.preload_act_table_set(EXP_LN)
                    banks, free = wait_spot(c, (step, 0))
                    root(sq[:, 0:4, :].rearrange("p (b a) t -> p b (a t)", b=2), banks, 1.0 / HD, free
                         ).then_inc(rstds.handle, 1)
                elif step == "knorm":
                    if c.sec == "kv":
                        activate(sq[:, 4, :], qk_m[:, 4, :], ACT.Square).then_inc(squares.handle, 1)
                        e_.preload_act_table_set(EXP_LN)
                    banks, free = wait_spot(c, (step, 0))
                    root(sq[:, 4, :], banks[:, 0, 0:T], 1.0 / HD, free).then_inc(rstds.handle, 1)
                    if c.sec != "kv":
                        e_.wait_ge(*g_sums.at(c, 1))
                        activate(cols[:, 0, 0:8], cols[:, 0, 0:8], ACT.Ln, scale=1.0 / HD, bias=EPS)
                        e_.drain()
                        activate(cols[:, 0, 0:8], cols[:, 0, 0:8], ACT.Exp, scale=-0.5).then_inc(rstds.handle, 1)
                elif step == "kdup":
                    banks, free = wait_spot(c, (step, 0))
                    activate(keys[:, :, T:], banks[:, 0, :].rearrange("p (k t) -> p k t", k=2), ACT.Copy,
                             scale=HD ** -0.5).then_inc(free, 1)
                elif step == "fourier":
                    banks, free = wait_spot(c, (step, 0), 0)
                    activate(f_mid.rearrange("p (m a) t -> p m (a t)", m=2), banks, ACT.Copy).then_inc(free, 1)

            def two(c, order):
                for step, i in order:
                    e_.drain()
                    if step == "norm":
                        shifts(c, i)
                    elif step == "final":
                        e_.wait_ge(final_made, KD)
                        square_piece(c, 0, 0)
                    elif step == "sum":
                        for k in range(4 if c.sec != "kv" else 0):
                            square_piece(c, 0, k)
                        res_root(c, 0)
                    elif step == "lin":
                        lin_two(c, *i)
                    elif step == "scores":
                        scores_two(c, i)
                    elif step == "turn":
                        if i:
                            e_.wait_ge(*spot_ready.at(c, SPOT[c.sec]["values", i - 1] + 1))
                        banks, free = wait_spot(c, ("turn", i))
                        n = 2 * T if c.sec == "two" else T
                        activate(probT2[:, :, 0:n], banks[:, :, 0:n], ACT.Copy).then_inc(free, 1)
                    else:
                        rest_two(c, step)
                if c.sec == "kv":
                    return
                u0 = GROUP[c.sec]["m1", 0][1]

                def up(it, s):
                    for k in (2 * s, 2 * s + 1):
                        e_.wait_ge(*lin_taken[(k - 1) % 2].at(c, it * 3 + (u0 + k - 1) // 2 + 1))
                        src, _ = wait_unit(c, u0 + k, it * 6)
                        activate(sg[:, :, :].rearrange("p a t -> p (a t)"), src, ACT.Relu).then_inc(gate_made.handle, 1)

                with e_.Fori(0, 2) as it:
                    for s in range(3):
                        up(it, s)
                for s in range(6, 8):
                    up(0, s)
                for m in range(KD):
                    square_piece(c, 1, m)
                res_root(c, 1)

            e_.wait_ge(x_here, 16)
            square_piece(Place("load"), 0, 0)
            res_root(Place("load"), 0)
            e_.wait_ge(cond_here, 16)
            activate(cond_s, cond_s, ACT.Silu).then_inc(cond_made, 1)
            e_.wait_ge(turn_here, 1)
            activate(cossin[:, 1, :], angle[:, 0, :], ACT.Sin)
            activate(cossin[:, 0, :], angle[:, 1, :], ACT.Sin)
            e_.drain()
            activate(cossin[:, :, :], cossin[:, :, :], ACT.Copy, scale=cst[:, C_LIVE:C_LIVE + 1]).then_inc(turn_done, 1)
            with e_.Fori(0, DEPTH) as l:
                c = Place("one", l)
                ffn(c, 0)
                mixer(c)
                ffn(c, 1)
            e_.wait_ge(ctx_here, 16)
            square_piece(Place("cload"), 0, 0)
            res_root(Place("cload"), 0)
            two(Place("ctx"), CTX)
            two(Place("kv"), KV)
            e_.wait_ge(*kept.at(Place("two"), 0))
            with e_.Fori(0, DEPTH) as l:
                two(Place("two", l), TWO)

        @block.vector
        def _(ve):
            def wait_spot(c, step, i=0):
                n, banks, s = spot_of(c, step, i)
                ve.wait_ge(*spot_ready.at(c, n + 1))
                return banks, spot_taken[s].handle

            def wait_unit(c, u, before=0):
                ve.wait_ge(*lin_ready.at(c, before + u + 1))
                return lin[:, u % 2, :], lin_taken[u % 2].handle

            def two(tile):
                return tile.rearrange("p (a t) -> p a t", a=2)

            def norm(c, dst, gain, roots):
                ve.wait_ge(*res_rstd.at(c, roots))
                for kt in range(KD):
                    ve.scalar_tensor_tensor(dst[:, kt, :], xT[:, kt, :], gain[:, kt:kt + 1], rstd[:, :],
                                            ALU.mult, ALU.mult).then_inc(normed.handle, 1)

            def all_squares(c):
                ve.drain()
                ve.wait_ge(*res_squares.at(c, 1))
                ve.tensor_reduce(part[:, :], sq[:, :, :].rearrange("p k t -> p t k"), AX_X, ALU.add
                                 ).then_inc(res_sums.handle, 1)

            def add_squares(c, i, k):
                units, base = pieces(c, i)
                n = KD // len(units)
                for kt in range(max(n * k, 1), n * k + n):
                    ve.drain()
                    if kt == max(n * k, 1):
                        ve.wait_ge(*res_squares.at(c, base + k + 1))
                    ins = ve.tensor_tensor(part[:, :], sq[:, 0, :] if kt == 1 else part[:, :], sq[:, kt, :], ALU.add)
                if k == len(units) - 2:
                    ins.then_inc(res_sums.handle, 1)

            def ada_bias(c, i):
                banks, free = wait_spot(c, ("ada", i))
                m = bass.ds(c.turn * (4 * ADA_TURN) + 4 * i, 4)
                ve.tensor_tensor(mod[:, m, :], banks[:, 0, 0:8].rearrange("p (m j) -> p m j", m=4),
                                 bias_a[:, m].unsqueeze(2).to_broadcast([P, 4, 2]), ALU.add).then_inc(free, 1)

            def ffn(c, which):
                ve.drain()
                ubase, gain = ((0, V_FFN1), (FFN2_UNIT, V_FFN2))[which]
                if which == 0:
                    ve.wait_ge(*vec_here.at(c, 16))
                norm(c, act, vec[:, gain:gain + KD], 2 * which)
                def gu(it, s):
                    for f in range(2):
                        u = ubase + 2 * s + f
                        silus = 2 * GU_GROUPS * which + 2 * s + f + 1
                        ve.wait_ge(*gate_made.at(c, it * 6 + silus))
                        src, free = wait_unit(c, u, it * 6)
                        ve.tensor_tensor(hT[:, it * 6 + (2 * s + f), :], sg[:, f, :], src[:, T:2 * T], ALU.mult
                                         ).then_inc(free, 1)

                with ve.Fori(0, GU_GROUPS // 3) as it:
                    for s in range(3):
                        gu(it, s)
                for s in range(GU_GROUPS // 3 * 3, GU_GROUPS):
                    gu(0, s)
                for m in range(KD):
                    src, free = wait_unit(c, unit(c, "down", 8 * which + m)[0])
                    ve.scalar_tensor_tensor(xT[:, m, :], src[:, 0:T], 0.5, xT[:, m, :], ALU.mult, ALU.add
                                            ).then_inc(free, 1)
                    if m > 0:
                        add_squares(c, 2 * which, m - 1)
                    if m % 2 == 1:
                        ada_bias(c, 7 * which + m // 2)
                ada_bias(c, 7 * which + 4)

            def plain(c, name, part):
                u = unit(c, name, 0, part)[0]
                if name == "fk":
                    src, free = wait_unit(c, u)
                    ve.tensor_copy(qk_f[:, 4 + 2 * part:6 + 2 * part, :], two(src)).then_inc(free, 1)
                if name in ("fv", "uv"):
                    src, free = wait_unit(c, u)
                    ve.tensor_copy((vn_f if name == "fv" else vn_m)[:, part, :], src).then_inc(free, 1)

            def latnorm(c):
                ve.wait_ge(*rstds.at(c, 1))
                for j in range(3):
                    ins = ve.scalar_tensor_tensor(latn[:, j, :], lat[:, j, :], vec[:, V_QN + j:V_QN + j + 1],
                                                  sg[:, j // 2, :], ALU.mult, ALU.mult)
                ins.then_inc(lat_made.handle, 1)

            def rows(c):
                a, b = slice(ROWA, ROWA + ROWS), slice(ROWB, ROWB + H)
                ve.tensor_scalar(row[a, 0, :], lat[a, 3, :], vec[a, V_BIAS:V_BIAS + 1], cst[a, C_SIGN:C_SIGN + 1],
                                 ALU.add, ALU.mult)
                ve.drain()
                ve.scalar_tensor_tensor(row[a, 3, :], row[a, 0, :], -1.0, row[a, 0, :], ALU.mult, ALU.max
                                        ).then_inc(rows_abs.handle, 1)
                ve.wait_ge(*rows_exp.at(c, 1))
                ve.scalar_tensor_tensor(row[a, 0, :], row[a, 0, :], 0.0, row[a, 3, :], ALU.max, ALU.add)
                ve.tensor_scalar(row[b, 0, :], row[b, 0, :], 1.0, None, ALU.add)
                ve.drain()
                ve.tensor_scalar(row[a, 0, :], row[a, 0, :], alog[a, 0:1], None, ALU.mult)
                ve.reciprocal(row[b, 1, :], row[b, 0, :])
                ve.drain()
                ve.tensor_tensor_scan(row[a, 1, :], cst[a, C_RESET:C_RESET + T], row[a, 0, :], 0.0, ALU.mult, ALU.add)
                ve.drain()
                chunks = row[a, 1, :].rearrange("p (c i) -> p c i", c=CHUNKS)
                ve.tensor_tensor(row[a, 3, :].rearrange("p (c i) -> p c i", c=CHUNKS), chunks,
                                 chunks[:, :, CHUNK - 1:CHUNK].to_broadcast([ROWS, CHUNKS, CHUNK]), ALU.subtract)
                ve.tensor_scalar(row[a, 2, :], row[a, 1, :], -1.0, None, ALU.mult).then_inc(rows_cum.handle, 1)

            def rowcols(c):
                banks, free = wait_spot(c, ("rowcols", 0))
                ve.tensor_copy(cols[:, :, 0:32], banks[:, 0, 0:96].rearrange("p (t k) -> p t k", t=TT)[:, :, 0:32])
                ve.tensor_copy(cols[:, :, 32:40], banks[:, 1, 0:16].rearrange("p (t k) -> p t k", t=TT)
                               ).then_inc(free, 1)
                ve.drain()
                ve.tensor_tensor(cols[:, :, 40:48], cols[:, :, 32:40], cols[:, :, 8:16], ALU.mult)

            def krot(c):
                ve.wait_ge(turn_done, 1)
                banks, free = wait_spot(c, ("krot", 0))
                ve.tensor_tensor(part[:, :], banks[:, 0, 0:T], cossin[:, 1, :], ALU.mult).then_inc(free, 1)
                ve.tensor_tensor(kr[:, :], lat[:, 3, :], cossin[:, 0, :], ALU.mult)
                ve.drain()
                ve.tensor_tensor(kr[:, :], kr[:, :], part[:, :], ALU.add).then_inc(rope_k.handle, 1)

            def qrot(c):
                banks, free = wait_spot(c, ("qrot", 0))
                def table(k):
                    return cossin[:, k, :].unsqueeze(1).to_broadcast([P, PAIRS, T])
                turned = hT[:, 0:4, :]
                ve.tensor_tensor(turned, banks.rearrange("p b (a t) -> p (b a) t", a=2), table(1), ALU.mult
                                 ).then_inc(free, 1)
                ve.tensor_tensor(qr[:, :, :], qr[:, :, :], table(0), ALU.mult)
                ve.drain()
                ve.tensor_tensor(qr[:, :, :], qr[:, :, :], turned, ALU.add).then_inc(rope_q.handle, 1)

            def scores(c, i):
                banks, _ = wait_spot(c, ("scores", i))
                for t, cols_ in enumerate((slice(0, P), slice(P, P + T))):
                    ins = ve.tensor_reduce(mx[:, i % 2, t, :], banks[:, :, cols_], AX_X, ALU.max, negate=True)
                ins.then_inc(max_made.handle, 1)

            def normalise(c, i):
                n, _, s = spot_of(c, ("scores", i))
                ve.wait_ge(*spot_taken[s].at(c, n // 3 + 1))
                ve.reciprocal(rs[:, i % 2, :, :], rs[:, i % 2, :, :])
                ve.drain()
                for t, cols_ in enumerate((slice(0, P), slice(P, P + T))):
                    keys = cols_.stop - cols_.start
                    ins = ve.tensor_tensor(prob[:, i % 2, :, cols_], prob[:, i % 2, :, cols_],
                                           rs[:, i % 2, t, :].unsqueeze(2).to_broadcast([P, 2, keys]), ALU.mult)
                ins.then_inc(prob_made.handle, 1)

            def values(c, i):
                banks, free = wait_spot(c, ("values", i))
                ve.tensor_copy(o_att[:, i, :], banks[:, 0, 0:T]).then_inc(free, 1)

            def conv(c, tap):
                u = unit(c, "dv", 0)[0]
                ve.wait_ge(*taken(c, u))
                ve.wait_ge(*taken(c, u + 1))
                for m in range(12):
                    w = vec[:, V_TAP + 12 * tap + m:V_TAP + 12 * tap + m + 1]
                    src = conv_in[:, m, tap:tap + T]
                    if tap == 0:
                        ins = ve.tensor_scalar(qkv[:, m, :], src, w, None, ALU.mult)
                    else:
                        ins = ve.scalar_tensor_tensor(qkv[:, m, :], src, w, qkv[:, m, :], ALU.mult, ALU.add)
                if tap == TAPS - 1:
                    ins.then_inc(conv_done.handle, 1)

            def l2(c):
                ve.wait_ge(*rstds.at(c, 2))
                ve.scalar_tensor_tensor(qkv[:, 0:4, :], qkv[:, 0:4, :], HD ** -0.5, sq[:, 0:4, :], ALU.mult, ALU.mult)
                ve.wait_ge(*rstds.at(c, 3))
                ve.tensor_tensor(qkv[:, 4:8, :], qkv[:, 4:8, :], sq[:, 4:8, :], ALU.mult).then_inc(l2_made.handle, 1)
                ve.drain()

            def spread(c):
                banks, free = wait_spot(c, ("spread", 0), 0)
                ve.tensor_tensor(k_beta, qkv[:, 4:8, :], banks.rearrange("p b (a t) -> p (b a) t", a=2), ALU.mult
                                 ).then_inc(free, 1)
                banks, free = wait_spot(c, ("spread", 0), 1)
                wide = banks.rearrange("p b (a t) -> p (b a) t", a=2)
                ve.tensor_copy(glast[:, :, :], wide[:, :, CHUNK - 1::CHUNK])
                ve.tensor_tensor(q_dec, qkv[:, 0:4, :], wide, ALU.mult).then_inc(free, 1)
                ve.drain()
                ve.memset(vnew[:, :], 0.0)
                ve.memset(state[:, :, :], 0.0)
                ve.drain().then_inc(k_beta_made.handle, 1)

            def natural(c):
                def per_head(col):
                    return cols[:, :, col:col + H].unsqueeze(3).to_broadcast([P, TT, H, HD])

                def heads(t):
                    return t.rearrange("p t (h d) -> p t h d", h=H)
                banks, free = wait_spot(c, ("natural", 0), 0)
                ve.tensor_tensor(heads(kbe), heads(banks), per_head(40), ALU.mult)
                ve.tensor_tensor(heads(kdn), heads(banks), per_head(24), ALU.mult).then_inc(free, 1)
                banks, free = wait_spot(c, ("natural", 0), 1)
                ve.tensor_tensor(heads(vb), heads(banks), per_head(32), ALU.mult).then_inc(free, 1)

            def with_decay(c, name, dst):
                for t in range(TT):
                    banks, free = wait_spot(c, (name, 0), t)
                    n, _, s = spot_of(c, ("decay", 0), t)
                    ve.wait_ge(*spot_taken[s].at(c, n // 3 + 1))
                    ve.tensor_tensor(dst[:, t].rearrange("p e q c -> p e (q c)"), banks,
                                     x_m[:, t].rearrange("p e q c -> p e (q c)"), ALU.mult).then_inc(free, 1)

            def all_mats(m):
                return m.rearrange("p t e q c -> p (t e q) c")

            def level_mask(s):
                mask = cst[:, C_LEVEL + s * P:C_LEVEL + s * P + P].unsqueeze(1).to_broadcast([P, 16, P])
                return ve.tensor_tensor(all_mats(b_m), all_mats(m_t), mask, ALU.mult)

            def level1(c):
                ve.drain()
                level_mask(0)
                ve.drain()
                ve.tensor_tensor(all_mats(inv_t), ident.unsqueeze(1).to_broadcast([P, 16, P]), all_mats(b_m),
                                 ALU.subtract).then_inc(level_made.handle, 1)
                ve.drain()
                level_mask(1).then_inc(level_made.handle, 1)

            def level(c, s):
                def less(i, t, dst):
                    banks, free = wait_spot(c, ("level", s), i)
                    flat = dst[:, t].rearrange("p e q c -> p e (q c)")
                    ve.tensor_tensor(flat, flat, banks, ALU.subtract).then_inc(free, 1)
                if s < 5:
                    wait_spot(c, ("level", s), 1)
                    level_mask(s + 1).then_inc(level_made.handle, 1)
                    for t in range(TT):
                        less(2 + 2 * t, t, inv)
                        less(3 + 2 * t, t, inv_t)
                else:
                    for t in range(TT):
                        less(2 + t, t, inv_t)

            def wu(c):
                banks, free = wait_spot(c, ("wu", 0), 1)
                ve.tensor_copy(kbe, banks).then_inc(free, 1)
                ve.drain().then_inc(state_made.handle, 1)

            def scan_v(c, k):
                banks, free = wait_spot(c, ("scan_v", k))
                half = slice(HD * (k % 2), HD * (k % 2) + HD)
                ve.tensor_tensor(vnew[half, :], kbe[half, k // 2, :], banks[half, 0, :], ALU.subtract).then_inc(free, 1)

            def scan_s(c, k):
                banks, free = wait_spot(c, ("scan_s", k))
                ve.tensor_copy(o_dn[:, :, k * CHUNK:(k + 1) * CHUNK],
                               banks[:, 0, 0:T].rearrange("p (a i) -> p a i", a=PAIRS))
                step = sg[:, :, :].rearrange("p a (b c) -> p (a b) c", c=P)
                ve.tensor_tensor(step, banks[:, 1, :].rearrange("p (q c) -> p q c", q=PAIRS),
                                 blk.unsqueeze(1).to_broadcast([P, PAIRS, P]), ALU.mult).then_inc(free, 1)
                ve.tensor_tensor(state[:, :, :], state[:, :, :], glast[:, :, k:k + 1].to_broadcast([P, PAIRS, P]),
                                 ALU.mult)
                ve.drain()
                ve.tensor_tensor(state[:, :, :], state[:, :, :], step, ALU.add).then_inc(state_made.handle, 1)
                ve.drain()

            def onorm(c):
                ve.wait_ge(*rstds.at(c, 4))
                ve.scalar_tensor_tensor(o_dn, o_dn, vec[:, V_ON:V_ON + 1], sq[:, 4:8, :], ALU.mult, ALU.mult)
                ve.drain()
                ve.wait_ge(*z_made.at(c, 1))
                ve.tensor_tensor(o_dn, o_dn, zs, ALU.mult).then_inc(delta_done.handle, 1)

            def branch(c, i):
                u, g = unit(c, "br", i // 2, i % 2)[0], unit(c, "gate", i // 2, i % 2)[0]
                src, free = wait_unit(c, u)
                ve.wait_ge(*taken(c, g))
                dst = merged[:, 2 * (i % 4):2 * (i % 4) + 2, :]
                if i < 4:
                    ve.tensor_tensor(dst, two(src), gt[:, i % 2], ALU.mult).then_inc(free, 1)
                else:
                    tmp = sg[:, :, :]
                    ve.tensor_tensor(tmp, two(src), gt[:, i % 2], ALU.mult).then_inc(free, 1)
                    ve.drain()
                    ve.tensor_tensor(dst, dst, tmp, ALU.add)
                    ve.drain()
                if i == 11:
                    ve.drain().then_inc(merged_made.handle, 1)

            def mix_out(c, i):
                src, free = wait_unit(c, unit(c, "out", i // 2, i % 2)[0])
                ve.tensor_tensor(xT[:, 2 * i:2 * i + 2, :], xT[:, 2 * i:2 * i + 2, :], two(src), ALU.add
                                 ).then_inc(free, 1)
                if i > 0:
                    add_squares(c, 1, i - 1)
                if i == 2:
                    ada_bias(c, 5)
                if i == 3:
                    ada_bias(c, 6)

            def mixer(c):
                for step, i in MIXER:
                    ve.drain()
                    if step == "norm":
                        ve.memset(conv_in[:, :, 0:TAPS - 1], 0.0)
                        ve.drain()
                        norm(c, act, vec[:, V_MIX:V_MIX + KD], 1)
                    elif step == "lin":
                        plain(c, *i)
                    elif step == "kk":
                        with_decay(c, "kk", m_t)
                    elif step == "qk":
                        with_decay(c, "qk", qk_t)
                    elif step in ("latnorm", "rows", "rowcols", "krot", "qrot", "l2", "spread", "natural", "level1", "wu", "onorm"):
                        {"latnorm": latnorm, "rows": rows, "rowcols": rowcols, "krot": krot, "qrot": qrot, "l2": l2,
                         "spread": spread, "natural": natural, "level1": level1, "wu": wu, "onorm": onorm}[step](c)
                    elif step in ("conv", "scores", "soft", "values", "level", "scan_v", "scan_s", "br", "out"):
                        {"conv": conv, "scores": scores, "soft": normalise, "values": values, "level": level, "scan_v": scan_v, "scan_s": scan_s,
                         "br": branch, "out": mix_out}[step](c, i)

            def norm_two(c, i):
                res, root = residual(c)
                if i == 0:
                    ve.wait_ge(*vec_b_here.at(c, 0 if c.sec == "two" else 16))
                    if c.sec == "two":
                        ve.tensor_copy(cur[:, :], mod[:, bass.ds(c.turn * 48, 48), 0])
                    else:
                        l = 0 if c.sec == "ctx" else 1
                        ve.tensor_copy(cur[:, :], mod[:, 48 * l:48 * l + 48, 1])
                    ve.drain()
                    for at, w in ((8, W_N1), (32, W_N2)):
                        ve.scalar_tensor_tensor(cur[:, at:at + 8], cur[:, at:at + 8], 1.0, vectors(c)[:, w:w + 8],
                                                ALU.add, ALU.mult)
                    ve.drain()
                ve.wait_ge(*res_rstd.at(c, i))
                for kt in range(KD):
                    ve.scalar_tensor_tensor(act[:, kt, :], res[:, kt, :], cur[:, 24 * i + 8 + kt:24 * i + 9 + kt],
                                            root[:, :], ALU.mult, ALU.mult).then_inc(scaled.handle, 1)

            def rest_two(c, step):
                if step == "knorm":
                    if c.sec != "kv":
                        for t in range(TT):
                            ve.wait_ge(*taken(c, unit(c, "fg", 0, t)[0]))
                        ve.tensor_tensor(hT[:, 0:2, :], g_nat, g_nat, ALU.mult)
                        ve.drain()
                        ve.tensor_reduce(cols[:, 0, 0:8].rearrange("p (t h) -> p t h", t=TT),
                                         hT[:, 0:2, :].rearrange("p t (h d) -> p t h d", h=4), AX_X, ALU.add
                                         ).then_inc(g_sums.handle, 1)
                        ve.wait_ge(*rstds.at(c, 1))
                        ve.scalar_tensor_tensor(qk_m[:, 0:4, :], qk_m[:, 0:4, :], vec_b[:, W_QG:W_QG + 1],
                                                sq[:, 0:4, :], ALU.mult, ALU.mult)
                    ve.wait_ge(*rstds.at(c, 1 if c.sec == "kv" else 2))
                    ve.scalar_tensor_tensor(qk_m[:, 4, :], qk_m[:, 4, :], vectors(c)[:, W_KG:W_KG + 1], sq[:, 4, :],
                                            ALU.mult, ALU.mult)
                    ve.drain().then_inc(qk_scaled.handle, 1)
                    if c.sec != "kv":
                        ve.wait_ge(*rstds.at(c, 3))
                        heads = g_nat.rearrange("p t (h d) -> p t h d", h=4)
                        ve.tensor_tensor(heads, heads, cols[:, 0, 0:8].rearrange("p (t h) -> p t h", t=TT
                                         ).unsqueeze(3).to_broadcast([P, TT, 4, HD]), ALU.mult).then_inc(g_made.handle, 1)
                elif step == "rot":
                    def table(at, n):
                        return tbl[:, at:at + T].unsqueeze(1).to_broadcast([P, n, T])
                    banks, free = wait_spot(c, (step, 0), 0)
                    ve.tensor_tensor(hT[:, 0:4, :], banks.rearrange("p b (a t) -> p (b a) t", a=2), table(B_SIN, 4),
                                     ALU.mult).then_inc(free, 1)
                    banks, free = wait_spot(c, (step, 0), 1)
                    ve.tensor_tensor(hT[:, 4, :], banks[:, 0, 0:T], tbl[:, B_SIN:B_SIN + T], ALU.mult).then_inc(free, 1)
                    ve.tensor_tensor(qk_m[:, 0:5, :], qk_m[:, 0:5, :], table(B_COS, 5), ALU.mult)
                    ve.drain()
                    ve.tensor_tensor(qk_m[:, 0:5, :], qk_m[:, 0:5, :], hT[:, 0:5, :], ALU.add
                                     ).then_inc(qk_turned.handle, 1)
                elif step == "fourier":
                    banks, free = wait_spot(c, (step, 0), 1)
                    ve.tensor_copy(o_att[:, 4:6, :], two_tiles(banks[:, 0, :])).then_inc(free, 1)
                elif step == "spatial":
                    banks, free = wait_spot(c, (step, 0))
                    for m in range(2):
                        ins = ve.scalar_tensor_tensor(
                            o_att[:, 6 + m, :].rearrange("p (t c) -> p t c", t=TT),
                            banks[:, 0, m * T:m * T + T].rearrange("p (t c) -> p t c", t=TT),
                            vec_b[:, W_VG + m:W_VG + m + 1],
                            vec_b[:, W_BS + m * P:W_BS + m * P + P].unsqueeze(1).to_broadcast([P, TT, P]),
                            ALU.mult, ALU.add)
                    ins.then_inc(free, 1)
                    ve.drain()
                    ve.tensor_tensor(o_att[:, 6:8, :], o_att[:, 6:8, :], u_two, ALU.mult).then_inc(mix_made.handle, 1)

            def two_tiles(tile):
                return tile.rearrange("p (a t) -> p a t", a=2)

            def two_pass(c, order):
                n = 2 * T if c.sec == "two" else T
                for step, i in order:
                    ve.drain()
                    if step == "norm":
                        norm_two(c, i)
                    elif step == "lin" and i[0] == "q":
                        src, free = wait_unit(c, unit(c, "q", 0, i[1])[0])
                        ve.tensor_copy(qk_m[:, 2 * i[1]:2 * i[1] + 2, :], two_tiles(src)).then_inc(free, 1)
                    elif step == "scores":
                        banks, _ = wait_spot(c, ("scores", i))
                        ve.tensor_reduce(mx[:, i % 2, 0, :], banks[:, :, 0:n], AX_X, ALU.max, negate=True
                                         ).then_inc(max_made.handle, 1)
                    elif step == "soft":
                        k, _, s = spot_of(c, ("scores", i))
                        ve.wait_ge(*spot_taken[s].at(c, k // 3 + 1))
                        ve.reciprocal(rs[:, i % 2, 0, :], rs[:, i % 2, 0, :])
                        ve.drain()
                        ve.tensor_tensor(prob2[:, i % 2, :, 0:n], prob2[:, i % 2, :, 0:n],
                                         rs[:, i % 2, 0, :].unsqueeze(2).to_broadcast([P, 2, n]), ALU.mult
                                         ).then_inc(prob_made.handle, 1)
                    elif step == "values":
                        banks, free = wait_spot(c, ("values", i))
                        ve.tensor_copy(o_att[:, i // 2, i % 2 * P:i % 2 * P + P], banks[:, 0, 0:P]).then_inc(free, 1)
                    elif step == "out":
                        src, free = wait_unit(c, unit(c, "out", i // 2, i % 2)[0])
                        res = residual(c)[0]
                        for m in range(2):
                            ins = ve.scalar_tensor_tensor(res[:, 2 * i + m, :], src[:, m * T:m * T + T],
                                                          cur[:, 16 + 2 * i + m:17 + 2 * i + m], res[:, 2 * i + m, :],
                                                          ALU.mult, ALU.add)
                        ins.then_inc(free, 1)
                        if i > 0:
                            add_squares(c, 0, i - 1)
                    elif step == "final":
                        for kt in range(KD):
                            ve.scalar_tensor_tensor(xT[:, kt, :], xT[:, kt, :], cst[:, C_FINAL + kt:C_FINAL + kt + 1],
                                                    rstd[:, :], ALU.mult, ALU.mult).then_inc(final_made, 1)
                        all_squares(c)
                    elif step == "sum":
                        continue
                    else:
                        rest_two(c, step)
                if c.sec == "kv":
                    return
                u0 = GROUP[c.sec]["m1", 0][1]

                def up(it, s):
                    for part_ in range(2):
                        k = 2 * s + part_
                        ve.wait_ge(*lin_ready.at(c, it * 6 + (u0 + k + 1)))
                        src, free = lin[:, (u0 + k) % 2, :], lin_taken[(u0 + k) % 2].handle
                        ve.wait_ge(*gate_made.at(c, it * 6 + (k + 1)))
                        dst = hT[:, bass.ds(it * 12 + 2 * k, 2), :] if s < 6 else hT[:, 2 * k:2 * k + 2, :]
                        ve.tensor_tensor(dst, sg[:, :, :], two_tiles(src), ALU.mult).then_inc(free, 1)

                with ve.Fori(0, 2) as it:
                    for s in range(3):
                        up(it, s)
                for s in range(6, 8):
                    up(0, s)
                u1 = GROUP[c.sec]["m2", 0][1]
                for m in range(KD):
                    src, free = wait_unit(c, u1 + m)
                    res = residual(c)[0]
                    ve.scalar_tensor_tensor(res[:, m, :], src[:, 0:T], cur[:, 40 + m:41 + m], res[:, m, :],
                                            ALU.mult, ALU.add).then_inc(free, 1)
                    if m > 0:
                        add_squares(c, 1, m - 1)

            ve.wait_ge(consts_here, 16)
            ve.memset(ones[:, :], 1.0)
            ve.tensor_copy(identb[:, :], ident)
            ve.tensor_copy(causal[:, :], cst[:, C_CAUSAL:C_CAUSAL + P])
            ve.tensor_copy(delta_mask[:, :], cst[:, C_DELTA:C_DELTA + P])
            ve.drain().then_inc(consts_made, 1)

            all_squares(Place("load"))

            ve.wait_ge(pos_here, 16)
            ve.tensor_copy(angle[:, 3, :], angle[:, 2, :].bitcast(I32))
            ve.drain()
            ve.tensor_scalar(angle[:, 3, :], angle[:, 3, :], cst[:, C_FREQ:C_FREQ + 1], None, ALU.mult)
            ve.drain()
            ve.tensor_scalar(angle[:, 4, :], angle[:, 3, :], 1 / TURN, None, ALU.mult)
            ve.drain()
            ve.tensor_scalar(angle[:, 4, :], angle[:, 4, :], ROUND, None, ALU.add)
            ve.drain()
            ve.tensor_scalar(angle[:, 4, :], angle[:, 4, :], ROUND, None, ALU.subtract)
            ve.drain()
            for piece in TURN_PARTS:
                ve.scalar_tensor_tensor(angle[:, 3, :], angle[:, 4, :], -piece, angle[:, 3, :], ALU.mult, ALU.add)
                ve.drain()
            ve.tensor_scalar(angle[:, 0, :], angle[:, 3, :], HALF_TURN, -HALF_TURN, ALU.min, ALU.max)
            ve.drain()
            ve.scalar_tensor_tensor(angle[:, 1, :], angle[:, 0, :], -1.0, angle[:, 0, :], ALU.mult, ALU.max)
            ve.drain()
            ve.tensor_scalar(angle[:, 1, :], angle[:, 1, :], -1.0, QUARTER_TURN, ALU.mult, ALU.add).then_inc(turn_here, 1)
            ve.wait_ge(bias_here, 16)
            with ve.Fori(0, DEPTH) as l:
                c = Place("one", l)
                ffn(c, 0)
                mixer(c)
                ffn(c, 1)
            all_squares(Place("cload"))
            two_pass(Place("ctx"), CTX)
            two_pass(Place("kv"), KV)
            with ve.Fori(0, DEPTH) as l:
                two_pass(Place("two", l), TWO)


def tiles(w, width):
    *lead, k, n = w.shape
    w = w.reshape(*lead, k // P, P, n // width, width)
    order = list(range(len(lead))) + [len(lead) + 2, len(lead) + 1, len(lead), len(lead) + 3]
    return w.transpose(order).reshape(*lead, n // width, P, k // P * width)


def feature_major(v):
    return np.moveaxis(v.reshape(*v.shape[:-1], -1, P), -1, -2)


def pack_one(i, l):
    def ffn(gu, down, which):
        both = np.stack([gu[:, :FF].reshape(D, GU_GROUPS, 256), gu[:, FF:].reshape(D, GU_GROUPS, 256)], 2)
        parts, down = [tiles(both.reshape(D, 2 * FF), 512)], tiles(down, P)
        for n in range(4):
            parts += [down[2 * n], ada[7 * which + n], down[2 * n + 1]]
        return parts + [ada[7 * which + 4]]

    ada = tiles(i["w_ada_2"][l], 512)
    w = i["w_in"][l]
    ends = np.cumsum([512, 512, 512, 8, 256, 128, 32, 512, 512, 512, 512, 8, 8, 3072])
    fq, fk, fv, ff, cq, ckv, kr, dq, dk, dv, dz, db, da, gate = np.split(w, ends[:-1], axis=1)
    rows = np.zeros((D, P), w.dtype)
    rows[:, 0:32] = rows[:, 64:96] = kr
    rows[:, 32:40], rows[:, 40:48], rows[:, 96:104] = ff, da, db
    uq = i["mla_w_uq"][l].reshape(256, H, 96)
    rope = np.zeros((256, H, HD), w.dtype)
    rope[:, :, 0:32] = uq[:, :, HD:]
    uq = np.concatenate([uq[:, :, :HD].reshape(256, 512), rope.reshape(256, 512)], 1)
    ukv = i["mla_w_ukv"][l].reshape(P, H, 2, HD)
    parts = ffn(i["ffn1_w_gu"][l], i["ffn1_w_down"][l], 0)
    parts += [tiles(np.concatenate([cq, ckv, rows], 1), 512)]
    parts += [tiles(x, 512) for x in (fq, fk, fv, dq, dk, dv)]
    parts += [tiles(uq, 1024), tiles(ukv[:, :, 0].reshape(P, 512), 512), tiles(ukv[:, :, 1].reshape(P, 512), 512),
              tiles(dz, 512)]
    gates = tiles(gate, 512)
    branches = np.concatenate([tiles(i[n][l], 512) for n in ("w_br_fox", "w_br_mla", "w_br_dn")])
    for g in range(6):
        parts += [gates[g], branches[g]]
    out = tiles(i["w_out"][l], 512)
    parts += [out[0], ada[5], out[1], ada[6]]
    return parts + ffn(i["ffn2_w_gu"][l], i["ffn2_w_down"][l], 1)


def vectors_one(i):
    out = np.zeros((DEPTH, P, NV), np.float32)
    for at, name in ((V_FFN1, "ffn1_norm"), (V_MIX, "mix_norm"), (V_FFN2, "ffn2_norm"), (V_BGATE, "b_gate"),
                     (V_QN, "mla_q_norm"), (V_KVN, "mla_kv_norm")):
        v = feature_major(i[name])
        out[:, :, at:at + v.shape[-1]] = v
    taps = feature_major(i["dn_conv_w"])
    out[:, :, V_TAP:V_TAP + 48] = taps.transpose(0, 2, 1, 3).reshape(DEPTH, P, 48)
    out[:, 0:HD, V_ON] = out[:, HD:, V_ON] = i["dn_o_norm"]
    out[:, 32:40, V_BIAS], out[:, 40:48, V_BIAS], out[:, 40:48, V_ALOG] = i["fox_b_f"], i["dn_dt_bias"], i["dn_a_log"]
    return out


def constants():
    c = np.zeros((P, NC_), np.float32)
    p = np.arange(P)
    row, col = p[:, None], p[None, :]
    c[:, C_ID:C_ID + P] = np.eye(P)
    c[:, C_BLK:C_BLK + P] = row // HD == col // HD
    c[:, C_ROT:C_ROT + P] = 1.0 * ((row == col - 16) & (col % 32 >= 16)) - 1.0 * ((row == col + 16) & (col % 32 < 16))
    c[:, C_CAUSAL:C_CAUSAL + P] = np.where(col <= row, 0, NEG)
    c[:, C_DELTA:C_DELTA + P] = np.where((row // CHUNK == col // CHUNK) & (row <= col), 0, NEG)
    for n, s in enumerate(LEVELS):
        c[:, C_LEVEL + n * P:C_LEVEL + n * P + P] = (row // (2 * s) == col // (2 * s)) & (row // s % 2 == 0) & (col // s % 2 == 1)
    for pair in range(PAIRS):
        for e in range(2):
            at = C_PAIR + pair * P + e * HD
            c[ROWA + H + 2 * pair + e, at:at + HD] = 1
            c[ROWB + 2 * pair + e, at:at + HD] = 1
    freq = np.float32(10000.0) ** (-np.arange(16, dtype=np.float32) / np.float32(16))
    for at in (0, 16, 64, 80):
        c[at:at + 16, C_FREQ] = freq
        c[at:at + 16, C_LIVE] = 1
    c[32:40, C_SIGN], c[40:48, C_SIGN] = -1, 1
    c[ROWA:ROWA + ROWS, C_RESET:C_RESET + T] = 1
    c[ROWA + H:ROWA + ROWS, C_RESET:C_RESET + T:CHUNK] = 0
    for j in range(2):
        c[j::32, C_TWO + j] = 1
    return c


def second_tables():
    t = np.zeros((P, NB), np.float64)
    n, d = np.arange(T), np.arange(HD)
    angle = 2 * np.pi * (n[:, None] * n[None, :] % T) / T
    dft = np.concatenate([np.cos(angle), np.sin(angle)], 1) / np.sqrt(T * HD)
    t[:, B_DFT:B_DFT + TT * 512] = dft.reshape(TT, P, 512).transpose(1, 0, 2).reshape(P, TT * 512)
    angle = 2 * np.pi * (d[:, None] * d[None, :] % HD) / HD
    t[:, B_CD:B_CD + P] = np.kron(np.eye(2), np.cos(angle))
    t[:, B_SD:B_SD + P] = np.kron(np.eye(2), -np.sin(angle))
    inv = np.float32(10000.0) ** (-np.arange(0, 32, 2, dtype=np.float32) / np.float32(32))
    at = np.stack([n // 64, n % 64]).astype(np.float32)
    both = (at[:, None, :] * inv[None, :, None]).repeat(2, 0).reshape(2, 2, 16, T).reshape(HD, T)
    t[:, B_COS:B_COS + T] = np.tile(np.cos(both), (2, 1))
    t[:, B_SIN:B_SIN + T] = np.tile(np.sin(both), (2, 1))
    for k in range(2):
        for e in range(2):
            t[k * HD + d, B_DUP + k * P + e * HD + d] = 1
    return t.astype(np.float32)


def pack_two(i, l):
    q, k, v, f, u, g = np.split(i["w_in_2"][l], np.cumsum([512, P, P, 256, 256]), axis=1)
    parts = [tiles(q, 512), tiles(np.concatenate([k, u, v], 1), 512), tiles(np.concatenate([f, g], 1), 512)]
    return parts + [tiles(i["w_out_2"][l], 512), tiles(i["w_mlp1_2"][l], 512), tiles(i["w_mlp2_2"][l], P)]


def vectors_two(i):
    out = np.zeros((DEPTH, P, NW), np.float32)
    out[:, :, W_N1:W_N1 + 8], out[:, :, W_N2:W_N2 + 8] = feature_major(i["norm1_g_2"]), feature_major(i["norm2_g_2"])
    out[:, :, W_QG], out[:, :, W_KG] = np.tile(i["q_norm_g_2"], (1, 2)), np.tile(i["k_norm_g_2"], (1, 2))
    out[:, :, W_VG:W_VG + 2] = feature_major(i["gmlp_v_g_2"])
    bias = i["b_spatial_2"].reshape(DEPTH, 2, 2, 1, P).repeat(HD, 3)
    out[:, :, W_BS:W_BS + 2 * P] = bias.transpose(0, 2, 3, 1, 4).reshape(DEPTH, P, 2 * P)
    out[:, :, W_WS:] = i["w_spatial_2"].transpose(0, 3, 1, 2).reshape(DEPTH, P, 4 * P)
    return out


def tokens(x):
    return x.reshape(T, KD, P).transpose(2, 1, 0)


def laid_out(i):
    two = [pack_two(i, l) for l in range(DEPTH)]
    parts = [part for l in range(DEPTH) for part in pack_one(i, l)] + two[0] + [two[1][1]] + two[0] + two[1]
    consts = constants()
    consts[:, C_FINAL:C_FINAL + KD] = feature_major(i["final_norm"])
    cond = np.zeros((P, KD, 32), np.float32)
    cond[:, :, 0], cond[:, :, 1] = feature_major(i["c_2"][0]), feature_major(i["c_ctx_2"])
    bada = feature_major(i["b_ada_2"]).transpose(1, 0, 2).reshape(P, DEPTH * 48)
    return {"stream": np.concatenate([p.ravel() for p in parts]), "x_in": tokens(i["x"][0]),
            "ctx_in": tokens(i["ctx_2"][0]), "cond": cond, "positions": i["positions"].astype(np.int32),
            "vec1": vectors_one(i), "vec2": vectors_two(i), "bada": bada, "consts": consts,
            "tables": second_tables()}


def kernel(**inputs):
    import concourse.bacc as bacc
    from concourse.bass_utils import run_bass_kernel_spmd

    nc = bacc.Bacc("TRN2", target_bir_lowering=False, num_devices=1)
    arrays, args = {}, []
    for name, a in laid_out({k: np.asarray(v) for k, v in inputs.items()}).items():
        arrays[name] = np.ascontiguousarray(a)
        args.append(nc.dram_tensor(name, a.shape, mybir.dt.from_np(a.dtype), kind="ExternalInput").ap())
    out = nc.dram_tensor("out", (P, KD, T), F32, kind="ExternalOutput").ap()
    build(nc, *args, out)
    got = run_bass_kernel_spmd(nc, [arrays], core_ids=[0]).results[0]["out"]
    return np.ascontiguousarray(got.transpose(2, 1, 0).reshape(1, T, D))
```
